# Optimizing a Trainium2 kernel written in Bass

```python
import jax, jax.numpy as jnp
from jax import lax
import numpy as np

D_MODEL = 1024
BATCH = 1
SEQ = 256
DEPTH = 2

CHUNK = 64
N_META = 16
NORM_EPS = 1e-6
HEAD_DIM = 64
MIX_WIDTH = D_MODEL
ATTN_HEADS = MIX_WIDTH // 2 // HEAD_DIM
KV_HEADS = ATTN_HEADS // 4
Q_PER_KV = ATTN_HEADS // KV_HEADS
ATTN_Q = ATTN_HEADS * HEAD_DIM
ATTN_KV = KV_HEADS * HEAD_DIM
ATTN_COLS = ATTN_Q + 2 * ATTN_KV
WINDOW = 128
WINDOW_CHUNKS = WINDOW // CHUNK
RWKV_HEADS = MIX_WIDTH // 4 // HEAD_DIM
RWKV_W = RWKV_HEADS * HEAD_DIM
W_RANK = 64
A_RANK = 64
G_RANK = 128
RWKV_COLS = 3 * RWKV_W + W_RANK + A_RANK + G_RANK
GN_EPS = 64e-5
CONV_CH = MIX_WIDTH - ATTN_Q - RWKV_W
CONV_K = 31
CONV_COLS = 2 * CONV_CH
IN_COLS = ATTN_COLS + RWKV_COLS + CONV_COLS
PEER_HEADS = 8
N_KEYS = 128
N_EXPERTS = N_KEYS * N_KEYS
PEER_TOPK = 16
PEER_QDIM = 256
PEER_HALF = PEER_QDIM // 2
PEER_BLOCK = 256

kernel_name = "hymba_rwkv7_conformer_swa_peer_trunk"

def _rms(x, g):
    xf = x.astype(jnp.float32)
    y = xf * lax.rsqrt(jnp.mean(xf * xf, axis=-1, keepdims=True) + NORM_EPS)
    return y.astype(x.dtype) * g

def _layernorm(x, g, b):
    xf = x.astype(jnp.float32)
    mu = jnp.mean(xf, axis=-1, keepdims=True)
    var = jnp.mean(jnp.square(xf - mu), axis=-1, keepdims=True)
    return ((xf - mu) * lax.rsqrt(var + NORM_EPS)).astype(x.dtype) * g + b

def _sink_attend(q, k, v, dist, valid, slopes, sink):
    s = jnp.einsum('bcqgrd,bckgd->bcgrqk', q, k).astype(jnp.float32) * (HEAD_DIM ** -0.5)
    s = s - slopes[None, :, :, None, None] * dist[:, None, None]
    s = jnp.where(valid[None, :, None, None, None, :], s, -jnp.inf)
    sk = sink.astype(jnp.float32)[None, None, :, :, None, None]
    m = jnp.maximum(jnp.max(s, axis=-1, keepdims=True), sk)
    p = jnp.exp(s - m)
    p = p / (jnp.sum(p, axis=-1, keepdims=True) + jnp.exp(sk - m))
    return jnp.einsum('bcgrqk,bckgd->bcqgrd', p.astype(v.dtype), v)

def _attention_group(z, q_norm_g, k_norm_g, sinks):
    B, L, _ = z.shape
    n_chunks = (L - N_META) // CHUNK
    q = _rms(z[..., :ATTN_Q].reshape(B, L, KV_HEADS, Q_PER_KV, HEAD_DIM), q_norm_g)
    k = _rms(z[..., ATTN_Q:ATTN_Q + ATTN_KV].reshape(B, L, KV_HEADS, HEAD_DIM), k_norm_g)
    v = z[..., ATTN_Q + ATTN_KV:].reshape(B, L, KV_HEADS, HEAD_DIM)
    slopes = jnp.exp2(-8.0 * jnp.arange(1, ATTN_HEADS + 1, dtype=jnp.float32) / ATTN_HEADS).reshape(KV_HEADS, Q_PER_KV)
    sink = sinks.reshape(KV_HEADS, Q_PER_KV)
    pos_m = jnp.arange(N_META)
    dist_m = jnp.abs(pos_m[:, None] - pos_m[None, :]).astype(jnp.float32)[None]
    valid_m = jnp.ones((1, N_META), dtype=bool)
    out_m = _sink_attend(q[:, None, :N_META], k[:, None, :N_META], v[:, None, :N_META], dist_m, valid_m, slopes, sink)
    qr = q[:, N_META:].reshape(B, n_chunks, CHUNK, KV_HEADS, Q_PER_KV, HEAD_DIM)
    kr = k[:, N_META:].reshape(B, n_chunks, CHUNK, KV_HEADS, HEAD_DIM)
    vr = v[:, N_META:].reshape(B, n_chunks, CHUNK, KV_HEADS, HEAD_DIM)
    shifts = list(range(WINDOW_CHUNKS - 1, 0, -1))

    def shift(t, n):
        return jnp.pad(t[:, :n_chunks - n], ((0, 0), (n, 0), (0, 0), (0, 0), (0, 0)))

    def meta_b(t):
        return jnp.broadcast_to(t[:, None, :N_META], (B, n_chunks, N_META, KV_HEADS, HEAD_DIM))

    kb = jnp.concatenate([meta_b(k)] + [shift(kr, n) for n in shifts] + [kr], axis=2)
    vb = jnp.concatenate([meta_b(v)] + [shift(vr, n) for n in shifts] + [vr], axis=2)
    cidx = jnp.arange(n_chunks)
    qpos = N_META + cidx[:, None] * CHUNK + jnp.arange(CHUNK)[None, :]
    kpos = jnp.concatenate([jnp.broadcast_to(pos_m[None], (n_chunks, N_META))]
                           + [qpos - n * CHUNK for n in shifts] + [qpos], axis=1)
    valid = jnp.concatenate([jnp.ones((n_chunks, N_META), bool)]
                            + [jnp.broadcast_to((cidx >= n)[:, None], (n_chunks, CHUNK)) for n in shifts]
                            + [jnp.ones((n_chunks, CHUNK), bool)], axis=1)
    dist = jnp.abs(qpos[:, :, None] - kpos[:, None, :]).astype(jnp.float32)
    out_r = _sink_attend(qr, kb, vb, dist, valid, slopes, sink)
    return jnp.concatenate([out_m.reshape(B, N_META, ATTN_Q),
                            out_r.reshape(B, n_chunks * CHUNK, ATTN_Q)], axis=1)

def _rwkv7_step(S, inp):
    r, w, k, v, kk, a = inp
    sa = jnp.einsum('bhvk,bhk->bhv', S, kk)
    S = S * w[:, :, None, :] - sa[..., None] * (kk * a)[:, :, None, :] + v[..., None] * k[:, :, None, :]
    y = jnp.einsum('bhvk,bhk->bhv', S, r)
    return S, y

def _rwkv_group(z, mu, w0, w_lora, a0, a_lora, g_lora, k_k, k_a, r_k, gn_g, gn_b):
    B, L, _ = z.shape
    prev = jnp.pad(z[:, :-1], ((0, 0), (1, 0), (0, 0)))
    z = z + (prev - z) * mu
    o = np.cumsum([RWKV_W, RWKV_W, RWKV_W, W_RANK, A_RANK]).tolist()
    r, k, v, hw, ha, hg = jnp.split(z, o, axis=-1)
    w = -jax.nn.softplus(-(w0 + jnp.tanh(hw) @ w_lora)) - 0.5
    a = jax.nn.sigmoid(a0 + ha @ a_lora)
    g = jax.nn.sigmoid(hg) @ g_lora
    heads = lambda t: t.astype(jnp.float32).reshape(B, L, RWKV_HEADS, HEAD_DIM)
    kk = heads(k * k_k)
    kk = kk * lax.rsqrt(jnp.maximum(jnp.sum(kk * kk, axis=-1, keepdims=True), 1e-12))
    k = k * (1.0 + (a - 1.0) * k_a)
    rh, kh, vh, ah = heads(r), heads(k), heads(v), heads(a)
    decay = jnp.exp(-jnp.exp(heads(w)))
    tm = lambda t: jnp.moveaxis(t, 1, 0)
    S0 = jnp.zeros((B, RWKV_HEADS, HEAD_DIM, HEAD_DIM), jnp.float32)
    _, y = lax.scan(_rwkv7_step, S0, (tm(rh), tm(decay), tm(kh), tm(vh), tm(kk), tm(ah)))
    y = jnp.moveaxis(y, 0, 1)
    ym = jnp.mean(y, axis=-1, keepdims=True)
    yv = jnp.mean(jnp.square(y - ym), axis=-1, keepdims=True)
    y = ((y - ym) * lax.rsqrt(yv + GN_EPS)).reshape(B, L, RWKV_W) * gn_g + gn_b
    bonus = (jnp.sum(rh * kh * r_k, axis=-1, keepdims=True) * vh).reshape(B, L, RWKV_W)
    return ((y + bonus) * g).astype(z.dtype)

def _conv_group(z, conv_w, conv_b, ln_g, ln_b):
    u = z[..., :CONV_CH] * jax.nn.sigmoid(z[..., CONV_CH:])
    u = lax.conv_general_dilated(u, conv_w[:, None, :].astype(u.dtype), window_strides=(1,),
                                 padding=[(CONV_K - 1, 0)], dimension_numbers=('NWC', 'WIO', 'NWC'),
                                 feature_group_count=CONV_CH) + conv_b
    return jax.nn.silu(_layernorm(u, ln_g, ln_b))

def _peer(xn, wq, keys, u_tab, v_tab):
    B, L, D = xn.shape
    t = xn.reshape(B * L, D)
    T = t.shape[0]
    n_blk = -(-T // PEER_BLOCK)
    t = jnp.pad(t, ((0, n_blk * PEER_BLOCK - T), (0, 0))).reshape(n_blk, PEER_BLOCK, D)

    def one(tb):
        q = (tb @ wq).reshape(PEER_BLOCK, PEER_HEADS, 2, PEER_HALF)
        s = jnp.einsum('thpd,hpnd->thpn', q, keys).astype(jnp.float32)
        sv, si = lax.top_k(s, PEER_TOPK)
        comb = (sv[:, :, 0, :, None] + sv[:, :, 1, None, :]).reshape(PEER_BLOCK, PEER_HEADS, PEER_TOPK * PEER_TOPK)
        cidx = (si[:, :, 0, :, None] * N_KEYS + si[:, :, 1, None, :]).reshape(PEER_BLOCK, PEER_HEADS, PEER_TOPK * PEER_TOPK)
        fv, fi = lax.top_k(comb, PEER_TOPK)
        eidx = jnp.take_along_axis(cidx, fi, axis=-1)
        gate = jax.nn.softmax(fv, axis=-1)
        hid = jax.nn.gelu(jnp.einsum('td,thkd->thk', tb, jnp.take(u_tab, eidx, axis=0)))
        return jnp.einsum('thk,thkd->td', (gate * hid).astype(tb.dtype), jnp.take(v_tab, eidx, axis=0))

    return lax.map(one, t).reshape(n_blk * PEER_BLOCK, D)[:T].reshape(B, L, D)

def setup_inputs(seed: int = 0) -> dict:
    key = jax.random.key(seed)
    ks = iter(jax.random.split(key, 40))
    nrm = lambda shape, scale: jax.random.normal(next(ks), shape, jnp.float32) * scale
    return {
        "x": nrm((BATCH, SEQ, D_MODEL), 1.0),
        "meta": nrm((N_META, D_MODEL), 1.0),
        "norm1_g": 1.0 + nrm((DEPTH, D_MODEL), 0.02),
        "w_in": nrm((DEPTH, D_MODEL, IN_COLS), D_MODEL ** -0.5),
        "q_norm_g": 1.0 + nrm((DEPTH, HEAD_DIM), 0.02),
        "k_norm_g": 1.0 + nrm((DEPTH, HEAD_DIM), 0.02),
        "attn_sinks": nrm((DEPTH, ATTN_HEADS), 0.5),
        "rwkv_mu": 0.5 + nrm((DEPTH, RWKV_COLS), 0.2),
        "rwkv_w0": -1.0 + nrm((DEPTH, RWKV_W), 0.5),
        "rwkv_w_lora": nrm((DEPTH, W_RANK, RWKV_W), 0.1),
        "rwkv_a0": nrm((DEPTH, RWKV_W), 0.1),
        "rwkv_a_lora": nrm((DEPTH, A_RANK, RWKV_W), 0.5 * A_RANK ** -0.5),
        "rwkv_g_lora": nrm((DEPTH, G_RANK, RWKV_W), G_RANK ** -0.5),
        "rwkv_k_k": 0.85 + nrm((DEPTH, RWKV_W), 0.05),
        "rwkv_k_a": 1.0 + nrm((DEPTH, RWKV_W), 0.05),
        "rwkv_r_k": nrm((DEPTH, RWKV_HEADS, HEAD_DIM), 0.1),
        "rwkv_gn_g": 1.0 + nrm((DEPTH, RWKV_W), 0.02),
        "rwkv_gn_b": nrm((DEPTH, RWKV_W), 0.02),
        "conv_w": nrm((DEPTH, CONV_K, CONV_CH), CONV_K ** -0.5),
        "conv_b": nrm((DEPTH, CONV_CH), 0.02),
        "conv_ln_g": 1.0 + nrm((DEPTH, CONV_CH), 0.02),
        "conv_ln_b": nrm((DEPTH, CONV_CH), 0.02),
        "w_out": nrm((DEPTH, MIX_WIDTH, D_MODEL), 0.5 * MIX_WIDTH ** -0.5),
        "norm2_g": 1.0 + nrm((DEPTH, D_MODEL), 0.02),
        "peer_wq": nrm((DEPTH, D_MODEL, PEER_HEADS * PEER_QDIM), D_MODEL ** -0.5),
        "peer_keys": nrm((DEPTH, PEER_HEADS, 2, N_KEYS, PEER_HALF), PEER_HALF ** -0.5),
        "peer_u": nrm((DEPTH, N_EXPERTS, D_MODEL), D_MODEL ** -0.5),
        "peer_v": nrm((DEPTH, N_EXPERTS, D_MODEL), PEER_HEADS ** -0.5),
    }

def reference(x, meta, norm1_g, w_in, q_norm_g, k_norm_g, attn_sinks, rwkv_mu, rwkv_w0, rwkv_w_lora,
              rwkv_a0, rwkv_a_lora, rwkv_g_lora, rwkv_k_k, rwkv_k_a, rwkv_r_k, rwkv_gn_g, rwkv_gn_b,
              conv_w, conv_b, conv_ln_g, conv_ln_b, w_out, norm2_g, peer_wq, peer_keys, peer_u, peer_v):
    B = x.shape[0]
    h = jnp.concatenate([jnp.broadcast_to(meta[None].astype(x.dtype), (B, N_META, D_MODEL)), x], axis=1)
    for l in range(DEPTH):
        z = _rms(h, norm1_g[l]) @ w_in[l]
        za = z[..., :ATTN_COLS]
        zr = z[..., ATTN_COLS:ATTN_COLS + RWKV_COLS]
        zc = z[..., ATTN_COLS + RWKV_COLS:]
        ya = _attention_group(za, q_norm_g[l], k_norm_g[l], attn_sinks[l])
        yr = _rwkv_group(zr, rwkv_mu[l], rwkv_w0[l], rwkv_w_lora[l], rwkv_a0[l], rwkv_a_lora[l], rwkv_g_lora[l],
                         rwkv_k_k[l], rwkv_k_a[l], rwkv_r_k[l], rwkv_gn_g[l], rwkv_gn_b[l])
        yc = _conv_group(zc, conv_w[l], conv_b[l], conv_ln_g[l], conv_ln_b[l])
        h = h + jnp.concatenate([ya, yr, yc], axis=-1) @ w_out[l]
        h = h + _peer(_rms(h, norm2_g[l]), peer_wq[l], peer_keys[l], peer_u[l], peer_v[l])
    return h[:, N_META:]


_drawn_inputs = setup_inputs


def setup_inputs(seed=0):
    import zlib

    import numpy as np

    out = dict(_drawn_inputs(seed))
    spreads = {}
    factors = {'q_norm_g': 3.131,
     'k_norm_g': 3.554,
     'rwkv_k_k': 21.988,
     'rwkv_gn_b': 2.805,
     'conv_ln_b': 2.776,
     'attn_sinks': 64.0}
    for name, (base, spread) in spreads.items():
        noise = np.random.default_rng([zlib.crc32(name.encode()), seed]).standard_normal(out[name].shape)
        drawn = base * np.exp(spread * noise) if base else spread * noise
        out[name] = __import__('jax').numpy.asarray(drawn.astype(out[name].dtype))
    for name, factor in factors.items():
        out[name] = (out[name] * factor).astype(out[name].dtype)
    return out
```

```python
from contextlib import ExitStack

import numpy as np
import concourse.bass as bass
from concourse import mybir

ALU = mybir.AluOpType
ACT = mybir.ActivationFunctionType
AX = mybir.AxisListType
F32 = mybir.dt.float32
U32 = mybir.dt.uint32

P = 128
D = 1024
DC = D // P
SEQ = 256
NMETA = 16
T = SEQ + NMETA
DEPTH = 2
HD = 64
NORM_EPS = 1e-6
GN_EPS = 64e-5
CHUNK = 64
ZR, ZCU, ZCG, ZQ, ZK, ZV = 0, 8, 10, 12, 16, 17
NZ = 18
NOUT = D // P
NCH = -(-T // CHUNK)
PAD = NCH * CHUNK - T
TP = NCH * CHUNK
NMAT = NCH * 4
LEVELS = (1, 2, 4, 8, 16, 32)
CONV_K = 31
CPAD = CONV_K - 1
AH = 8
PH = 8
NKEYS = 128
TOPK = 16
NQ = PH * 2
TILES = ((0, NMETA), (NMETA, P), (NMETA + P, P))
NT = len(TILES)
NEG = -3.0e38
FAR = 1.0e30
VEC = dict(norm1=(0, 8), norm2=(8, 8), qg=(16, 1), kg=(17, 1), mu=(18, 8), w0=(26, 2), a0=(28, 2), k_k=(30, 2),
           k_a=(32, 2), r_k=(34, 2), gn_g=(36, 2), gn_b=(38, 2), conv_b=(40, 2), ln_g=(42, 2), ln_b=(44, 2),
           conv_w=(46, 2 * CONV_K), sink=(46 + 2 * CONV_K, AH))
NVEC = 46 + 2 * CONV_K + AH
RES = dict(ident=(0, P), ones=(P, P), iota=(2 * P, P))
NRES = 3 * P
MIX = {}
NMIX = 0
for _name, _n in (("blk", P), ("mask4", 4 * CHUNK), ("negm1", CHUNK), ("mT", len(LEVELS) * CHUNK),
                  ("distM", NMETA), ("distA", 144), ("distB", 208)):
    MIX[_name] = (NMIX, _n)
    NMIX += _n
WR, VR = 4, 4
NPROJ = NZ + NOUT + NQ
NW = NPROJ + NKEYS
LAYER_TILES = [len(range(s, NW, WR)) for s in range(WR)]
OHT = 4
NSTEP = T // OHT
YB = 3
YCOLS = DC * T
KEYS_OF = (NMETA, 144, 208)
V_TILES = (("z", 0, P, (0, 0)), ("z", P, 16, (0, 1)), ("vcat", 0, P, (1, 0)), ("vcat", P, 80, (1, 1)))
STEP, PE_STEPS = {}, 0
for _name, _n in (("kk", 1), ("bonus", 1), ("tok", 3 * NCH), ("gram", NCH), ("inv", 3 * (len(LEVELS) - 1)),
                  ("chunk", 3 * NCH), ("gn", 2), ("ln", 2), ("qk", 1), ("vkey", 1), ("att", NT * 3 * AH), ("sel", NT)):
    STEP[_name] = PE_STEPS
    PE_STEPS += _n
ACT_STEPS = 3 + (len(LEVELS) - 1) + 2 + 1 + NT + NT
SLOPES = [2.0 ** (-8.0 * (h + 1) / AH) for h in range(AH)]


def constants():
    res = np.zeros((P, NRES), np.float32)
    res[:, 0:P] = np.eye(P)
    res[:, P:2 * P] = 1.0
    res[:, 2 * P:3 * P] = np.arange(P)[None]
    mix = np.zeros((P, NMIX), np.float32)

    def put(name, a):
        a = np.asarray(a, np.float32)
        mix[:a.shape[0], MIX[name][0]:MIX[name][0] + MIX[name][1]] = a.reshape(a.shape[0], -1)

    p = np.arange(P)
    put("blk", p[:, None] // HD == p[None] // HD)
    s, t = np.arange(CHUNK)[:, None], np.arange(CHUNK)[None]
    put("mask4", np.stack([s < t, s <= t, s < t, s <= t], 1))
    cross = lambda b, r, c: (r // (2 * b) == c // (2 * b)) & ((r // b) % 2 == 1) & ((c // b) % 2 == 0)
    put("negm1", -1.0 * cross(1, s, t))
    put("mT", np.stack([cross(b, t, s) for b in LEVELS], 1))
    put("distM", np.abs(np.arange(NMETA)[:, None] - np.arange(NMETA)[None]))

    def dist(q0, keys):
        q = q0 + np.arange(P)[:, None]
        k = np.asarray(keys)[None]
        qc, kc = (q - NMETA) // CHUNK, (k - NMETA) // CHUNK
        ok = (k < NMETA) | ((kc <= qc) & (kc >= qc - 1))
        return np.where(ok, np.abs(q - k), FAR)

    put("distA", dist(NMETA, range(0, 144)))
    put("distB", dist(NMETA + P, list(range(16)) + list(range(80, 272))))
    return res, mix


class Link:

    def __init__(self, eng, sem):
        self.eng, self.sem, self.n = eng, sem, 0

    def __call__(self, ins):
        ins.then_inc(self.sem, 1)
        self.n = self.n + 1
        self.eng.wait_ge(self.sem, self.n)


class Arena:

    def __init__(self, tensor, start=0):
        self.t, self.at = tensor, start

    def take(self, n, parts=P):
        a = self.t[0:parts, self.at:self.at + n]
        self.at += n
        assert self.at <= self.t.shape[1], self.at
        return a


def splits(n):
    return [(a, min(P, n - a)) for a in range(0, n, P)]


def bc(ap, axis, n):
    a = ap.unsqueeze(axis)
    shape = list(a.shape)
    shape[axis] = n
    return a.broadcast_to(shape)


def trunk(nc, h0, vec, res_c, mix_c, lora_c, keys_c, w_c, u_c, v_c, out):
    with ExitStack() as ctx:
        def sb(name, cols, dt=F32, parts=P):
            return ctx.enter_context(nc.sbuf_tensor(name, [parts, cols], dt))

        def sem(name):
            return ctx.enter_context(nc.semaphore(name))

        h_t = sb("h", DC * T)
        xn_t = sb("xn", DC * T)
        res_t = sb("res", NRES)
        vec_t = sb("vecs", DEPTH * NVEC)
        wring_t = sb("wring", WR * D)
        vring_t = sb("vring", VR * D)
        sel_t = sb("sel", 3 * T)
        oh_t = sb("onehots", 2 * 2 * OHT * P)
        act_t = sb("acts", 3 * T)
        zero_t = sb("zeros", P)
        mhalf = sb("minus_half", 1)
        arena_t = sb("arena", P * T)
        ps = ctx.enter_context(nc.psum_tensor("ps", [P, 8, 512], F32))

        h = h_t[:, :].rearrange("p (c t) -> p c t", c=DC)
        xn = xn_t[:, :].rearrange("p (c t) -> p c t", c=DC)
        vecs = vec_t[:, :].rearrange("p (l n) -> p l n", l=DEPTH)
        wring = wring_t[:, :].rearrange("p (s k c) -> p s k c", s=WR, k=DC)
        vring = vring_t[:, :].rearrange("p (s n) -> p s n", s=VR)
        sel = sel_t[:, :].rearrange("p (s t) -> p s t", s=3)
        onehot = oh_t[:, :].rearrange("p (b s t n) -> p b s t n", b=2, s=2, t=OHT)
        acts = act_t[:, :].rearrange("p (b t) -> p b t", b=3)
        gates = arena_t[:, :].rearrange("p (i t) -> p i t", i=P)
        psf = ps[:, :, :].rearrange("p b n -> p (b n)")

        def res(name):
            a, n = RES[name]
            return res_t[:, a:a + n]

        ident, ones, iota = res("ident"), res("ones"), res("iota")

        def vcol(l, name, i=0, parts=slice(0, P)):
            a = VEC[name][0] + i
            return vecs[parts, l, a:a + 1]

        A = Arena(arena_t)
        mix_m = A.take(NMIX)
        lora = A.take(4 * P).rearrange("p (s n) -> p s n", s=2)
        sq = A.take(DC * T).rearrange("p (c t) -> p c t", c=DC)
        z = A.take(NZ * (T + 1)).rearrange("p (c t) -> p c t", c=NZ)
        cat = A.take(DC * T).rearrange("p (c t) -> p c t", c=DC)
        mixed_end = A.at

        def two(n=T):
            return A.take(2 * n).rearrange("p (j t) -> p j t", j=2)

        bonus, gg = two(), two()
        al, be, ka, rh = two(TP), two(TP), two(TP), two(TP)
        dall = two(TP)
        yT = two(TP)
        t1, t2, t3 = two(), two(), two(TP)
        vtok = A.take(NCH * 2 * P, CHUNK).rearrange("p (c j n) -> p c j n", c=NCH, j=2)
        ktok = A.take(NCH * 2 * P, CHUNK).rearrange("p (c j n) -> p c j n", c=NCH, j=2)
        btok = A.take(NCH * 2 * P, CHUNK).rearrange("p (c j n) -> p c j n", c=NCH, j=2)
        state = A.take(2 * P).rearrange("p (j n) -> p j n", j=2)
        stmp = A.take(2 * P).rearrange("p (j n) -> p j n", j=2)
        xs = A.take(2 * P, CHUNK).rearrange("p (j n) -> p j n", j=2)
        us = A.take(2 * P, CHUNK).rearrange("p (j n) -> p j n", j=2)
        over = A.at
        zs = A.take(8 * T).rearrange("p (c t) -> p c t", c=8)
        th = A.take(T)
        sg = A.take(T)
        ea, aa = two(), two()
        lw, cum = two(TP), two(TP)
        dinv, dexc = two(TP), two(TP)
        kk, km, bb = two(), two(), two()
        over_prep = A.at
        A.at = over
        gram = A.take(NCH * 2 * 2 * 4 * CHUNK, CHUNK).rearrange("p (c q j m t) -> p c q j m t", c=NCH, q=2, j=2, m=4)
        mats = lambda: A.take(NMAT * CHUNK, CHUNK).rearrange("p (n t) -> p n t", n=NMAT)
        ti, tt_, xm, cm = mats(), mats(), mats(), mats()
        over_mats = A.at
        A.at = over
        cu = A.take(2 * (CPAD + T)).rearrange("p (j t) -> p j t", j=2)
        cacc = two()
        qn = A.take(5 * T).rearrange("p (c t) -> p c t", c=5)
        kcat = A.take(208)
        vcat = A.take(208)
        vkey = A.take(2 * 2 * P).rearrange("p (s k n) -> p s k n", s=2, k=2)
        prob = A.take(AH * 208)
        pT = A.take(2 * 2 * P).rearrange("p (b k n) -> p b k n", b=2, k=2)
        small = A.take(8 * AH).rearrange("p (s h) -> p s h", s=8)
        over_attn = A.at
        A.at = 0
        keys = A.take(NQ * P).rearrange("p (m n) -> p m n", m=NQ)
        pq = A.take(NQ * T).rearrange("p (m t) -> p m t", m=NQ)
        sc = A.take(NT * NQ * P).rearrange("p (s m n) -> p s m n", s=NT, m=NQ)
        comb = A.take(PH * TOPK * TOPK).rearrange("p (h n) -> p h n", h=PH)
        eqm = A.take(PH * TOPK * TOPK)
        topv = A.take(NQ * TOPK).rearrange("p (h s k) -> p h s k", h=PH, s=2)
        topi = A.take(NQ * TOPK)
        topf = A.take(NQ * TOPK).rearrange("p (h s k) -> p h s k", h=PH, s=2)
        fv = A.take(P)
        fi = A.take(P)
        fa = A.take(2 * P).rearrange("p (s n) -> p s n", s=2)
        ff = A.take(2 * P).rearrange("p (s n) -> p s n", s=2)
        chosen = A.take(3 * P).rearrange("p (s n) -> p s n", s=3)
        gsum = A.take(PH)
        topi_u = topi.bitcast(U32).rearrange("p (h s k) -> p h s k", h=PH, s=2)
        fi_u = fi.bitcast(U32)
        fa_u = fa.bitcast(U32)

        def mix(name, parts=P):
            a, n = MIX[name]
            return mix_m[0:parts, a:a + n]

        blk = mix("blk")
        mask4 = mix("mask4", CHUNK).rearrange("p (m t) -> p m t", m=4)
        negm1 = mix("negm1", CHUNK)
        mT = mix("mT", CHUNK).rearrange("p (b t) -> p b t", b=len(LEVELS))

        s_h = sem("first_loads")
        s_zero = sem("zeros_set")
        s_mix = sem("mixer_constants_loaded")
        s_keys = sem("keys_loaded")
        s_w = [sem(f"weights_loaded_{i}") for i in range(WR)]
        s_v = [sem(f"v_loaded_{i}") for i in range(VR)]
        s_vu = sem("v_used")
        s_sq = sem("squares_ready")
        s_ss = sem("square_sums_ready")
        s_xn = sem("normed_ready")
        s_pj = sem("projection_done")
        s_ea = sem("evacuated_by_act")
        s_ed = sem("evacuated_by_dve")
        s_th = sem("tanh_ready")
        s_sg = sem("sigmoid_hg_ready")
        s_zs = sem("shifted_ready")
        s_lo = sem("lora_done")
        s_ag = sem("a_w_g_ready")
        s_pe = sem("vector_request")
        s_pd = sem("pe_step_done")
        s_ar = sem("act_request")
        s_ad = sem("act_step_done")
        s_var = sem("variance_ready")
        s_rs = sem("rsqrt_ready")
        s_qr = sem("scores_in_psum")
        s_sc = sem("scores_copied")
        s_oh = sem("onehots_ready")
        s_gp = sem("gate_tile_in_psum")
        s_g = sem("gate_tile_stored")
        s_sel = sem("selection_ready")
        s_hid = sem("hidden_in_psum")
        s_gelu = sem("gelu_done")
        s_act = sem("gated_act_ready")
        s_yu = sem("act_used")
        s_y = sem("peer_output_done")
        s_hd = sem("layer_done")
        s_out = sem("output_stored")
        s_dl = sem("dve_link")
        s_al = sem("act_link")

        block = ctx.enter_context(nc.Block())

        @block.sync
        def _(sp):
            sp.dma_start(h_t[:, :], h0).then_inc(s_h, 16)
            sp.dma_start(res_t[:, :], res_c).then_inc(s_h, 16)
            sp.dma_start(vec_t[:, :], vec).then_inc(s_h, 16)

            def load_w(l, n, src, it=0, unroll=0):
                slot = n % WR
                if n >= NPROJ + WR:
                    sp.wait_ge(s_hid, l * NKEYS + n - NPROJ - WR + 1 + unroll * it)
                elif n >= WR:
                    sp.wait_ge(s_pj, l * NPROJ + n - WR + 1 + unroll * it)
                elif l:
                    sp.wait_ge(s_hid, l * NKEYS)
                sp.dma_start(wring_t[:, slot * D:(slot + 1) * D], src).then_inc(s_w[slot], 16)

            for l in range(DEPTH):
                if l:
                    sp.wait_ge(s_hd, l)
                sp.dma_start(mix_m, mix_c).then_inc(s_mix, 16)
                sp.dma_start(lora.rearrange("p s n -> p (s n)"), lora_c[l]).then_inc(s_mix, 16)
                for n in range(WR):
                    load_w(l, n, w_c[l, n])
                with sp.Fori(0, (NPROJ - WR) // WR) as it:
                    for j in range(WR):
                        n = WR + j
                        load_w(l, n, w_c[l, WR * it + n], it, WR)
                for n in range(NPROJ - (NPROJ - WR) % WR, NPROJ):
                    load_w(l, n, w_c[l, n])
                sp.wait_ge(s_xn, (2 * l + 2) * DC)
                sp.wait_ge(s_ed, (l + 1) * NOUT)
                sp.dma_start(keys.rearrange("p m n -> p (m n)"), keys_c[l]).then_inc(s_keys, 16)

                def load_uv(first, it):
                    for j in range(WR):
                        load_w(l, NPROJ + j + (0 if first else WR),
                               u_c[l, j if first else WR * it + WR + j], 0 if first else it, WR)
                        if not first:
                            sp.wait_ge(s_vu, WR * it + l * NKEYS + j + 1)
                        elif l:
                            sp.wait_ge(s_vu, l * NKEYS)
                        sp.dma_start(vring[:, j, :], v_c[l, j if first else WR * it + WR + j]).then_inc(s_v[j], 16)

                load_uv(True, 0)
                with sp.Fori(0, NKEYS // WR - 1) as it:
                    load_uv(False, it)
            sp.wait_ge(s_hd, DEPTH)
            sp.dma_start(out, h[:, :, NMETA:T]).then_inc(s_out, 16)
            sp.wait_ge(s_out, 16)

        @block.gpsimd
        def _(pool):
            nc.gpsimd.memset(zero_t[:, :], 0.0).then_inc(s_zero, 1)
            nc.gpsimd.memset(mhalf[:, :], -0.5).then_inc(s_zero, 1)
            pool.wait_ge(s_zero, 2)
            n = 0
            for l in range(DEPTH):
                for a in (acts[:, 0:1, :], t2[:, :, :], t2[:, :, :], t3[:, 0:1, 0:T], qn[:, :, :], acts[:, 0:1, :]):
                    n += 1
                    pool.wait_ge(s_var, n)
                    nc.gpsimd.tensor_tensor(a, a, mhalf[:, :].unsqueeze(2).broadcast_to(a.shape),
                                            ALU.pow).then_inc(s_rs, 1)

        @block.scalar
        def _(act):
            link = Link(act, s_al)
            req = [0]
            done = [0]

            def asked():
                req[0] += 1
                act.wait_ge(s_ar, req[0])

            def squares(l, k):
                if 2 * l + k:
                    act.wait_ge(s_hd, l) if k == 0 else act.wait_ge(s_ed, (l + 1) * NOUT)
                else:
                    act.wait_ge(s_h, 48)
                nc.scalar.activation(sq[:, :, :], h[:, :, :], ACT.Square).then_inc(s_sq, 1)

            def evacuate(l, n, dst, before):
                act.wait_ge(s_pj, l * NPROJ + n + 1)
                nc.scalar.copy(dst, ps[:, 1 + n % 2, 0:T]).then_inc(s_ea, 1)

            for l in range(DEPTH):
                squares(l, 0)
                for n in range(8):
                    evacuate(l, n, z[:, n, 1:T + 1], n)
                act.wait_ge(s_zs, 2 * l + 2)
                nc.scalar.activation(th[0:HD, :], zs[0:HD, 6, :], ACT.Tanh).then_inc(s_th, 1)
                nc.scalar.activation(sg[:, :], zs[:, 7, :], ACT.Sigmoid).then_inc(s_sg, 1)
                act.wait_ge(s_lo, 6 * l + 6)
                for j in range(2):
                    nc.scalar.activation(ea[:, j, :], ps[:, 3 + j, 0:T], ACT.Sigmoid,
                                         bias=vcol(l, "w0", j)).then_inc(s_ag, 1)
                for j in range(2):
                    nc.scalar.activation(aa[:, j, :], ps[:, 5 + j, 0:T], ACT.Sigmoid,
                                         bias=vcol(l, "a0", j)).then_inc(s_ag, 1)
                for j in range(2):
                    nc.scalar.copy(gg[:, j, :], ps[:, 7 if j == 0 else 0, 0:T]).then_inc(s_ag, 1)
                for n in range(8, NZ):
                    evacuate(l, n, z[:, n, 1:T + 1], n)
                asked()
                nc.scalar.activation(dall[:, :, :], cum[:, :, :], ACT.Exp).then_inc(s_ad, 1)
                nc.scalar.activation(dinv[:, :, :], cum[:, :, :], ACT.Exp, scale=-1.0).then_inc(s_ad, 1)
                nc.scalar.activation(dexc[:, :, :], lw[:, :, :], ACT.Exp).then_inc(s_ad, 1)
                for b in range(len(LEVELS) - 1):
                    act.wait_ge(s_pd, l * PE_STEPS + STEP["inv"] + 3 * b + 1)
                    for g in range(3):
                        n0, n1 = 8 * g, min(8 * g + 8, NMAT)
                        ins = nc.scalar.copy(xm[:, n0:n1, :].rearrange("p n t -> p (n t)"),
                                             ps[0:CHUNK, 3 + g, 0:(n1 - n0) * CHUNK])
                    ins.then_inc(s_ad, 1)
                for j in range(2):
                    asked() if j == 0 else None
                    nc.scalar.activation(cacc[:, j, :], z[:, ZCG + j, 1:T + 1], ACT.Sigmoid).then_inc(s_ad, 1)
                asked()
                nc.scalar.activation(t2[:, :, :], t1[:, :, :], ACT.Sigmoid).then_inc(s_ad, 1)
                for s, (q0, nq) in enumerate(TILES):
                    nk = KEYS_OF[s]
                    asked()
                    pr = prob[0:nq, 0:AH * nk].rearrange("p (h k) -> p h k", h=AH)
                    for hh in range(AH):
                        nc.scalar.activation(pr[:, hh, :], pr[:, hh, :], ACT.Exp, bias=small[0:nq, 1, hh:hh + 1],
                                             scale=HD ** -0.5, accum_out=small[0:nq, 2, hh:hh + 1])
                    nc.scalar.activation(small[0:nq, 3, :], small[0:nq, 3, :], ACT.Exp).then_inc(s_ad, 1)
                squares(l, 1)
                for m in range(NQ):
                    n = NZ + NOUT + m
                    if m == 0:
                        act.wait_ge(s_xn, (2 * l + 2) * DC)
                    evacuate(l, n, pq[:, m, :], n)
                for s, (t0, nt) in enumerate(TILES):
                    for g in range(4):
                        k = 4 * s + g
                        act.wait_ge(s_qr, l * 4 * NT + k + 1)
                        nc.scalar.copy(sc[0:nt, s, 4 * g:4 * g + 4, :].rearrange("p m n -> p (m n)"),
                                       ps[0:nt, 3 + k % 2, :]).then_inc(s_sc, 1)
                for s, (t0, nt) in enumerate(TILES):
                    asked()
                    nc.scalar.activation(chosen[0:nt, 0, :], chosen[0:nt, 0, :], ACT.Exp).then_inc(s_ad, 1)
                with act.Fori(0, NSTEP // 2) as it:
                    for b in range(2):
                        act.wait_ge(s_gp, 2 * it + l * NSTEP + b + 1)
                        nc.scalar.copy(gates[:, :, bass.ds(2 * OHT * it + b * OHT, OHT)],
                                       ps[:, b, :].rearrange("p (t i) -> p i t", t=OHT)).then_inc(s_g, 1)
                with act.Fori(0, NKEYS // 2) as it:
                    for b in range(2):
                        act.wait_ge(s_hid, 2 * it + l * NKEYS + b + 1)
                        nc.scalar.activation(acts[:, b, :], ps[:, 1 + b, 0:T], ACT.Gelu_apprx_tanh).then_inc(s_gelu, 1)

        @block.tensor
        def _(pe):
            def mm(out_, lhsT, rhs, start, stop):
                return nc.tensor.matmul(out_, lhsT, rhs, start=start, stop=stop, skip_group_check=True)

            req = [0]

            def asked():
                req[0] += 1
                pe.wait_ge(s_pe, req[0])

            def square_sums(l, k):
                pe.wait_ge(s_sq, 2 * l + k + 1)
                for c in range(DC):
                    last = mm(ps[:, 0, 0:T], ones, sq[:, c, :], c == 0, c == DC - 1)
                last.then_inc(s_ss, 1)

            def project(l, n, slot, rhs, it=0, unroll=0):
                pe.wait_ge(s_w[slot], 16 * (l * LAYER_TILES[slot] + n // WR + 1 + (unroll // WR) * it))
                for c in range(DC):
                    last = mm(ps[:, 1 + n % 2, 0:T], wring[:, slot, c, :], rhs[:, c, :], c == 0, c == DC - 1)
                last.then_inc(s_pj, 1)
                return last

            for l in range(DEPTH):
                if l == 0:
                    pe.wait_ge(s_h, 48)
                    pe.wait_ge(s_zero, 1)
                pe.wait_ge(s_mix, 32 * (l + 1))
                square_sums(l, 0)
                pe.wait_ge(s_xn, (2 * l + 1) * DC)

                def proj_in(n):
                    if n >= 2:
                        pe.wait_ge(s_ea, l * (NZ + NQ) + n - 1)
                    project(l, n, n % WR, xn)

                for n in range(NZ):
                    if n == 8:
                        pe.wait_ge(s_th, l + 1)
                        pe.wait_ge(s_sg, l + 1)
                        for j in range(2):
                            mm(ps[:, 3 + j, 0:T], lora[0:HD, 0, j * P:(j + 1) * P], th[0:HD, :],
                               True, True).then_inc(s_lo, 1)
                        for j in range(2):
                            mm(ps[:, 5 + j, 0:T], lora[HD:P, 0, j * P:(j + 1) * P], zs[HD:P, 6, :],
                               True, True).then_inc(s_lo, 1)
                        for j in range(2):
                            mm(ps[:, 7 if j == 0 else 0, 0:T], lora[:, 1, j * P:(j + 1) * P], sg[:, :],
                               True, True).then_inc(s_lo, 1)
                    proj_in(n)

                pe.wait_ge(s_ag, 6 * l + 6)
                asked()
                for j in range(2):
                    last = mm(ps[:, 3 + j, 0:T], blk, t2[:, j, :], True, True)
                last.then_inc(s_pd, 1)
                asked()
                for j in range(2):
                    last = mm(ps[:, 5 + j, 0:T], blk, t1[:, j, :], True, True)
                last.then_inc(s_pd, 1)
                asked()
                for c in range(NCH):
                    for m, src in enumerate((None, ka, be)):
                        k = 3 * c + m
                        if k >= 2:
                            asked()
                        for j in range(2):
                            a = t3[:, j, c * CHUNK:(c + 1) * CHUNK] if src is None else \
                                src[:, j, c * CHUNK:(c + 1) * CHUNK]
                            last = nc.tensor.transpose(ps[0:CHUNK, 3 + k % 2, j * P:(j + 1) * P], a, ident)
                        last.then_inc(s_pd, 1)
                for c in range(NCH):
                    asked()
                    w = slice(c * CHUNK, (c + 1) * CHUNK)
                    for q in range(2):
                        r = slice(q * HD, (q + 1) * HD)
                        for j in range(2):
                            for m, (a, b) in enumerate(((ka, al), (ka, rh), (be, al), (be, rh))):
                                mm(ps[0:CHUNK, 3 + q, (j * 4 + m) * CHUNK:(j * 4 + m + 1) * CHUNK],
                                   a[r, j, w], b[r, j, w], True, True)
                            last = mm(ps[0:CHUNK, 5 + q, j * CHUNK:(j + 1) * CHUNK], al[r, j, w], be[r, j, w],
                                      True, True)
                    last.then_inc(s_pd, 1)
                for b in range(len(LEVELS) - 1):
                    asked()
                    for n in range(NMAT):
                        last = mm(ps[0:CHUNK, 3 + n // 8, (n % 8) * CHUNK:(n % 8 + 1) * CHUNK],
                                  cm[:, n, :], ti[:, n, :], True, True)
                    last.then_inc(s_pd, 1)
                    pe.wait_ge(s_ad, l * ACT_STEPS + 3 + b + 1)
                    for n in range(NMAT):
                        bank = (6, 7, 0)[n // 8]
                        last = mm(ps[0:CHUNK, bank, (n % 8) * CHUNK:(n % 8 + 1) * CHUNK],
                                  tt_[:, n, :], xm[:, n, :], True, True)
                    last.then_inc(s_pd, 1)
                    for n in range(NMAT):
                        last = mm(ps[0:CHUNK, 3 + n // 8, (n % 8) * CHUNK:(n % 8 + 1) * CHUNK],
                                  xm[:, n, :], tt_[:, n, :], True, True)
                    last.then_inc(s_pd, 1)
                for c in range(NCH):
                    w = slice(c * CHUNK, (c + 1) * CHUNK)
                    asked()
                    for j in range(2):
                        mm(ps[0:CHUNK, 3, j * P:(j + 1) * P], al[:, j, w], state[:, j, :], True, False)
                        for q in range(2):
                            last = mm(ps[0:CHUNK, 3, j * P + q * HD:j * P + (q + 1) * HD], gram[:, c, q, j, 0, :],
                                      vtok[:, c, j, q * HD:(q + 1) * HD], False, True)
                    last.then_inc(s_pd, 1)
                    asked()
                    for j in range(2):
                        for q in range(2):
                            last = mm(ps[0:CHUNK, 4, j * P + q * HD:j * P + (q + 1) * HD],
                                      tt_[:, c * 4 + q * 2 + j, :], xs[:, j, q * HD:(q + 1) * HD], True, True)
                    last.then_inc(s_pd, 1)
                    asked()
                    for j in range(2):
                        mm(ps[:, 5, j * P:(j + 1) * P], ktok[:, c, j, :], vtok[:, c, j, :], True, False)
                        mm(ps[:, 5, j * P:(j + 1) * P], btok[:, c, j, :], us[:, j, :], False, True)
                    for j in range(2):
                        mm(ps[:, 6, j * CHUNK:(j + 1) * CHUNK], state[:, j, :], rh[:, j, w], True, False)
                        for q in range(2):
                            o = ps[q * HD:(q + 1) * HD, 6, j * CHUNK:(j + 1) * CHUNK]
                            mm(o, vtok[:, c, j, q * HD:(q + 1) * HD], gram[:, c, q, j, 1, :], False, False)
                            last = mm(o, us[:, j, q * HD:(q + 1) * HD], gram[:, c, q, j, 3, :], False, True)
                    last.then_inc(s_pd, 1)
                for k in range(2):
                    asked()
                    for j in range(2):
                        last = mm(ps[:, 3 + j, 0:T], blk, yT[:, j, PAD:TP] if k == 0 else t2[:, j, :], True, True)
                    last.then_inc(s_pd, 1)
                for k in range(2):
                    asked()
                    for j in range(2):
                        last = mm(ps[:, 3, 0:T], ones, cacc[:, j, :] if k == 0 else t2[:, j, :], j == 0, j == 1)
                    last.then_inc(s_pd, 1)
                asked()
                for c in range(5):
                    last = mm(ps[:, 3 + c, 0:T], blk, sq[:, c, :], True, True)
                last.then_inc(s_pd, 1)
                asked()
                for s, (src, k0, nk, _) in enumerate(V_TILES):
                    a = z[:, ZV, 1 + k0:1 + k0 + nk] if src == "z" else vcat[:, k0:k0 + nk]
                    last = nc.tensor.transpose(ps[0:nk, 3 + s % 2, (s // 2) * P:(s // 2 + 1) * P], a, ident)
                last.then_inc(s_pd, 1)
                for s, (q0, nq) in enumerate(TILES):
                    nk = KEYS_OF[s]
                    kt = kcat if s == 2 else qn[:, 4, :]
                    for hh in range(AH):
                        if hh != 1:
                            asked()
                        r = slice((hh // 4) * HD, (hh // 4 + 1) * HD)
                        mm(ps[0:nq, 3 + hh % 2, 0:nk], qn[r, hh % 4, q0:q0 + nq], kt[r, 0:nk],
                           True, True).then_inc(s_pd, 1)
                    for hh in range(AH):
                        asked()
                        for b, (k0, kn) in enumerate(splits(nk)):
                            last = nc.tensor.transpose(ps[0:kn, 5 + hh % 2, b * P:b * P + nq],
                                                       prob[0:nq, hh * nk + k0:hh * nk + k0 + kn], ident[0:nq, 0:nq])
                        last.then_inc(s_pd, 1)
                        asked()
                        q, c = hh // 4, hh % 4
                        for b, (k0, kn) in enumerate(splits(nk)):
                            last = mm(ps[q * HD:(q + 1) * HD, 7 - 7 * (hh % 2), 0:nq],
                                      vkey[0:kn, max(s, 1) - 1, b, q * HD:(q + 1) * HD], pT[0:kn, hh % 2, b, 0:nq],
                                      b == 0, k0 + kn == nk)
                        last.then_inc(s_pd, 1)
                asked()
                for m in range(NOUT):
                    n = NZ + m
                    if m >= 2:
                        pe.wait_ge(s_ed, l * NOUT + m - 1)
                    else:
                        pe.wait_ge(s_ea, l * (NZ + NQ) + NZ)
                    project(l, n, n % WR, cat)
                square_sums(l, 1)
                pe.wait_ge(s_xn, (2 * l + 2) * DC)
                for m in range(NQ):
                    n = NZ + NOUT + m
                    if m >= 2:
                        pe.wait_ge(s_ea, l * (NZ + NQ) + NZ + m - 1)
                    project(l, n, n % WR, xn)
                pe.wait_ge(s_keys, 16 * (l + 1))
                pe.wait_ge(s_ea, (l + 1) * (NZ + NQ))
                for s, (t0, nt) in enumerate(TILES):
                    for g in range(4):
                        k = 4 * s + g
                        if k >= 2:
                            pe.wait_ge(s_sc, l * 4 * NT + k - 1)
                        for m in range(4):
                            last = mm(ps[0:nt, 3 + k % 2, m * P:(m + 1) * P], pq[:, 4 * g + m, t0:t0 + nt],
                                      keys[:, 4 * g + m, :], True, True)
                        last.then_inc(s_qr, 1)
                for s, (t0, nt) in enumerate(TILES):
                    asked()
                    for m in range(3):
                        last = nc.tensor.transpose(ps[:, 5 + s % 2, m * P:m * P + nt], chosen[0:nt, m, :],
                                                   ident[0:nt, 0:nt])
                    last.then_inc(s_pd, 1)

                def spread(b, it, first):
                    pe.wait_ge(s_oh, 2 * it + l * NSTEP + b + 1)
                    if not first:
                        pe.wait_ge(s_g, 2 * it + l * NSTEP + b - 1)
                    for t in range(OHT):
                        last = mm(ps[:, b, t * P:(t + 1) * P], onehot[:, b, 1, t, :], onehot[:, b, 0, t, :],
                                  True, True)
                    last.then_inc(s_gp, 1)

                for b in range(2):
                    spread(b, 0, True)
                with pe.Fori(1, NSTEP // 2) as it:
                    for b in range(2):
                        spread(b, it, False)
                for k in range(-(-YCOLS // 512)):
                    last = mm(ps[:, YB + k, :], zero_t[:, :], xn_t[:, 0:512], True, True)
                pe.wait_ge(s_g, (l + 1) * NSTEP)

                def hidden(j, it, bank, first):
                    n = NPROJ + j
                    slot = n % WR
                    pe.wait_ge(s_w[slot], 16 * it + 16 * (l * LAYER_TILES[slot] + n // WR + 1))
                    if not first:
                        pe.wait_ge(s_gelu, WR * it + l * NKEYS + j - 1)
                    for c in range(DC):
                        last = mm(ps[:, bank, 0:T], wring[:, slot, c, :], xn[:, c, :], c == 0, c == DC - 1)
                    last.then_inc(s_hid, 1)

                def output(j, it):
                    pe.wait_ge(s_v[j % VR], 16 * it + 16 * (l * (NKEYS // VR) + j // VR + 1))
                    pe.wait_ge(s_act, WR * it + l * NKEYS + j + 1)
                    for c in range(DC):
                        a, e = c * T, (c + 1) * T
                        while a < e:
                            b = min(e, (a // 512 + 1) * 512)
                            last = mm(psf[:, YB * 512 + a:YB * 512 + b], vring[:, j % VR, c * P:(c + 1) * P],
                                      acts[:, j % 2, a - c * T:b - c * T], False, True)
                            a = b
                    last.then_inc(s_vu, 1)

                hidden(0, 0, 1, True)
                hidden(1, 0, 2, True)
                output(0, 0)
                hidden(2, 0, 1, False)
                output(1, 0)
                hidden(3, 0, 2, False)
                output(2, 0)
                with pe.Fori(1, NKEYS // WR) as it:
                    for j in range(WR):
                        hidden(j, it, 1 + j % 2, False)
                        output((j - 1) % WR, it - (1 if j == 0 else 0))
                output(WR - 1, NKEYS // WR - 1)

        @block.vector
        def _(dve):
            v = nc.vector
            link = Link(dve, s_dl)
            npd, nad, npe = [0], [0], [0]

            def ask_pe(ins):
                ins.then_inc(s_pe, 1)
                npe[0] += 1

            def ask_pe_and_wait(ins):
                ask_pe(ins)
                dve.wait_ge(s_pe, npe[0])

            def pe_done():
                npd[0] += 1
                dve.wait_ge(s_pd, npd[0])

            def act_done(n=1):
                nad[0] += n
                dve.wait_ge(s_ad, nad[0])

            nrs = [0]

            def rsqrt(ins):
                ins.then_inc(s_var, 1)
                nrs[0] += 1
                dve.wait_ge(s_rs, nrs[0])

            def norm(l, k):
                dve.wait_ge(s_ss, 2 * l + k + 1)
                rsqrt(v.tensor_scalar(acts[:, 0, :], ps[:, 0, 0:T], 1.0 / D, NORM_EPS, ALU.mult, ALU.add))
                for c in range(DC):
                    v.scalar_tensor_tensor(xn[:, c, :], h[:, c, :], vcol(l, "norm2" if k else "norm1", c),
                                           acts[:, 0, :], ALU.mult, ALU.mult).then_inc(s_xn, 1)

            for l in range(DEPTH):
                if l == 0:
                    dve.wait_ge(s_h, 48)
                norm(l, 0)
                dve.wait_ge(s_mix, 32 * (l + 1))
                link(v.memset(z[:, :, 0:1], 0.0))
                dve.wait_ge(s_ea, l * (NZ + NQ) + 8)
                for c in (6, 7, 0, 1, 2, 3, 4, 5):
                    link(v.tensor_tensor(t1[:, 0, :], z[:, c, 0:T], z[:, c, 1:T + 1], ALU.subtract))
                    ins = v.scalar_tensor_tensor(zs[:, c, :], t1[:, 0, :], vcol(l, "mu", c), z[:, c, 1:T + 1],
                                                 ALU.mult, ALU.add)
                    if c in (6, 7):
                        ins.then_inc(s_zs, 1)
                        dve.wait_ge(s_zs, 2 * l + c - 5)
                    else:
                        link(ins)
                r_, k_, v_ = zs[:, 0:2, :], zs[:, 2:4, :], zs[:, 4:6, :]
                for j in range(2):
                    link(v.tensor_scalar(kk[:, j, :], k_[:, j, :], vcol(l, "k_k", j), None, ALU.mult))
                ask_pe(v.tensor_tensor(t2[:, :, :], kk[:, :, :], kk[:, :, :], ALU.mult))
                link(v.memset(lw[:, :, 0:PAD], 0.0))
                dve.wait_ge(s_ag, 6 * (l + 1))
                link(v.tensor_scalar(lw[:, :, PAD:TP], ea[:, :, :], -float(np.exp(-0.5)), None, ALU.mult))
                for j in range(2):
                    for c in range(NCH):
                        w = slice(c * CHUNK, (c + 1) * CHUNK)
                        link(v.tensor_tensor_scan(cum[:, j, w], ones[:, 0:CHUNK], lw[:, j, w], 0.0,
                                                  ALU.mult, ALU.add))
                v.tensor_tensor(lw[:, :, :], cum[:, :, :], lw[:, :, :], ALU.subtract).then_inc(s_ar, 1)
                for a in (al, be, ka, rh):
                    link(v.memset(a[:, :, 0:PAD], 0.0))
                for j in range(2):
                    link(v.tensor_scalar(t1[:, j, :], aa[:, j, :], -1.0, vcol(l, "k_a", j), ALU.add, ALU.mult))
                link(v.scalar_tensor_tensor(km[:, :, :], t1[:, :, :], 1.0, k_, ALU.add, ALU.mult))
                for j in range(2):
                    link(v.scalar_tensor_tensor(t1[:, j, :], r_[:, j, :], vcol(l, "r_k", j), km[:, j, :],
                                                ALU.mult, ALU.mult))
                link(v.memset(t3[:, :, 0:PAD], 0.0))
                ask_pe(v.tensor_copy(t3[:, :, PAD:TP], v_))
                pe_done()
                for j in range(2):
                    (link, rsqrt)[j](v.tensor_scalar(t2[:, j, :], ps[:, 3 + j, 0:T], 1e-12, None, ALU.max))
                link(v.tensor_tensor(kk[:, :, :], kk[:, :, :], t2[:, :, :], ALU.mult))
                link(v.tensor_tensor(bb[:, :, :], kk[:, :, :], aa[:, :, :], ALU.mult))
                pe_done()
                for j in range(2):
                    link(v.tensor_tensor(bonus[:, j, :], ps[:, 5 + j, 0:T], v_[:, j, :], ALU.mult))
                act_done(3)
                w = slice(PAD, TP)
                link(v.tensor_tensor(al[:, :, w], dexc[:, :, w], kk[:, :, :], ALU.mult))
                link(v.tensor_tensor(be[:, :, w], dinv[:, :, w], bb[:, :, :], ALU.mult))
                link(v.tensor_tensor(ka[:, :, w], dinv[:, :, w], km[:, :, :], ALU.mult))
                link(v.memset(state[:, :, :], 0.0))
                ask_pe(v.tensor_tensor(rh[:, :, w], dall[:, :, w], r_, ALU.mult))
                for c in range(NCH):
                    for m, dst in enumerate((vtok, ktok, btok)):
                        k = 3 * c + m
                        pe_done()
                        ins = v.tensor_copy(dst[:, c, :, :].rearrange("p j n -> p (j n)"),
                                            ps[0:CHUNK, 3 + k % 2, 0:2 * P])
                        if k == 3 * NCH - 2:
                            link(ins)
                        else:
                            ask_pe_and_wait(ins)
                for c in range(NCH):
                    pe_done()
                    for q in range(2):
                        link(v.tensor_tensor(gram[:, c, q, :, :, :].rearrange("p j m t -> p j (m t)"),
                                             ps[0:CHUNK, 3 + q, :].rearrange("p (j m) -> p j m", j=2),
                                             bc(mask4.rearrange("p m t -> p (m t)"), 1, 2), ALU.mult))
                        n0 = c * 4 + q * 2
                        link(v.tensor_tensor(ti[:, n0:n0 + 2, :],
                                             ps[0:CHUNK, 5 + q, 0:2 * CHUNK].rearrange("p (j t) -> p j t", j=2),
                                             bc(negm1, 1, 2), ALU.mult))
                        ins = v.tensor_tensor(ti[:, n0:n0 + 2, :], ti[:, n0:n0 + 2, :],
                                              bc(ident[0:CHUNK, 0:CHUNK], 1, 2), ALU.add)
                        if q == 1 and c < NCH - 1:
                            ask_pe_and_wait(ins)
                        else:
                            link(ins)
                gl = gram.rearrange("p c q j m t -> p (c q j) m t")[:, :, 2, :]
                link(v.tensor_tensor(cm[:, :, :], gl, bc(mT[:, 0, :], 1, NMAT), ALU.mult))
                link(v.scalar_tensor_tensor(tt_[:, :, :], cm[:, :, :], -1.0,
                                            bc(ident[0:CHUNK, 0:CHUNK], 1, NMAT), ALU.mult, ALU.add))
                for b in range(1, len(LEVELS)):
                    ask_pe(v.tensor_tensor(cm[:, :, :], gl, bc(mT[:, b, :], 1, NMAT), ALU.mult))
                    pe_done()
                    pe_done()
                    pe_done()
                    for g in range(3):
                        n0, n1 = 8 * g, min(8 * g + 8, NMAT)
                        bank = (6, 7, 0)[g]
                        link(v.tensor_tensor(ti[:, n0:n1, :].rearrange("p n t -> p (n t)"),
                                             ti[:, n0:n1, :].rearrange("p n t -> p (n t)"),
                                             ps[0:CHUNK, bank, 0:(n1 - n0) * CHUNK], ALU.subtract))
                        ins = v.tensor_tensor(tt_[:, n0:n1, :].rearrange("p n t -> p (n t)"),
                                              tt_[:, n0:n1, :].rearrange("p n t -> p (n t)"),
                                              ps[0:CHUNK, 3 + g, 0:(n1 - n0) * CHUNK], ALU.subtract)
                        (ask_pe if (b, g) == (len(LEVELS) - 1, 2) else link)(ins)
                nad[0] += len(LEVELS) - 1
                for c in range(NCH):
                    w = slice(c * CHUNK, (c + 1) * CHUNK)
                    pe_done()
                    ask_pe(v.tensor_copy(xs[:, :, :].rearrange("p j n -> p (j n)"), ps[0:CHUNK, 3, 0:2 * P]))
                    pe_done()
                    ask_pe(v.tensor_scalar(us[:, :, :].rearrange("p j n -> p (j n)"), ps[0:CHUNK, 4, 0:2 * P], -1.0,
                                           None, ALU.mult))
                    pe_done()
                    link(v.tensor_tensor(stmp[:, :, :].rearrange("p j n -> p (j n)"), ps[:, 5, 0:2 * P],
                                         state[:, :, :].rearrange("p j n -> p (j n)"), ALU.add))
                    link(v.tensor_copy(yT[:, :, w], ps[:, 6, 0:2 * CHUNK].rearrange("p (j t) -> p j t", j=2)))
                    e = (c + 1) * CHUNK
                    link(v.scalar_tensor_tensor(state[:, 0, :], stmp[:, 0, :], dall[:, 0, e - 1:e], blk,
                                                ALU.mult, ALU.mult))
                    ask_pe_and_wait(v.scalar_tensor_tensor(state[:, 1, :], stmp[:, 1, :], dall[:, 1, e - 1:e], blk,
                                                           ALU.mult, ALU.mult))
                pe_done()
                for j in range(2):
                    link(v.scalar_tensor_tensor(t1[:, j, :], ps[:, 3 + j, 0:T], -1.0 / HD, yT[:, j, PAD:TP],
                                                ALU.mult, ALU.add))
                ask_pe(v.tensor_tensor(t2[:, :, :], t1[:, :, :], t1[:, :, :], ALU.mult))
                pe_done()
                for j in range(2):
                    (link, rsqrt)[j](v.tensor_scalar(t2[:, j, :], ps[:, 3 + j, 0:T], 1.0 / HD, GN_EPS,
                                                     ALU.mult, ALU.add))
                link(v.tensor_tensor(t1[:, :, :], t1[:, :, :], t2[:, :, :], ALU.mult))
                for j in range(2):
                    link(v.tensor_scalar(t1[:, j, :], t1[:, j, :], vcol(l, "gn_g", j), vcol(l, "gn_b", j),
                                         ALU.mult, ALU.add))
                link(v.tensor_tensor(t1[:, :, :], t1[:, :, :], bonus[:, :, :], ALU.add))
                link(v.tensor_tensor(cat[:, 4:6, :], t1[:, :, :], gg[:, :, :], ALU.mult))
                dve.wait_ge(s_ea, l * (NZ + NQ) + NZ)
                v.memset(cu[:, :, 0:CPAD], 0.0).then_inc(s_ar, 1)
                act_done(2)
                link(v.tensor_tensor(cu[:, :, CPAD:CPAD + T], z[:, ZCU:ZCU + 2, 1:T + 1], cacc[:, :, :], ALU.mult))
                for k in range(CONV_K):
                    for j in range(2):
                        wk = vcol(l, "conv_w", j * CONV_K + k)
                        if k == 0:
                            ins = v.tensor_scalar(cacc[:, j, :], cu[:, j, 0:T], wk, vcol(l, "conv_b", j),
                                                  ALU.mult, ALU.add)
                        else:
                            ins = v.scalar_tensor_tensor(cacc[:, j, :], cu[:, j, k:k + T], wk, cacc[:, j, :],
                                                         ALU.mult, ALU.add)
                        if k == CONV_K - 1 and j == 1:
                            ask_pe(ins)
                        else:
                            link(ins)
                pe_done()
                for j in range(2):
                    link(v.scalar_tensor_tensor(cacc[:, j, :], ps[:, 3, 0:T], -1.0 / (2 * P), cacc[:, j, :],
                                                ALU.mult, ALU.add))
                ask_pe(v.tensor_tensor(t2[:, :, :], cacc[:, :, :], cacc[:, :, :], ALU.mult))
                pe_done()
                rsqrt(v.tensor_scalar(t3[:, 0, 0:T], ps[:, 3, 0:T], 1.0 / (2 * P), NORM_EPS, ALU.mult, ALU.add))
                link(v.tensor_tensor(t1[:, :, :], cacc[:, :, :], bc(t3[:, 0, 0:T], 1, 2), ALU.mult))
                for j in range(2):
                    ins = v.tensor_scalar(t1[:, j, :], t1[:, j, :], vcol(l, "ln_g", j), vcol(l, "ln_b", j),
                                          ALU.mult, ALU.add)
                    link(ins) if j == 0 else ins.then_inc(s_ar, 1)
                ask_pe(v.tensor_tensor(sq[:, 0:5, :], z[:, ZQ:ZQ + 5, 1:T + 1], z[:, ZQ:ZQ + 5, 1:T + 1], ALU.mult))
                pe_done()
                for c in range(5):
                    (rsqrt if c == 4 else link)(v.tensor_scalar(qn[:, c, :], ps[:, 3 + c, 0:T], 1.0 / HD, NORM_EPS,
                                                                ALU.mult, ALU.add))
                for c in range(5):
                    link(v.scalar_tensor_tensor(qn[:, c, :], z[:, ZQ + c, 1:T + 1], vcol(l, "kg" if c == 4 else "qg"),
                                                qn[:, c, :], ALU.mult, ALU.mult))
                for src, dst in ((qn[:, 4, :], kcat), (z[:, ZV, 1:T + 1], vcat)):
                    link(v.tensor_copy(dst[:, 0:NMETA], src[:, 0:NMETA]))
                    ins = v.tensor_copy(dst[:, NMETA:208], src[:, 80:T])
                    (link if dst is kcat else ask_pe)(ins)
                act_done(1)
                link(v.tensor_tensor(cat[:, 6:8, :], t1[:, :, :], t2[:, :, :], ALU.mult))
                pe_done()
                for s, (src, k0, nk, (sl, b)) in enumerate(V_TILES):
                    ins = v.tensor_copy(vkey[0:nk, sl, b, :], ps[0:nk, 3 + s % 2, (s // 2) * P:(s // 2 + 1) * P])
                    (ask_pe_and_wait if s == len(V_TILES) - 1 else link)(ins)
                for s, (q0, nq) in enumerate(TILES):
                    nk = KEYS_OF[s]
                    dist = mix(("distM", "distA", "distB")[s], nq)
                    pr = prob[0:nq, 0:AH * nk].rearrange("p (h k) -> p h k", h=AH)
                    m_, nm, rs, es, rd = (small[0:nq, i, :] for i in range(5))
                    sink = vecs[0:nq, l, VEC["sink"][0]:VEC["sink"][0] + AH]
                    for hh in range(AH):
                        pe_done()
                        ins = v.scalar_tensor_tensor(pr[:, hh, :], dist, -SLOPES[hh] * HD ** 0.5,
                                                     ps[0:nq, 3 + hh % 2, 0:nk], ALU.mult, ALU.add)
                        if hh < AH - 2:
                            ask_pe_and_wait(ins)
                        else:
                            link(ins)
                    link(v.tensor_reduce(m_, pr, AX.X, ALU.max))
                    link(v.scalar_tensor_tensor(m_, m_, HD ** -0.5, sink, ALU.mult, ALU.max))
                    link(v.tensor_scalar(nm, m_, -1.0, None, ALU.mult))
                    v.tensor_tensor(es, sink, m_, ALU.subtract).then_inc(s_ar, 1)
                    act_done(1)
                    link(v.tensor_tensor(rs, rs, es, ALU.add))
                    link(v.reciprocal(rd, rs))
                    ask_pe(v.tensor_tensor(pr, pr, bc(rd, 2, nk), ALU.mult))
                    for hh in range(AH):
                        pe_done()
                        for b, (k0, kn) in enumerate(splits(nk)):
                            ins = v.tensor_copy(pT[0:kn, hh % 2, b, 0:nq], ps[0:kn, 5 + hh % 2, b * P:b * P + nq])
                            (ask_pe if k0 + kn == nk else link)(ins)
                        pe_done()
                        q, c = hh // 4, hh % 4
                        ins = v.tensor_copy(cat[q * HD:(q + 1) * HD, c, q0:q0 + nq],
                                            ps[q * HD:(q + 1) * HD, 7 - 7 * (hh % 2), 0:nq])
                        ask_pe_and_wait(ins)
                for m in range(NOUT):
                    dve.wait_ge(s_pj, l * NPROJ + NZ + m + 1)
                    v.tensor_tensor(h[:, m, :], h[:, m, :], ps[:, 1 + (NZ + m) % 2, 0:T], ALU.add).then_inc(s_ed, 1)
                dve.wait_ge(s_ed, (l + 1) * NOUT)
                norm(l, 1)
                for s, (t0, nt) in enumerate(TILES):
                    dve.wait_ge(s_sc, l * 4 * NT + 4 * s + 4)
                    hs = [(hh, p) for hh in range(PH) for p in range(2)]
                    score = lambda hh, p: sc[0:nt, s, 2 * hh + p, :]

                    def top16(items, val, idx, src):
                        def each(f):
                            for it_ in items[:-1]:
                                f(*it_).then_inc(s_dl, 1)
                                link.n += 1
                            link(f(*items[-1]))

                        each(lambda *a: v.max(val(*a)[:, 0:8], src(*a)))
                        each(lambda *a: v.max_index(idx(*a)[:, 0:8], val(*a)[:, 0:8], src(*a)))
                        each(lambda *a: v.match_replace(src(*a), val(*a)[:, 0:8], src(*a), NEG))
                        each(lambda *a: v.max(val(*a)[:, 8:16], src(*a)))
                        each(lambda *a: v.max_index(idx(*a)[:, 8:16], val(*a)[:, 8:16], src(*a)))

                    top16(hs, lambda hh, p: topv[0:nt, hh, p, :], lambda hh, p: topi_u[0:nt, hh, p, :], score)
                    link(v.tensor_copy(topf[0:nt].rearrange("p h s k -> p (h s k)"),
                                       topi_u[0:nt].rearrange("p h s k -> p (h s k)")))
                    cb = comb[0:nt].rearrange("p h (a b) -> p h a b", a=TOPK)
                    link(v.tensor_tensor(cb, bc(topv[0:nt, :, 0, :], 3, TOPK), bc(topv[0:nt, :, 1, :], 2, TOPK),
                                         ALU.add))
                    fvh = fv[0:nt].rearrange("p (h k) -> p h k", h=PH)
                    fih = fi_u[0:nt].rearrange("p (h k) -> p h k", h=PH)
                    top16([(hh,) for hh in range(PH)], lambda hh: fvh[:, hh, :], lambda hh: fih[:, hh, :],
                          lambda hh: comb[0:nt, hh, :])
                    link(v.tensor_scalar(fa_u[0:nt, 0, :], fi_u[0:nt], 4, None, ALU.logical_shift_right))
                    link(v.tensor_scalar(fa_u[0:nt, 1, :], fi_u[0:nt], 15, None, ALU.bitwise_and))
                    link(v.tensor_copy(ff[0:nt].rearrange("p s n -> p (s n)"),
                                       fa_u[0:nt].rearrange("p s n -> p (s n)")))
                    gh = chosen[0:nt, 0, :].rearrange("p (h k) -> p h k", h=PH)
                    v.tensor_tensor(gh, fvh, fvh[:, :, 0:1].broadcast_to([nt, PH, TOPK]),
                                    ALU.subtract).then_inc(s_ar, 1)
                    e4 = eqm[0:nt].rearrange("p (n a) -> p n a", a=TOPK)
                    e5 = eqm[0:nt].rearrange("p (h k a) -> p h k a", h=PH, a=TOPK)
                    for p in range(2):
                        link(v.tensor_tensor(e4, bc(ff[0:nt, p, :], 2, TOPK), bc(iota[0:nt, 0:TOPK], 1, P),
                                             ALU.is_equal))
                        link(v.tensor_tensor(e5, e5, bc(topf[0:nt, :, p, :], 2, TOPK), ALU.mult))
                        link(v.tensor_reduce(chosen[0:nt, 1 + p, :], e4, AX.X, ALU.add))
                    act_done(1)
                    link(v.tensor_reduce(gsum[0:nt, :], gh, AX.X, ALU.add))
                    link(v.reciprocal(gsum[0:nt, :], gsum[0:nt, :]))
                    ask_pe(v.tensor_tensor(gh, gh, bc(gsum[0:nt, :], 2, TOPK), ALU.mult))
                    pe_done()
                    v.tensor_copy(sel[:, :, t0:t0 + nt],
                                  ps[:, 5 + s % 2, 0:3 * P].rearrange("p (m n) -> p m n", m=3)[:, :, 0:nt]
                                  ).then_inc(s_sel, 1)
                dve.wait_ge(s_sel, NT * (l + 1))

                def gated(t0, b):
                    for t in range(OHT):
                        v.tensor_scalar(onehot[:, b, 0, t, :], iota, sel[:, 1, bass.ds(t0 + t, 1)],
                                        sel[:, 0, bass.ds(t0 + t, 1)], ALU.is_equal, ALU.mult)
                    v.tensor_tensor(onehot[:, b, 1], bc(iota, 1, OHT), bc(sel[:, 2, bass.ds(t0, OHT)], 2, P),
                                    ALU.is_equal).then_inc(s_oh, 1)

                for b in range(2):
                    gated(b * OHT, b)
                with dve.Fori(0, NSTEP // 2 - 1) as it:
                    for b in range(2):
                        dve.wait_ge(s_gp, 2 * it + l * NSTEP + b + 1)
                        gated(2 * OHT * it + (2 + b) * OHT, b)
                dve.wait_ge(s_g, (l + 1) * NSTEP)
                with dve.Fori(0, NKEYS // 2) as it:
                    for b in range(2):
                        dve.wait_ge(s_gelu, 2 * it + l * NKEYS + b + 1)
                        v.tensor_tensor(acts[:, b, :], acts[:, b, :], gates[:, bass.ds(2 * it + b, 1), :].squeeze(1),
                                        ALU.mult).then_inc(s_act, 1)
                dve.wait_ge(s_vu, (l + 1) * NKEYS)
                hf = h_t[:, :]
                for k in range(-(-YCOLS // 512)):
                    a, e = 512 * k, min(512 * (k + 1), YCOLS)
                    ins = v.tensor_tensor(hf[:, a:e], hf[:, a:e], psf[:, YB * 512 + a:YB * 512 + e], ALU.add)
                    if e < YCOLS:
                        link(ins)
                    else:
                        ins.then_inc(s_hd, 1)
                dve.wait_ge(s_hd, l + 1)


def weight_tiles(w):
    n = w.shape[1] // P
    return w.reshape(DC, P, n, P).transpose(2, 1, 0, 3).reshape(n, P, D)


def lay_out(a):
    f = {k: np.asarray(v) for k, v in a.items()}
    tokens = np.concatenate([f["meta"], f["x"][0]], 0)
    h0 = tokens.T.reshape(DC, P, T).transpose(1, 0, 2).reshape(P, DC * T)
    res, mix = constants()
    vec = np.zeros((P, DEPTH, NVEC), np.float32)
    lora = np.zeros((DEPTH, P, 2, 2 * P), np.float32)
    attn, rwkv = 768, 1024
    q_cols = np.concatenate([np.arange(HD) + HD * hh for c in range(4) for hh in (c, c + 4)])
    cols = np.concatenate([attn + np.arange(rwkv), attn + rwkv + np.arange(512), q_cols, 512 + np.arange(256)])
    rows = np.concatenate([q_cols, 512 + np.arange(512)])
    w, u, keys = [], [], []
    for l in range(DEPTH):
        def put(name, value):
            at, n = VEC[name]
            vec[:, l, at:at + n] = value

        for name, key in (("norm1", "norm1_g"), ("norm2", "norm2_g"), ("mu", "rwkv_mu"), ("w0", "rwkv_w0"),
                          ("a0", "rwkv_a0"), ("k_k", "rwkv_k_k"), ("k_a", "rwkv_k_a"), ("r_k", "rwkv_r_k"),
                          ("gn_g", "rwkv_gn_g"), ("gn_b", "rwkv_gn_b"), ("conv_b", "conv_b"),
                          ("ln_g", "conv_ln_g"), ("ln_b", "conv_ln_b")):
            put(name, f[key][l].reshape(-1, P).T)
        put("qg", np.concatenate([f["q_norm_g"][l]] * 2)[:, None])
        put("kg", np.concatenate([f["k_norm_g"][l]] * 2)[:, None])
        put("conv_w", f["conv_w"][l].reshape(CONV_K, 2, P).transpose(2, 1, 0).reshape(P, 2 * CONV_K))
        put("sink", np.broadcast_to(f["attn_sinks"][l], (P, AH)))
        lora[l, 0:HD, 0] = f["rwkv_w_lora"][l]
        lora[l, HD:P, 0] = f["rwkv_a_lora"][l]
        lora[l, :, 1] = f["rwkv_g_lora"][l]
        w.append(np.concatenate([weight_tiles(f["w_in"][l][:, cols]), weight_tiles(f["w_out"][l][rows]),
                                 weight_tiles(f["peer_wq"][l])], 0))
        u.append(f["peer_u"][l].reshape(NKEYS, P, DC, P).transpose(0, 3, 2, 1).reshape(NKEYS, P, D))
        keys.append(f["peer_keys"][l].reshape(NQ, NKEYS, P).transpose(2, 0, 1).reshape(P, NQ * NKEYS))
    return dict(h0=h0, vec=vec.reshape(P, DEPTH * NVEC), res_c=res, mix_c=mix,
                lora_c=lora.reshape(DEPTH, P, 4 * P), keys_c=np.stack(keys), w_c=np.stack(w), u_c=np.stack(u),
                v_c=f["peer_v"].reshape(DEPTH, NKEYS, P, D))


def kernel(**inputs):
    import concourse.bacc as bacc
    from concourse.bass_utils import run_bass_kernel_spmd

    arrays = {k: np.ascontiguousarray(a) for k, a in lay_out(inputs).items()}
    nc = bacc.Bacc("TRN2", target_bir_lowering=False, num_devices=1)
    aps = {k: nc.dram_tensor(k, a.shape, mybir.dt.from_np(a.dtype), kind="ExternalInput").ap()
           for k, a in arrays.items()}
    out = nc.dram_tensor("out", (P, DC, SEQ), F32, kind="ExternalOutput").ap()
    trunk(nc, out=out, **aps)
    got = run_bass_kernel_spmd(nc, [arrays], core_ids=[0]).results[0]["out"]
    return got.transpose(2, 1, 0).reshape(1, SEQ, D)
```

```python
from contextlib import ExitStack

import numpy as np
import concourse.bass as bass
from concourse import mybir

ALU = mybir.AluOpType
ACT = mybir.ActivationFunctionType
AX = mybir.AxisListType
F32 = mybir.dt.float32
F32R = mybir.dt.float32r
U32 = mybir.dt.uint32

P = 128
D = 1024
DC = D // P
SEQ = 256
NMETA = 16
T = SEQ + NMETA
DEPTH = 2
HD = 64
NORM_EPS = 1e-6
GN_EPS = 64e-5
CHUNK = 64
ZR, ZCU, ZCG, ZQ, ZK, ZV = 0, 8, 10, 12, 16, 17
NZ = 18
NOUT = D // P
NCH = -(-T // CHUNK)
PAD = NCH * CHUNK - T
TP = NCH * CHUNK
NMAT = NCH * 4
LEVELS = (1, 2, 4, 8, 16, 32)
CONV_K = 31
CPAD = CONV_K - 1
AH = 8
PH = 8
NKEYS = 128
TOPK = 16
NQ = PH * 2
TILES = ((0, NMETA), (NMETA, P), (NMETA + P, P))
NT = len(TILES)
NEG = -3.0e38
FAR = 1.0e30
VEC = dict(norm1=(0, 8), norm2=(8, 8), qg=(16, 1), kg=(17, 1), mu=(18, 8), w0=(26, 2), a0=(28, 2), k_k=(30, 2),
           k_a=(32, 2), r_k=(34, 2), gn_g=(36, 2), gn_b=(38, 2), conv_b=(40, 2), ln_g=(42, 2), ln_b=(44, 2),
           conv_w=(46, 2 * CONV_K), sink=(46 + 2 * CONV_K, AH))
NVEC = 46 + 2 * CONV_K + AH
RES = dict(ident=(0, P), ones=(P, P), iota=(2 * P, P))
NRES = 3 * P
MIX = {}
NMIX = 0
for _name, _n in (("blk", P), ("mask4", 4 * CHUNK), ("negm1", CHUNK), ("mT", len(LEVELS) * CHUNK),
                  ("distM", NMETA), ("distA", 144), ("distB", 208)):
    MIX[_name] = (NMIX, _n)
    NMIX += _n
WR = 4
AHEAD = WR - 2
NPROJ = NZ + NOUT + NQ
NU0 = NPROJ
NV0 = NU0 + NKEYS
NW = NV0 + NKEYS
OHT = 4


class Layer:

    def __init__(self, l):
        self.last = l == DEPTH - 1
        self.t0 = NMETA if self.last else 0
        self.nt = T - self.t0
        self.steps = self.nt // OHT
        self.split = NKEYS - self.steps
        self.quiet = 56 if not self.last else 40
        self.tiles = [x for x in TILES if x[0] >= self.t0]
        if 2 * self.nt <= 512:
            self.gate_banks = (0, 1)
            self.out_at = [[(4 + c // 2, (c % 2) * self.nt, 0, self.nt)] for c in range(DC)]
        else:
            self.gate_banks = (0, 0)
            self.out_at = [[(1 + c, 0, 0, self.nt)] for c in range(DC - 1)]
            rest = 512 - self.nt
            self.out_at.append([(1, self.nt, 0, rest), (2, self.nt, rest, self.nt - rest)])
        assert self.split % WR == 0 and self.quiet % WR == 0 and self.quiet <= self.split


LAYERS = [Layer(l) for l in range(DEPTH)]
G0 = [sum(2 * LAYERS[m].steps for m in range(l)) for l in range(DEPTH + 1)]
SC0 = [sum(4 * len(LAYERS[m].tiles) for m in range(l)) for l in range(DEPTH)]
KEYS_OF = (NMETA, 144, 208)
V_TILES = (("z", 0, P, (0, 0)), ("z", P, 16, (0, 1)), ("vcat", 0, P, (1, 0)), ("vcat", P, 80, (1, 1)))
INV = 2 + 3 * NCH + NCH
PE0, ACT0 = [0], [0]
for _l in range(DEPTH):
    _n = len(LAYERS[_l].tiles)
    PE0.append(PE0[-1] + INV + 3 * (len(LEVELS) - 1) + 3 * NCH + 2 + 2 + 1 + 1 + 3 * AH * _n + 1)
    ACT0.append(ACT0[-1] + 3 + (len(LEVELS) - 1) + 1 + _n + 1)
SLOPES = [2.0 ** (-8.0 * (h + 1) / AH) for h in range(AH)]


def constants():
    res = np.zeros((P, NRES), np.float32)
    res[:, 0:P] = np.eye(P)
    res[:, P:2 * P] = 1.0
    res[:, 2 * P:3 * P] = np.arange(P)[None]
    mix = np.zeros((P, NMIX), np.float32)

    def put(name, a):
        a = np.asarray(a, np.float32)
        mix[:a.shape[0], MIX[name][0]:MIX[name][0] + MIX[name][1]] = a.reshape(a.shape[0], -1)

    p = np.arange(P)
    put("blk", p[:, None] // HD == p[None] // HD)
    s, t = np.arange(CHUNK)[:, None], np.arange(CHUNK)[None]
    put("mask4", np.stack([s < t, s <= t, s < t, s <= t], 1))
    cross = lambda b, r, c: (r // (2 * b) == c // (2 * b)) & ((r // b) % 2 == 1) & ((c // b) % 2 == 0)
    put("negm1", -1.0 * cross(1, s, t))
    put("mT", np.stack([cross(b, t, s) for b in LEVELS], 1))
    put("distM", np.abs(np.arange(NMETA)[:, None] - np.arange(NMETA)[None]))

    def dist(q0, keys):
        q = q0 + np.arange(P)[:, None]
        k = np.asarray(keys)[None]
        qc, kc = (q - NMETA) // CHUNK, (k - NMETA) // CHUNK
        ok = (k < NMETA) | ((kc <= qc) & (kc >= qc - 1))
        return np.where(ok, np.abs(q - k), FAR)

    put("distA", dist(NMETA, range(0, 144)))
    put("distB", dist(NMETA + P, list(range(16)) + list(range(80, 272))))
    return res, mix


class Link:

    def __init__(self, eng, sem):
        self.eng, self.sem, self.n = eng, sem, 0

    def __call__(self, ins):
        ins.then_inc(self.sem, 1)
        self.n = self.n + 1
        self.eng.wait_ge(self.sem, self.n)


class Arena:

    def __init__(self, tensor, start=0):
        self.t, self.at = tensor, start

    def take(self, n, parts=P):
        a = self.t[0:parts, self.at:self.at + n]
        self.at += n
        assert self.at <= self.t.shape[1], self.at
        return a


def splits(n):
    return [(a, min(P, n - a)) for a in range(0, n, P)]


def bc(ap, axis, n):
    a = ap.unsqueeze(axis)
    shape = list(a.shape)
    shape[axis] = n
    return a.broadcast_to(shape)


def trunk(nc, h0, vec, res_c, mix_c, lora_c, keys_c, w_c, u_c, v_c, out):
    with ExitStack() as ctx:
        def sb(name, cols, dt=F32, parts=P):
            return ctx.enter_context(nc.sbuf_tensor(name, [parts, cols], dt))

        def twice(raw, low, cols):
            with nc.sbuf_tensor(raw, [P, cols], F32) as a:
                pass
            return a, sb(low, cols, F32R)

        def sem(name):
            return ctx.enter_context(nc.semaphore(name))

        h_t = sb("h", DC * T)
        xh_t = sb("x_hi", DC * T, F32R)
        xn_t, xl_t = twice("x", "x_lo", DC * T)
        res_t = sb("res", NRES)
        vec_t = sb("vecs", DEPTH * NVEC)
        whi_t = sb("w_hi", WR * D, F32R)
        wraw_t, wlo_t = twice("w", "w_lo", WR * D)
        sel_t = sb("sel", 3 * T)
        ohB_t = sb("onehots_j", 2 * OHT * P)
        ohA_t = sb("onehots_i", 2 * OHT * 68)
        zero_t = sb("zeros", P)
        arena_t = sb("arena", P * T)
        ps = ctx.enter_context(nc.psum_tensor("ps", [P, 8, 512], F32))

        h = h_t[:, :].rearrange("p (c t) -> p c t", c=DC)
        tok = lambda t: t[:, :].rearrange("p (c t) -> p c t", c=DC)
        xn, xh, xl = tok(xn_t), tok(xh_t), tok(xl_t)
        vecs = vec_t[:, :].rearrange("p (l n) -> p l n", l=DEPTH)
        ring = lambda t: t[:, :].rearrange("p (s k c) -> p s k c", s=WR, k=DC)
        whi, wlo = ring(whi_t), ring(wlo_t)
        sel = sel_t[:, :].rearrange("p (s t) -> p s t", s=3)
        ohB = ohB_t[:, :].rearrange("p (b t n) -> p b t n", b=2, t=OHT)
        ohA = ohA_t[:, :].rearrange("p (b t n) -> p b t n", b=2, t=OHT)
        var = ohB_t[:, 0:T]
        act_hi = xh_t[:, 0:2 * T].rearrange("p (b t) -> p b t", b=2)
        act_lo = xh_t[:, 2 * T:4 * T].rearrange("p (b t) -> p b t", b=2)
        hid = [arena_t[:, 0:P * L.nt].rearrange("p (i t) -> p i t", i=P) for L in LAYERS]

        def res(name):
            a, n = RES[name]
            return res_t[:, a:a + n]

        ident, ones, iota = res("ident"), res("ones"), res("iota")

        def vcol(l, name, i=0, parts=slice(0, P)):
            a = VEC[name][0] + i
            return vecs[parts, l, a:a + 1]

        A = Arena(arena_t)
        mix_m = A.take(NMIX)
        lora = A.take(4 * P).rearrange("p (s n) -> p s n", s=2)
        sq = A.take(DC * T).rearrange("p (c t) -> p c t", c=DC)
        z = A.take(NZ * (T + 1)).rearrange("p (c t) -> p c t", c=NZ)
        cat = A.take(DC * T).rearrange("p (c t) -> p c t", c=DC)
        mixed_end = A.at

        def two(n=T):
            return A.take(2 * n).rearrange("p (j t) -> p j t", j=2)

        cu = A.take(2 * (CPAD + T)).rearrange("p (j t) -> p j t", j=2)
        cacc, ctmp = two(), two()
        bonus, gg = two(), two()
        al, be, ka, rh = two(TP), two(TP), two(TP), two(TP)
        dall = two(TP)
        yT = two(TP)
        t1, t2, t3 = two(), two(), two(TP)
        vtok = A.take(NCH * 2 * P, CHUNK).rearrange("p (c j n) -> p c j n", c=NCH, j=2)
        ktok = A.take(NCH * 2 * P, CHUNK).rearrange("p (c j n) -> p c j n", c=NCH, j=2)
        btok = A.take(NCH * 2 * P, CHUNK).rearrange("p (c j n) -> p c j n", c=NCH, j=2)
        state = A.take(2 * P).rearrange("p (j n) -> p j n", j=2)
        stmp = A.take(2 * P).rearrange("p (j n) -> p j n", j=2)
        xs = A.take(2 * P, CHUNK).rearrange("p (j n) -> p j n", j=2)
        us = A.take(2 * P, CHUNK).rearrange("p (j n) -> p j n", j=2)
        over = A.at
        zs = A.take(8 * T).rearrange("p (c t) -> p c t", c=8)
        th = A.take(T)
        sg = A.take(T)
        ea, aa = two(), two()
        lw, cum = two(TP), two(TP)
        dinv, dexc = two(TP), two(TP)
        kk, km, bb = two(), two(), two()
        over_prep = A.at
        A.at = over
        gram = A.take(NCH * 2 * 2 * 4 * CHUNK, CHUNK).rearrange("p (c q j m t) -> p c q j m t", c=NCH, q=2, j=2, m=4)
        mats = lambda: A.take(NMAT * CHUNK, CHUNK).rearrange("p (n t) -> p n t", n=NMAT)
        ti, tt_, xm, cm = mats(), mats(), mats(), mats()
        over_mats = A.at
        A.at = over
        qn = A.take(5 * T).rearrange("p (c t) -> p c t", c=5)
        kcat = A.take(208)
        vcat = A.take(208)
        vkey = A.take(2 * 2 * P).rearrange("p (s k n) -> p s k n", s=2, k=2)
        prob = A.take(AH * 208)
        pT = A.take(2 * 2 * P).rearrange("p (b k n) -> p b k n", b=2, k=2)
        small = A.take(8 * AH).rearrange("p (s h) -> p s h", s=8)
        over_attn = A.at
        A.at = 56 * T
        keys = A.take(NQ * P).rearrange("p (m n) -> p m n", m=NQ)
        pq = A.take(NQ * T).rearrange("p (m t) -> p m t", m=NQ)
        sc = A.take(NT * NQ * P).rearrange("p (s m n) -> p s m n", s=NT, m=NQ)
        comb = A.take(PH * TOPK * TOPK).rearrange("p (h n) -> p h n", h=PH)
        eqm = A.take(PH * TOPK * TOPK)
        topv = A.take(NQ * TOPK).rearrange("p (h s k) -> p h s k", h=PH, s=2)
        topi = A.take(NQ * TOPK)
        topf = A.take(NQ * TOPK).rearrange("p (h s k) -> p h s k", h=PH, s=2)
        fi = A.take(P)
        fa = A.take(2 * P).rearrange("p (s n) -> p s n", s=2)
        ff = A.take(2 * P).rearrange("p (s n) -> p s n", s=2)
        chosen = A.take(NT * 3 * P).rearrange("p (s m n) -> p s m n", s=NT, m=3)
        gsum = A.take(PH)
        topi_u = topi.bitcast(U32).rearrange("p (h s k) -> p h s k", h=PH, s=2)
        fi_u = fi.bitcast(U32)
        fa_u = fa.bitcast(U32)

        def mix(name, parts=P):
            a, n = MIX[name]
            return mix_m[0:parts, a:a + n]

        blk = mix("blk")
        mask4 = mix("mask4", CHUNK).rearrange("p (m t) -> p m t", m=4)
        negm1 = mix("negm1", CHUNK)
        mT = mix("mT", CHUNK).rearrange("p (b t) -> p b t", b=len(LEVELS))

        s_h = sem("first_loads")
        s_zero = sem("zeros_set")
        s_mix = sem("mixer_constants_loaded")
        s_keys = sem("keys_loaded")
        s_w = [sem(f"weights_loaded_{i}") for i in range(WR)]
        s_hi = sem("weights_high_ready")
        s_lo = sem("weights_low_ready")
        s_use = sem("weight_tile_used")
        s_sq = sem("squares_ready")
        s_ss = sem("square_sums_ready")
        s_xn = sem("normed_ready")
        s_cat = sem("mixed_ready")
        s_xh = sem("x_high_ready")
        s_xl = sem("x_low_ready")
        s_ea = sem("evacuated_by_act")
        s_ed = sem("evacuated_by_dve")
        s_th = sem("tanh_ready")
        s_sg = sem("sigmoid_hg_ready")
        s_zs = sem("shifted_ready")
        s_lora = sem("lora_done")
        s_ag = sem("a_w_g_ready")
        s_pe = sem("vector_request")
        s_pd = sem("pe_step_done")
        s_ar = sem("act_request")
        s_ad = sem("act_step_done")
        s_var = sem("variance_ready")
        s_rs = sem("sqrt_ready")
        s_qr = sem("scores_in_psum")
        s_sc = sem("scores_copied")
        s_oh = sem("onehots_ready")
        s_gp = sem("gates_in_psum")
        s_gm = sem("gates_applied")
        s_gelu = sem("gelu_done")
        s_ah = sem("act_high_ready")
        s_act = sem("act_low_ready")
        s_cg = sem("conv_gate_ready")
        s_conv = sem("conv_done")
        s_gl = sem("pool_link")
        s_hd = sem("layer_done")
        s_out = sem("output_stored")
        s_dl = sem("dve_link")
        s_al = sem("act_link")

        block = ctx.enter_context(nc.Block())

        @block.sync
        def _(sp):
            sp.dma_start(h_t[:, :], h0).then_inc(s_h, 16)
            sp.dma_start(res_t[:, :], res_c).then_inc(s_h, 16)
            sp.dma_start(vec_t[:, :], vec).then_inc(s_h, 16)

            def load(l, n, src, it=0):
                slot = (l * NW + n) % WR
                if l or n >= WR:
                    sp.wait_ge(s_use, l * NW + n - WR + 1 + WR * it)
                sp.dma_start(wraw_t[:, slot * D:(slot + 1) * D], src).then_inc(s_w[slot], 16)

            for l in range(DEPTH):
                for n in range(WR):
                    load(l, n, w_c[l, n])
                if l:
                    sp.wait_ge(s_hd, l)
                sp.dma_start(mix_m, mix_c).then_inc(s_mix, 16)
                sp.dma_start(lora.rearrange("p s n -> p (s n)"), lora_c[l]).then_inc(s_mix, 16)
                with sp.Fori(0, (NPROJ - WR) // WR) as it:
                    for j in range(WR):
                        load(l, WR + j, w_c[l, WR * it + WR + j], it)
                for n in range(NPROJ - (NPROJ - WR) % WR, NPROJ):
                    load(l, n, w_c[l, n])
                sp.wait_ge(s_xn, (2 * l + 2) * DC)
                sp.dma_start(keys.rearrange("p m n -> p (m n)"), keys_c[l]).then_inc(s_keys, 16)
                for first, src in ((NU0, u_c), (NV0, v_c)):
                    with sp.Fori(0, NKEYS // WR) as it:
                        for j in range(WR):
                            load(l, first + j, src[l, WR * it + j], it)
            sp.wait_ge(s_hd, DEPTH)
            sp.dma_start(out, h[:, :, NMETA:T]).then_inc(s_out, 16)
            sp.wait_ge(s_out, 16)

        @block.gpsimd
        def _(pool):
            nc.gpsimd.memset(zero_t[:, :], 0.0).then_inc(s_zero, 1)
            g = nc.gpsimd
            link = Link(pool, s_gl)

            def low(l, n, it=0):
                at = (l * NW + n) % WR * D
                slot = slice(at, at + D)
                pool.wait_ge(s_hi, l * NW + n + 1 + WR * it)
                g.tensor_tensor(wlo_t[:, slot], wraw_t[:, slot], whi_t[:, slot].bitcast(F32),
                                ALU.subtract).then_inc(s_lo, 1)

            def lows(l, n0, n1):
                whole = (n1 - n0) // WR
                with pool.Fori(0, whole) as it:
                    for j in range(WR):
                        low(l, n0 + j, it)
                for n in range(n0 + whole * WR, n1):
                    low(l, n)

            for l in range(DEPTH):
                lows(l, 0 if l == 0 else AHEAD, NZ + AHEAD)
                pool.wait_ge(s_cg, 2 * (l + 1))
                link(g.memset(cu[:, :, 0:CPAD], 0.0))
                link(g.tensor_tensor(cu[:, :, CPAD:CPAD + T], z[:, ZCU:ZCU + 2, 1:T + 1], cacc[:, :, :], ALU.mult))
                for k in range(CONV_K):
                    for j in range(2):
                        dst = cacc if k == 0 else ctmp
                        ins = g.tensor_scalar(dst[:, j, :], cu[:, j, k:k + T], vcol(l, "conv_w", j * CONV_K + k),
                                              vcol(l, "conv_b", j) if k == 0 else None, ALU.mult,
                                              *((ALU.add,) if k == 0 else ()))
                        if j == 0:
                            ins.then_inc(s_gl, 1)
                            link.n += 1
                        else:
                            link(ins)
                    if k:
                        ins = g.tensor_tensor(cacc[:, :, :], cacc[:, :, :], ctmp[:, :, :], ALU.add)
                        link(ins) if k < CONV_K - 1 else ins.then_inc(s_conv, 1)
                lows(l, NZ + AHEAD, NW)
                if l < DEPTH - 1:
                    for n in range(AHEAD):
                        low(l + 1, n)

        @block.scalar
        def _(act):
            link = Link(act, s_al)
            req = [0]
            done = [0]

            def asked():
                req[0] += 1
                act.wait_ge(s_ar, req[0])

            nvar = [0]

            def root(a):
                nvar[0] += 1
                act.wait_ge(s_var, nvar[0])
                nc.scalar.activation(a, a, ACT.Sqrt).then_inc(s_rs, 1)

            def high(l, n, it=0):
                if n >= NW:
                    l, n = l + 1, n - NW
                if l == DEPTH:
                    return
                slot = (l * NW + n) % WR
                act.wait_ge(s_w[slot], 16 * it + 16 * ((l * NW + n) // WR + 1))
                if l or n >= WR:
                    act.wait_ge(s_use, l * NW + n - WR + 1 + WR * it)
                nc.scalar.copy(whi_t[:, slot * D:(slot + 1) * D],
                               wraw_t[:, slot * D:(slot + 1) * D]).then_inc(s_hi, 1)

            def x_high(l, k, src, t0=0):
                for c in range(DC):
                    if k == 1:
                        act.wait_ge(s_cat, l + 1)
                    else:
                        act.wait_ge(s_xn, (2 * l + k // 2) * DC + c + 1)
                    nc.scalar.copy(xh[:, c, t0:T], src[:, c, t0:T]).then_inc(s_xh, 1)

            def squares(l, k):
                if 2 * l + k:
                    act.wait_ge(s_hd, l) if k == 0 else act.wait_ge(s_ed, (l + 1) * NOUT)
                else:
                    act.wait_ge(s_h, 48)
                nc.scalar.activation(sq[:, :, :], h[:, :, :], ACT.Square).then_inc(s_sq, 1)

            def evacuate(l, n, dst, nt):
                high(l, n + AHEAD)
                act.wait_ge(s_use, l * NW + n + 1)
                nc.scalar.copy(dst, ps[:, 1 + n % 2, 0:nt]).then_inc(s_ea, 1)

            for l in range(DEPTH):
                L = LAYERS[l]
                squares(l, 0)
                if l == 0:
                    for n in range(AHEAD):
                        high(0, n)
                root(var)
                x_high(l, 0, xn)
                for n in range(12):
                    evacuate(l, n, z[:, n, 1:T + 1], T)
                act.wait_ge(s_zs, 2 * l + 2)
                nc.scalar.activation(th[0:HD, :], zs[0:HD, 6, :], ACT.Tanh).then_inc(s_th, 1)
                nc.scalar.activation(sg[:, :], zs[:, 7, :], ACT.Sigmoid).then_inc(s_sg, 1)
                act.wait_ge(s_lora, 6 * l + 6)
                for j in range(2):
                    nc.scalar.activation(ea[:, j, :], ps[:, 3 + j, 0:T], ACT.Sigmoid,
                                         bias=vcol(l, "w0", j)).then_inc(s_ag, 1)
                for j in range(2):
                    nc.scalar.activation(aa[:, j, :], ps[:, 5 + j, 0:T], ACT.Sigmoid,
                                         bias=vcol(l, "a0", j)).then_inc(s_ag, 1)
                for j in range(2):
                    nc.scalar.copy(gg[:, j, :], ps[:, 7 if j == 0 else 0, 0:T]).then_inc(s_ag, 1)
                for j in range(2):
                    nc.scalar.activation(cacc[:, j, :], z[:, ZCG + j, 1:T + 1], ACT.Sigmoid).then_inc(s_cg, 1)
                for n in range(12, NZ):
                    evacuate(l, n, z[:, n, 1:T + 1], T)
                root(t2[:, :, :])
                asked()
                nc.scalar.activation(dall[:, :, :], cum[:, :, :], ACT.Exp).then_inc(s_ad, 1)
                nc.scalar.activation(dinv[:, :, :], cum[:, :, :], ACT.Exp, scale=-1.0).then_inc(s_ad, 1)
                nc.scalar.activation(dexc[:, :, :], lw[:, :, :], ACT.Exp).then_inc(s_ad, 1)
                for b in range(len(LEVELS) - 1):
                    act.wait_ge(s_pd, PE0[l] + INV + 3 * b + 1)
                    for g in range(3):
                        n0, n1 = 8 * g, min(8 * g + 8, NMAT)
                        ins = nc.scalar.copy(xm[:, n0:n1, :].rearrange("p n t -> p (n t)"),
                                             ps[0:CHUNK, 3 + g, 0:(n1 - n0) * CHUNK])
                    ins.then_inc(s_ad, 1)
                root(t2[:, :, :])
                root(t3[:, 0, 0:T])
                asked()
                nc.scalar.activation(t2[:, :, :], t1[:, :, :], ACT.Sigmoid).then_inc(s_ad, 1)
                root(qn[:, :, :])
                for s, (q0, nq) in enumerate(TILES):
                    nk = KEYS_OF[s]
                    if (q0, nq) not in L.tiles:
                        continue
                    asked()
                    pr = prob[0:nq, 0:AH * nk].rearrange("p (h k) -> p h k", h=AH)
                    for hh in range(AH):
                        nc.scalar.activation(pr[:, hh, :], pr[:, hh, :], ACT.Exp, bias=small[0:nq, 1, hh:hh + 1],
                                             scale=HD ** -0.5, accum_out=small[0:nq, 2, hh:hh + 1])
                    nc.scalar.activation(small[0:nq, 3, :], small[0:nq, 3, :], ACT.Exp).then_inc(s_ad, 1)
                x_high(l, 1, cat, L.t0)
                for m in range(NOUT):
                    high(l, NZ + m + AHEAD)
                squares(l, 1)
                root(var)
                x_high(l, 2, xn, L.t0)
                for m in range(NQ):
                    if m == 0:
                        act.wait_ge(s_xn, (2 * l + 2) * DC)
                    evacuate(l, NZ + NOUT + m, pq[:, m, L.t0:T], L.nt)
                for s, (t0, nt) in enumerate(L.tiles):
                    for g in range(4):
                        k = 4 * s + g
                        act.wait_ge(s_qr, SC0[l] + k + 1)
                        nc.scalar.copy(sc[0:nt, s, 4 * g:4 * g + 4, :].rearrange("p m n -> p (m n)"),
                                       ps[0:nt, 3 + k % 2, :]).then_inc(s_sc, 1)

                def gelus(i0, i1):
                    with act.Fori(0, (i1 - i0) // WR) as it:
                        for j in range(WR):
                            high(l, NU0 + i0 + j + AHEAD, it)
                            act.wait_ge(s_use, l * NW + NU0 + i0 + j + 1 + WR * it)
                            nc.scalar.activation(hid[l][:, bass.ds(WR * it + (i0 + j), 1), :].squeeze(1),
                                                 ps[:, 1 + j % 2, 0:L.nt], ACT.Gelu_apprx_tanh).then_inc(s_gelu, 1)

                gelus(0, L.quiet)
                asked()
                for s, (t0, nt) in enumerate(L.tiles):
                    ins = nc.scalar.activation(chosen[0:nt, s, 0, :], chosen[0:nt, s, 0, :], ACT.Exp)
                ins.then_inc(s_ad, 1)
                gelus(L.quiet, NKEYS)

                def act_highs(i0, i1):
                    with act.Fori(0, (i1 - i0) // WR) as it:
                        for j in range(WR):
                            act.wait_ge(s_use, l * NW + NV0 + i0 + j - 1 + WR * it)
                            nc.scalar.copy(act_hi[:, j % 2, 0:L.nt],
                                           hid[l][:, bass.ds(WR * it + (i0 + j), 1), :].squeeze(1)).then_inc(s_ah, 1)
                            high(l, NV0 + i0 + j + AHEAD, it)

                act.wait_ge(s_gm, G0[l] + L.steps)
                act_highs(0, L.split)
                act.wait_ge(s_gm, G0[l + 1])
                act_highs(L.split, NKEYS - WR)
                for i in range(NKEYS - WR, NKEYS):
                    act.wait_ge(s_use, l * NW + NV0 + i - 1)
                    nc.scalar.copy(act_hi[:, i % 2, 0:L.nt], hid[l][:, i, :]).then_inc(s_ah, 1)
                    high(l, NV0 + i + AHEAD)

        @block.tensor
        def _(pe):
            def mm(out_, lhsT, rhs, start, stop):
                return nc.tensor.matmul(out_, lhsT, rhs, start=start, stop=stop, skip_group_check=True)

            req = [0]

            def asked():
                req[0] += 1
                pe.wait_ge(s_pe, req[0])

            def square_sums(l, k):
                pe.wait_ge(s_sq, 2 * l + k + 1)
                for c in range(DC):
                    last = mm(ps[:, 0, 0:T], ones, sq[:, c, :], c == 0, c == DC - 1)
                last.then_inc(s_ss, 1)

            def tile(l, n, out_of, hi_of, lo_of, it=0, between=None):
                slot = (l * NW + n) % WR
                pe.wait_ge(s_lo, l * NW + n + 1 + WR * it)
                for c in range(DC):
                    if between and c == DC // 2:
                        between()
                    for o, w in out_of(c):
                        for k, (a, b) in enumerate(((whi, hi_of), (whi, lo_of), (wlo, hi_of))):
                            last = mm(o, a[:, slot, c, :], b(c, w), *flags(out_of, c, k))
                last.then_inc(s_use, 1)

            def flags(out_of, c, k):
                return (False, True) if out_of.keeps else (c == 0 and k == 0, c == DC - 1 and k == 2)

            def summed(bank, t0=0):
                def f(c):
                    return [(ps[:, bank, 0:T - t0], slice(t0, T))]
                f.keeps = False
                return f

            def project(l, n, t0=0, it=0):
                tile(l, n, summed(1 + n % 2, t0), lambda c, w: xh[:, c, w], lambda c, w: xl[:, c, w], it)

            def x_split(l, k):
                pe.wait_ge(s_xl, (3 * l + k + 1) * DC)

            for l in range(DEPTH):
                if l == 0:
                    pe.wait_ge(s_h, 48)
                    pe.wait_ge(s_zero, 1)
                pe.wait_ge(s_mix, 32 * (l + 1))
                square_sums(l, 0)
                x_split(l, 0)
                L = LAYERS[l]

                def proj_in(n):
                    if n >= 2:
                        pe.wait_ge(s_ea, l * (NZ + NQ) + n - 1)
                    project(l, n)

                for n in range(NZ):
                    if n == 12:
                        pe.wait_ge(s_th, l + 1)
                        pe.wait_ge(s_sg, l + 1)
                        for j in range(2):
                            mm(ps[:, 3 + j, 0:T], lora[0:HD, 0, j * P:(j + 1) * P], th[0:HD, :],
                               True, True).then_inc(s_lora, 1)
                        for j in range(2):
                            mm(ps[:, 5 + j, 0:T], lora[HD:P, 0, j * P:(j + 1) * P], zs[HD:P, 6, :],
                               True, True).then_inc(s_lora, 1)
                        for j in range(2):
                            mm(ps[:, 7 if j == 0 else 0, 0:T], lora[:, 1, j * P:(j + 1) * P], sg[:, :],
                               True, True).then_inc(s_lora, 1)
                    proj_in(n)

                pe.wait_ge(s_ag, 6 * l + 6)
                asked()
                for j in range(2):
                    last = mm(ps[:, 3 + j, 0:T], blk, t2[:, j, :], True, True)
                last.then_inc(s_pd, 1)
                asked()
                for j in range(2):
                    last = mm(ps[:, 5 + j, 0:T], blk, t1[:, j, :], True, True)
                last.then_inc(s_pd, 1)
                asked()
                for c in range(NCH):
                    for m, src in enumerate((None, ka, be)):
                        k = 3 * c + m
                        if k >= 2:
                            asked()
                        for j in range(2):
                            a = t3[:, j, c * CHUNK:(c + 1) * CHUNK] if src is None else \
                                src[:, j, c * CHUNK:(c + 1) * CHUNK]
                            last = nc.tensor.transpose(ps[0:CHUNK, 3 + k % 2, j * P:(j + 1) * P], a, ident)
                        last.then_inc(s_pd, 1)
                for c in range(NCH):
                    asked()
                    w = slice(c * CHUNK, (c + 1) * CHUNK)
                    for q in range(2):
                        r = slice(q * HD, (q + 1) * HD)
                        for j in range(2):
                            for m, (a, b) in enumerate(((ka, al), (ka, rh), (be, al), (be, rh))):
                                mm(ps[0:CHUNK, 3 + q, (j * 4 + m) * CHUNK:(j * 4 + m + 1) * CHUNK],
                                   a[r, j, w], b[r, j, w], True, True)
                            last = mm(ps[0:CHUNK, 5 + q, j * CHUNK:(j + 1) * CHUNK], al[r, j, w], be[r, j, w],
                                      True, True)
                    last.then_inc(s_pd, 1)
                for b in range(len(LEVELS) - 1):
                    asked()
                    for n in range(NMAT):
                        last = mm(ps[0:CHUNK, 3 + n // 8, (n % 8) * CHUNK:(n % 8 + 1) * CHUNK],
                                  cm[:, n, :], ti[:, n, :], True, True)
                    last.then_inc(s_pd, 1)
                    pe.wait_ge(s_ad, ACT0[l] + 3 + b + 1)
                    for n in range(NMAT):
                        bank = (6, 7, 0)[n // 8]
                        last = mm(ps[0:CHUNK, bank, (n % 8) * CHUNK:(n % 8 + 1) * CHUNK],
                                  tt_[:, n, :], xm[:, n, :], True, True)
                    last.then_inc(s_pd, 1)
                    for n in range(NMAT):
                        last = mm(ps[0:CHUNK, 3 + n // 8, (n % 8) * CHUNK:(n % 8 + 1) * CHUNK],
                                  xm[:, n, :], tt_[:, n, :], True, True)
                    last.then_inc(s_pd, 1)
                for c in range(NCH):
                    w = slice(c * CHUNK, (c + 1) * CHUNK)
                    asked()
                    for j in range(2):
                        mm(ps[0:CHUNK, 3, j * P:(j + 1) * P], al[:, j, w], state[:, j, :], True, False)
                        for q in range(2):
                            last = mm(ps[0:CHUNK, 3, j * P + q * HD:j * P + (q + 1) * HD], gram[:, c, q, j, 0, :],
                                      vtok[:, c, j, q * HD:(q + 1) * HD], False, True)
                    last.then_inc(s_pd, 1)
                    asked()
                    for j in range(2):
                        for q in range(2):
                            last = mm(ps[0:CHUNK, 4, j * P + q * HD:j * P + (q + 1) * HD],
                                      tt_[:, c * 4 + q * 2 + j, :], xs[:, j, q * HD:(q + 1) * HD], True, True)
                    last.then_inc(s_pd, 1)
                    asked()
                    for j in range(2):
                        mm(ps[:, 5, j * P:(j + 1) * P], ktok[:, c, j, :], vtok[:, c, j, :], True, False)
                        mm(ps[:, 5, j * P:(j + 1) * P], btok[:, c, j, :], us[:, j, :], False, True)
                    for j in range(2):
                        mm(ps[:, 6, j * CHUNK:(j + 1) * CHUNK], state[:, j, :], rh[:, j, w], True, False)
                        for q in range(2):
                            o = ps[q * HD:(q + 1) * HD, 6, j * CHUNK:(j + 1) * CHUNK]
                            mm(o, vtok[:, c, j, q * HD:(q + 1) * HD], gram[:, c, q, j, 1, :], False, False)
                            last = mm(o, us[:, j, q * HD:(q + 1) * HD], gram[:, c, q, j, 3, :], False, True)
                    last.then_inc(s_pd, 1)
                for k in range(2):
                    asked()
                    for j in range(2):
                        last = mm(ps[:, 3 + j, 0:T], blk, yT[:, j, PAD:TP] if k == 0 else t2[:, j, :], True, True)
                    last.then_inc(s_pd, 1)
                pe.wait_ge(s_conv, l + 1)
                for k in range(2):
                    asked()
                    for j in range(2):
                        last = mm(ps[:, 3, 0:T], ones, cacc[:, j, :] if k == 0 else t2[:, j, :], j == 0, j == 1)
                    last.then_inc(s_pd, 1)
                asked()
                for c in range(5):
                    last = mm(ps[:, 3 + c, 0:T], blk, sq[:, c, :], True, True)
                last.then_inc(s_pd, 1)
                asked()
                for s, (src, k0, nk, _) in enumerate(V_TILES):
                    a = z[:, ZV, 1 + k0:1 + k0 + nk] if src == "z" else vcat[:, k0:k0 + nk]
                    last = nc.tensor.transpose(ps[0:nk, 3 + s % 2, (s // 2) * P:(s // 2 + 1) * P], a, ident)
                last.then_inc(s_pd, 1)
                for s, (q0, nq) in enumerate(TILES):
                    nk = KEYS_OF[s]
                    if (q0, nq) not in L.tiles:
                        continue
                    kt = kcat if s == 2 else qn[:, 4, :]
                    for hh in range(AH):
                        if hh != 1:
                            asked()
                        r = slice((hh // 4) * HD, (hh // 4 + 1) * HD)
                        mm(ps[0:nq, 3 + hh % 2, 0:nk], qn[r, hh % 4, q0:q0 + nq], kt[r, 0:nk],
                           True, True).then_inc(s_pd, 1)
                    for hh in range(AH):
                        asked()
                        for b, (k0, kn) in enumerate(splits(nk)):
                            last = nc.tensor.transpose(ps[0:kn, 5 + hh % 2, b * P:b * P + nq],
                                                       prob[0:nq, hh * nk + k0:hh * nk + k0 + kn], ident[0:nq, 0:nq])
                        last.then_inc(s_pd, 1)
                        asked()
                        q, c = hh // 4, hh % 4
                        for b, (k0, kn) in enumerate(splits(nk)):
                            last = mm(ps[q * HD:(q + 1) * HD, 7 - 7 * (hh % 2), 0:nq],
                                      vkey[0:kn, max(s, 1) - 1, b, q * HD:(q + 1) * HD], pT[0:kn, hh % 2, b, 0:nq],
                                      b == 0, k0 + kn == nk)
                        last.then_inc(s_pd, 1)
                x_split(l, 1)
                for m in range(NOUT):
                    n = NZ + m
                    if m >= 2:
                        pe.wait_ge(s_ed, l * NOUT + m - 1)
                    else:
                        pe.wait_ge(s_ea, l * (NZ + NQ) + NZ)
                    project(l, n, L.t0)
                square_sums(l, 1)
                x_split(l, 2)
                for m in range(NQ):
                    n = NZ + NOUT + m
                    if m >= 2:
                        pe.wait_ge(s_ea, l * (NZ + NQ) + NZ + m - 1)
                    project(l, n, L.t0)
                pe.wait_ge(s_keys, 16 * (l + 1))
                pe.wait_ge(s_ea, (l + 1) * (NZ + NQ))
                for s, (t0, nt) in enumerate(L.tiles):
                    for g in range(4):
                        k = 4 * s + g
                        if k >= 2:
                            pe.wait_ge(s_sc, SC0[l] + k - 1)
                        for m in range(4):
                            last = mm(ps[0:nt, 3 + k % 2, m * P:(m + 1) * P], pq[:, 4 * g + m, t0:t0 + nt],
                                      keys[:, 4 * g + m, :], True, True)
                        last.then_inc(s_qr, 1)

                def hidden(i, it):
                    if not (isinstance(it, int) and i < 2):
                        pe.wait_ge(s_gelu, l * NKEYS + i - 1 + WR * it)
                    project(l, NU0 + i, L.t0, it)

                def spread(k, it, banks, n, first, every=WR):
                    pe.wait_ge(s_oh, G0[l] + k + 1 + every * it)
                    if not first:
                        pe.wait_ge(s_gm, G0[l] + k - (banks[0] != banks[1]) + every * it)
                    for t in range(OHT):
                        last = mm(ps[:, banks[k % 2], t * n:(t + 1) * n], ohB[:, k % 2, t, :],
                                  ohA[:, k % 2, t, 0:n], True, True)
                    last.then_inc(s_gp, 1)

                for i in range(WR):
                    hidden(i, 0)
                with pe.Fori(0, L.split // WR - 1) as it:
                    for j in range(WR):
                        hidden(WR + j, it)
                asked()
                for s, (t0, nt) in enumerate(L.tiles):
                    for m in range(3):
                        last = nc.tensor.transpose(ps[:, 5 + s, m * P:m * P + nt], chosen[0:nt, s, m, :],
                                                   ident[0:nt, 0:nt])
                last.then_inc(s_pd, 1)
                for j in range(WR):
                    hidden(L.split + j, 0)
                    spread(j, 0, (0, 3), L.split, j < 2)
                with pe.Fori(0, L.steps // WR - 1) as it:
                    for j in range(WR):
                        hidden(L.split + WR + j, it)
                        spread(WR + j, it, (0, 3), L.split, False)
                pe.wait_ge(s_gm, G0[l] + L.steps)
                pe.wait_ge(s_gelu, (l + 1) * NKEYS)
                for bank in sorted({q[0] for c in range(DC) for q in L.out_at[c]}):
                    mm(ps[:, bank, :], zero_t[:, :], h_t[:, 0:512], True, True)

                def pieces(c):
                    return [(ps[:, bank, at:at + n], slice(t0, t0 + n)) for bank, at, t0, n in L.out_at[c]]

                pieces.keeps = True

                def output(i, it, between=None):
                    pe.wait_ge(s_act, l * NKEYS + i + 1 + WR * it)
                    tile(l, NV0 + i, pieces, lambda c, w: act_hi[:, i % 2, w], lambda c, w: act_lo[:, i % 2, w], it,
                         between)

                double = L.steps - L.split
                n2 = NKEYS - L.split
                if double:
                    with pe.Fori(0, double // WR) as it:
                        for j in range(WR):
                            k = L.steps + 2 * j
                            output(j, it, lambda: spread(k, it, L.gate_banks, n2, False, 2 * WR))
                            spread(k + 1, it, L.gate_banks, n2, False, 2 * WR)
                with pe.Fori(0, (L.split - double) // WR) as it:
                    for j in range(WR):
                        output(double + j, it)
                        spread(L.steps + 2 * double + j, it, L.gate_banks, n2, False)
                pe.wait_ge(s_gm, G0[l + 1])
                with pe.Fori(0, (NKEYS - L.split) // WR) as it:
                    for j in range(WR):
                        output(L.split + j, it)

        @block.vector
        def _(dve):
            v = nc.vector
            link = Link(dve, s_dl)
            npd, nad, npe = [0], [0], [0]

            def ask_pe(ins):
                ins.then_inc(s_pe, 1)
                npe[0] += 1

            def ask_pe_and_wait(ins):
                ask_pe(ins)
                dve.wait_ge(s_pe, npe[0])

            def pe_done():
                npd[0] += 1
                dve.wait_ge(s_pd, npd[0])

            def act_done(n=1):
                nad[0] += n
                dve.wait_ge(s_ad, nad[0])

            nrs = [0]

            def rsqrt(ins, a):
                ins.then_inc(s_var, 1)
                nrs[0] += 1
                dve.wait_ge(s_rs, nrs[0])
                link(v.reciprocal(a, a))

            def x_low(l, k, src, dst, t0, c):
                dve.wait_ge(s_xh, (3 * l + k) * DC + c + 1)
                v.tensor_tensor(dst[:, c, t0:T], src[:, c, t0:T], xh[:, c, t0:T].bitcast(F32),
                                ALU.subtract).then_inc(s_xl, 1)

            def norm(l, k, t0=0):
                dve.wait_ge(s_ss, 2 * l + k + 1)
                rsqrt(v.tensor_scalar(var, ps[:, 0, 0:T], 1.0 / D, NORM_EPS, ALU.mult, ALU.add),
                      var)
                for c in range(DC):
                    v.scalar_tensor_tensor(xn[:, c, t0:T], h[:, c, t0:T], vcol(l, "norm2" if k else "norm1", c),
                                           var[:, t0:T], ALU.mult, ALU.mult).then_inc(s_xn, 1)
                    if c:
                        x_low(l, 2 * k, xn, xl, t0, c - 1)
                x_low(l, 2 * k, xn, xl, t0, DC - 1)

            for l in range(DEPTH):
                if l == 0:
                    dve.wait_ge(s_h, 48)
                L = LAYERS[l]
                norm(l, 0)
                dve.wait_ge(s_mix, 32 * (l + 1))
                link(v.memset(z[:, :, 0:1], 0.0))
                dve.wait_ge(s_ea, l * (NZ + NQ) + 8)
                for c in (6, 7, 0, 1, 2, 3, 4, 5):
                    link(v.tensor_tensor(t1[:, 0, :], z[:, c, 0:T], z[:, c, 1:T + 1], ALU.subtract))
                    ins = v.scalar_tensor_tensor(zs[:, c, :], t1[:, 0, :], vcol(l, "mu", c), z[:, c, 1:T + 1],
                                                 ALU.mult, ALU.add)
                    if c in (6, 7):
                        ins.then_inc(s_zs, 1)
                        dve.wait_ge(s_zs, 2 * l + c - 5)
                    else:
                        link(ins)
                r_, k_, v_ = zs[:, 0:2, :], zs[:, 2:4, :], zs[:, 4:6, :]
                for j in range(2):
                    link(v.tensor_scalar(kk[:, j, :], k_[:, j, :], vcol(l, "k_k", j), None, ALU.mult))
                ask_pe(v.tensor_tensor(t2[:, :, :], kk[:, :, :], kk[:, :, :], ALU.mult))
                link(v.memset(lw[:, :, 0:PAD], 0.0))
                dve.wait_ge(s_ag, 6 * (l + 1))
                link(v.tensor_scalar(lw[:, :, PAD:TP], ea[:, :, :], -float(np.exp(-0.5)), None, ALU.mult))
                for j in range(2):
                    for c in range(NCH):
                        w = slice(c * CHUNK, (c + 1) * CHUNK)
                        link(v.tensor_tensor_scan(cum[:, j, w], ones[:, 0:CHUNK], lw[:, j, w], 0.0,
                                                  ALU.mult, ALU.add))
                v.tensor_tensor(lw[:, :, :], cum[:, :, :], lw[:, :, :], ALU.subtract).then_inc(s_ar, 1)
                for a in (al, be, ka, rh):
                    link(v.memset(a[:, :, 0:PAD], 0.0))
                for j in range(2):
                    link(v.tensor_scalar(t1[:, j, :], aa[:, j, :], -1.0, vcol(l, "k_a", j), ALU.add, ALU.mult))
                link(v.scalar_tensor_tensor(km[:, :, :], t1[:, :, :], 1.0, k_, ALU.add, ALU.mult))
                for j in range(2):
                    link(v.scalar_tensor_tensor(t1[:, j, :], r_[:, j, :], vcol(l, "r_k", j), km[:, j, :],
                                                ALU.mult, ALU.mult))
                link(v.memset(t3[:, :, 0:PAD], 0.0))
                ask_pe(v.tensor_copy(t3[:, :, PAD:TP], v_))
                pe_done()
                for j in range(2):
                    ins = v.tensor_scalar(t2[:, j, :], ps[:, 3 + j, 0:T], 1e-12, None, ALU.max)
                    link(ins) if j == 0 else rsqrt(ins, t2[:, :, :])
                link(v.tensor_tensor(kk[:, :, :], kk[:, :, :], t2[:, :, :], ALU.mult))
                link(v.tensor_tensor(bb[:, :, :], kk[:, :, :], aa[:, :, :], ALU.mult))
                pe_done()
                for j in range(2):
                    link(v.tensor_tensor(bonus[:, j, :], ps[:, 5 + j, 0:T], v_[:, j, :], ALU.mult))
                act_done(3)
                w = slice(PAD, TP)
                link(v.tensor_tensor(al[:, :, w], dexc[:, :, w], kk[:, :, :], ALU.mult))
                link(v.tensor_tensor(be[:, :, w], dinv[:, :, w], bb[:, :, :], ALU.mult))
                link(v.tensor_tensor(ka[:, :, w], dinv[:, :, w], km[:, :, :], ALU.mult))
                link(v.memset(state[:, :, :], 0.0))
                ask_pe(v.tensor_tensor(rh[:, :, w], dall[:, :, w], r_, ALU.mult))
                for c in range(NCH):
                    for m, dst in enumerate((vtok, ktok, btok)):
                        k = 3 * c + m
                        pe_done()
                        ins = v.tensor_copy(dst[:, c, :, :].rearrange("p j n -> p (j n)"),
                                            ps[0:CHUNK, 3 + k % 2, 0:2 * P])
                        if k == 3 * NCH - 2:
                            link(ins)
                        else:
                            ask_pe_and_wait(ins)
                for c in range(NCH):
                    pe_done()
                    for q in range(2):
                        link(v.tensor_tensor(gram[:, c, q, :, :, :].rearrange("p j m t -> p j (m t)"),
                                             ps[0:CHUNK, 3 + q, :].rearrange("p (j m) -> p j m", j=2),
                                             bc(mask4.rearrange("p m t -> p (m t)"), 1, 2), ALU.mult))
                        n0 = c * 4 + q * 2
                        link(v.tensor_tensor(ti[:, n0:n0 + 2, :],
                                             ps[0:CHUNK, 5 + q, 0:2 * CHUNK].rearrange("p (j t) -> p j t", j=2),
                                             bc(negm1, 1, 2), ALU.mult))
                        ins = v.tensor_tensor(ti[:, n0:n0 + 2, :], ti[:, n0:n0 + 2, :],
                                              bc(ident[0:CHUNK, 0:CHUNK], 1, 2), ALU.add)
                        if q == 1 and c < NCH - 1:
                            ask_pe_and_wait(ins)
                        else:
                            link(ins)
                gl = gram.rearrange("p c q j m t -> p (c q j) m t")[:, :, 2, :]
                link(v.tensor_tensor(cm[:, :, :], gl, bc(mT[:, 0, :], 1, NMAT), ALU.mult))
                link(v.scalar_tensor_tensor(tt_[:, :, :], cm[:, :, :], -1.0,
                                            bc(ident[0:CHUNK, 0:CHUNK], 1, NMAT), ALU.mult, ALU.add))
                for b in range(1, len(LEVELS)):
                    ask_pe(v.tensor_tensor(cm[:, :, :], gl, bc(mT[:, b, :], 1, NMAT), ALU.mult))
                    pe_done()
                    pe_done()
                    pe_done()
                    for g in range(3):
                        n0, n1 = 8 * g, min(8 * g + 8, NMAT)
                        bank = (6, 7, 0)[g]
                        link(v.tensor_tensor(ti[:, n0:n1, :].rearrange("p n t -> p (n t)"),
                                             ti[:, n0:n1, :].rearrange("p n t -> p (n t)"),
                                             ps[0:CHUNK, bank, 0:(n1 - n0) * CHUNK], ALU.subtract))
                        ins = v.tensor_tensor(tt_[:, n0:n1, :].rearrange("p n t -> p (n t)"),
                                              tt_[:, n0:n1, :].rearrange("p n t -> p (n t)"),
                                              ps[0:CHUNK, 3 + g, 0:(n1 - n0) * CHUNK], ALU.subtract)
                        (ask_pe if (b, g) == (len(LEVELS) - 1, 2) else link)(ins)
                nad[0] += len(LEVELS) - 1
                for c in range(NCH):
                    w = slice(c * CHUNK, (c + 1) * CHUNK)
                    pe_done()
                    ask_pe(v.tensor_copy(xs[:, :, :].rearrange("p j n -> p (j n)"), ps[0:CHUNK, 3, 0:2 * P]))
                    pe_done()
                    ask_pe(v.tensor_scalar(us[:, :, :].rearrange("p j n -> p (j n)"), ps[0:CHUNK, 4, 0:2 * P], -1.0,
                                           None, ALU.mult))
                    pe_done()
                    link(v.tensor_tensor(stmp[:, :, :].rearrange("p j n -> p (j n)"), ps[:, 5, 0:2 * P],
                                         state[:, :, :].rearrange("p j n -> p (j n)"), ALU.add))
                    link(v.tensor_copy(yT[:, :, w], ps[:, 6, 0:2 * CHUNK].rearrange("p (j t) -> p j t", j=2)))
                    e = (c + 1) * CHUNK
                    link(v.scalar_tensor_tensor(state[:, 0, :], stmp[:, 0, :], dall[:, 0, e - 1:e], blk,
                                                ALU.mult, ALU.mult))
                    ask_pe_and_wait(v.scalar_tensor_tensor(state[:, 1, :], stmp[:, 1, :], dall[:, 1, e - 1:e], blk,
                                                           ALU.mult, ALU.mult))
                pe_done()
                for j in range(2):
                    link(v.scalar_tensor_tensor(t1[:, j, :], ps[:, 3 + j, 0:T], -1.0 / HD, yT[:, j, PAD:TP],
                                                ALU.mult, ALU.add))
                ask_pe(v.tensor_tensor(t2[:, :, :], t1[:, :, :], t1[:, :, :], ALU.mult))
                pe_done()
                for j in range(2):
                    ins = v.tensor_scalar(t2[:, j, :], ps[:, 3 + j, 0:T], 1.0 / HD, GN_EPS, ALU.mult, ALU.add)
                    link(ins) if j == 0 else rsqrt(ins, t2[:, :, :])
                link(v.tensor_tensor(t1[:, :, :], t1[:, :, :], t2[:, :, :], ALU.mult))
                for j in range(2):
                    link(v.tensor_scalar(t1[:, j, :], t1[:, j, :], vcol(l, "gn_g", j), vcol(l, "gn_b", j),
                                         ALU.mult, ALU.add))
                link(v.tensor_tensor(t1[:, :, :], t1[:, :, :], bonus[:, :, :], ALU.add))
                ask_pe_and_wait(v.tensor_tensor(cat[:, 4:6, :], t1[:, :, :], gg[:, :, :], ALU.mult))
                pe_done()
                for j in range(2):
                    link(v.scalar_tensor_tensor(cacc[:, j, :], ps[:, 3, 0:T], -1.0 / (2 * P), cacc[:, j, :],
                                                ALU.mult, ALU.add))
                ask_pe(v.tensor_tensor(t2[:, :, :], cacc[:, :, :], cacc[:, :, :], ALU.mult))
                pe_done()
                rsqrt(v.tensor_scalar(t3[:, 0, 0:T], ps[:, 3, 0:T], 1.0 / (2 * P), NORM_EPS, ALU.mult, ALU.add),
                      t3[:, 0, 0:T])
                link(v.tensor_tensor(t1[:, :, :], cacc[:, :, :], bc(t3[:, 0, 0:T], 1, 2), ALU.mult))
                for j in range(2):
                    ins = v.tensor_scalar(t1[:, j, :], t1[:, j, :], vcol(l, "ln_g", j), vcol(l, "ln_b", j),
                                          ALU.mult, ALU.add)
                    link(ins) if j == 0 else ins.then_inc(s_ar, 1)
                dve.wait_ge(s_ea, l * (NZ + NQ) + NZ)
                ask_pe(v.tensor_tensor(sq[:, 0:5, :], z[:, ZQ:ZQ + 5, 1:T + 1], z[:, ZQ:ZQ + 5, 1:T + 1], ALU.mult))
                pe_done()
                for c in range(5):
                    ins = v.tensor_scalar(qn[:, c, :], ps[:, 3 + c, 0:T], 1.0 / HD, NORM_EPS, ALU.mult, ALU.add)
                    link(ins) if c < 4 else rsqrt(ins, qn[:, :, :])
                for c in range(5):
                    link(v.scalar_tensor_tensor(qn[:, c, :], z[:, ZQ + c, 1:T + 1], vcol(l, "kg" if c == 4 else "qg"),
                                                qn[:, c, :], ALU.mult, ALU.mult))
                for src, dst in ((qn[:, 4, :], kcat), (z[:, ZV, 1:T + 1], vcat)):
                    link(v.tensor_copy(dst[:, 0:NMETA], src[:, 0:NMETA]))
                    ins = v.tensor_copy(dst[:, NMETA:208], src[:, 80:T])
                    (link if dst is kcat else ask_pe)(ins)
                act_done(1)
                link(v.tensor_tensor(cat[:, 6:8, :], t1[:, :, :], t2[:, :, :], ALU.mult))
                pe_done()
                for s, (src, k0, nk, (sl, b)) in enumerate(V_TILES):
                    ins = v.tensor_copy(vkey[0:nk, sl, b, :], ps[0:nk, 3 + s % 2, (s // 2) * P:(s // 2 + 1) * P])
                    (ask_pe_and_wait if s == len(V_TILES) - 1 else link)(ins)
                for s, (q0, nq) in enumerate(TILES):
                    nk = KEYS_OF[s]
                    if (q0, nq) not in L.tiles:
                        continue
                    dist = mix(("distM", "distA", "distB")[s], nq)
                    pr = prob[0:nq, 0:AH * nk].rearrange("p (h k) -> p h k", h=AH)
                    m_, nm, rs, es, rd = (small[0:nq, i, :] for i in range(5))
                    sink = vecs[0:nq, l, VEC["sink"][0]:VEC["sink"][0] + AH]
                    for hh in range(AH):
                        pe_done()
                        ins = v.scalar_tensor_tensor(pr[:, hh, :], dist, -SLOPES[hh] * HD ** 0.5,
                                                     ps[0:nq, 3 + hh % 2, 0:nk], ALU.mult, ALU.add)
                        if hh < AH - 2:
                            ask_pe_and_wait(ins)
                        else:
                            link(ins)
                    link(v.tensor_reduce(m_, pr, AX.X, ALU.max))
                    link(v.scalar_tensor_tensor(m_, m_, HD ** -0.5, sink, ALU.mult, ALU.max))
                    link(v.tensor_scalar(nm, m_, -1.0, None, ALU.mult))
                    v.tensor_tensor(es, sink, m_, ALU.subtract).then_inc(s_ar, 1)
                    act_done(1)
                    link(v.tensor_tensor(rs, rs, es, ALU.add))
                    link(v.reciprocal(rd, rs))
                    ask_pe(v.tensor_tensor(pr, pr, bc(rd, 2, nk), ALU.mult))
                    for hh in range(AH):
                        pe_done()
                        for b, (k0, kn) in enumerate(splits(nk)):
                            ins = v.tensor_copy(pT[0:kn, hh % 2, b, 0:nq], ps[0:kn, 5 + hh % 2, b * P:b * P + nq])
                            (ask_pe if k0 + kn == nk else link)(ins)
                        pe_done()
                        q, c = hh // 4, hh % 4
                        ins = v.tensor_copy(cat[q * HD:(q + 1) * HD, c, q0:q0 + nq],
                                            ps[q * HD:(q + 1) * HD, 7 - 7 * (hh % 2), 0:nq])
                        if s == NT - 1 and hh == AH - 1:
                            ins.then_inc(s_cat, 1)
                        else:
                            ask_pe_and_wait(ins)
                for c in range(DC):
                    x_low(l, 1, cat, xl, L.t0, c)
                for m in range(NOUT):
                    dve.wait_ge(s_use, l * NW + NZ + m + 1)
                    v.tensor_tensor(h[:, m, L.t0:T], h[:, m, L.t0:T], ps[:, 1 + (NZ + m) % 2, 0:L.nt],
                                    ALU.add).then_inc(s_ed, 1)
                dve.wait_ge(s_ed, (l + 1) * NOUT)
                norm(l, 1, L.t0)
                for s, (t0, nt) in enumerate(L.tiles):
                    dve.wait_ge(s_sc, SC0[l] + 4 * s + 4)
                    hs = [(hh, p) for hh in range(PH) for p in range(2)]
                    score = lambda hh, p: sc[0:nt, s, 2 * hh + p, :]

                    def top16(items, val, idx, src):
                        def each(f):
                            for it_ in items[:-1]:
                                f(*it_).then_inc(s_dl, 1)
                                link.n += 1
                            link(f(*items[-1]))

                        each(lambda *a: v.max(val(*a)[:, 0:8], src(*a)))
                        each(lambda *a: v.max_index(idx(*a)[:, 0:8], val(*a)[:, 0:8], src(*a)))
                        each(lambda *a: v.match_replace(src(*a), val(*a)[:, 0:8], src(*a), NEG))
                        each(lambda *a: v.max(val(*a)[:, 8:16], src(*a)))
                        each(lambda *a: v.max_index(idx(*a)[:, 8:16], val(*a)[:, 8:16], src(*a)))

                    top16(hs, lambda hh, p: topv[0:nt, hh, p, :], lambda hh, p: topi_u[0:nt, hh, p, :], score)
                    link(v.tensor_copy(topf[0:nt].rearrange("p h s k -> p (h s k)"),
                                       topi_u[0:nt].rearrange("p h s k -> p (h s k)")))
                    cb = comb[0:nt].rearrange("p h (a b) -> p h a b", a=TOPK)
                    link(v.tensor_tensor(cb, bc(topv[0:nt, :, 0, :], 3, TOPK), bc(topv[0:nt, :, 1, :], 2, TOPK),
                                         ALU.add))
                    fvh = chosen[0:nt, s, 0, :].rearrange("p (h k) -> p h k", h=PH)
                    fih = fi_u[0:nt].rearrange("p (h k) -> p h k", h=PH)
                    top16([(hh,) for hh in range(PH)], lambda hh: fvh[:, hh, :], lambda hh: fih[:, hh, :],
                          lambda hh: comb[0:nt, hh, :])
                    link(v.tensor_scalar(fa_u[0:nt, 0, :], fi_u[0:nt], 4, None, ALU.logical_shift_right))
                    link(v.tensor_scalar(fa_u[0:nt, 1, :], fi_u[0:nt], 15, None, ALU.bitwise_and))
                    link(v.tensor_copy(ff[0:nt].rearrange("p s n -> p (s n)"),
                                       fa_u[0:nt].rearrange("p s n -> p (s n)")))
                    e4 = eqm[0:nt].rearrange("p (n a) -> p n a", a=TOPK)
                    e5 = eqm[0:nt].rearrange("p (h k a) -> p h k a", h=PH, a=TOPK)
                    for p in range(2):
                        link(v.tensor_tensor(e4, bc(ff[0:nt, p, :], 2, TOPK), bc(iota[0:nt, 0:TOPK], 1, P),
                                             ALU.is_equal))
                        link(v.tensor_tensor(e5, e5, bc(topf[0:nt, :, p, :], 2, TOPK), ALU.mult))
                        link(v.tensor_reduce(chosen[0:nt, s, 1 + p, :], e4, AX.X, ALU.add))
                    link(v.tensor_copy(gsum[0:nt, :], fvh[:, :, 0]))
                    ins = v.tensor_tensor(fvh, fvh, bc(gsum[0:nt, :], 2, TOPK), ALU.subtract)
                    link(ins) if s < len(L.tiles) - 1 else ins.then_inc(s_ar, 1)
                act_done(1)
                for s, (t0, nt) in enumerate(L.tiles):
                    gh = chosen[0:nt, s, 0, :].rearrange("p (h k) -> p h k", h=PH)
                    link(v.tensor_reduce(gsum[0:nt, :], gh, AX.X, ALU.add))
                    link(v.reciprocal(gsum[0:nt, :], gsum[0:nt, :]))
                    ins = v.tensor_tensor(gh, gh, bc(gsum[0:nt, :], 2, TOPK), ALU.mult)
                    (ask_pe if s == len(L.tiles) - 1 else link)(ins)
                pe_done()
                for s, (t0, nt) in enumerate(L.tiles):
                    link(v.tensor_copy(sel[:, :, t0:t0 + nt],
                                       ps[:, 5 + s, 0:3 * P].rearrange("p (m n) -> p m n", m=3)[:, :, 0:nt]))

                def onehots(k, part, it, every, first):
                    i0, n = (0, L.split) if part == 0 else (L.split, NKEYS - L.split)
                    b = k % 2
                    t0 = OHT * every * it + (L.t0 + OHT * (k - part * L.steps))
                    if not first:
                        dve.wait_ge(s_gp, G0[l] + k - 1 + every * it)
                    v.tensor_tensor(ohB[:, b], bc(iota, 1, OHT), bc(sel[:, 2, bass.ds(t0, OHT)], 2, P),
                                    ALU.is_equal).then_inc(s_dl, 1)
                    link.n = link.n + 1
                    a = ohA[:, b, :, 0:n]
                    link(v.tensor_tensor(a, bc(iota[:, i0:i0 + n], 1, OHT), bc(sel[:, 1, bass.ds(t0, OHT)], 2, n),
                                         ALU.is_equal))
                    v.tensor_tensor(a, a, bc(sel[:, 0, bass.ds(t0, OHT)], 2, n), ALU.mult).then_inc(s_oh, 1)

                def apply(k, part, it, every, banks):
                    i0, n = (0, L.split) if part == 0 else (L.split, NKEYS - L.split)
                    t0 = OHT * every * it + OHT * (k - part * L.steps)
                    dve.wait_ge(s_gp, G0[l] + k + 1 + every * it)
                    hv = hid[l][:, i0:i0 + n, bass.ds(t0, OHT)]
                    v.tensor_tensor(hv, hv, ps[:, banks[k % 2], 0:OHT * n].rearrange("p (t i) -> p i t", t=OHT),
                                    ALU.mult).then_inc(s_gm, 1)

                def act_low(i, it):
                    dve.wait_ge(s_ah, l * NKEYS + i + 1 + WR * it)
                    v.tensor_tensor(act_lo[:, i % 2, 0:L.nt], hid[l][:, bass.ds(WR * it + i, 1), :].squeeze(1),
                                    act_hi[:, i % 2, 0:L.nt].bitcast(F32), ALU.subtract).then_inc(s_act, 1)

                dve.wait_ge(s_gelu, l * NKEYS + L.split)
                steps, per_step = L.steps, 2
                onehots(0, 0, 0, WR, True)
                for k in range(1, WR + 1):
                    onehots(k, 0, 0, WR, k < 2)
                    apply(k - 1, 0, 0, WR, (0, 3))
                base = link.n
                with dve.Fori(0, steps // WR - 2) as it:
                    for j in range(WR):
                        link.n = base + per_step * (WR * it + j)
                        onehots(WR + 1 + j, 0, it, WR, False)
                        apply(WR + j, 0, it, WR, (0, 3))
                link.n = base + per_step * (steps - 2 * WR)
                for k in range(steps - WR + 1, steps):
                    onehots(k, 0, 0, WR, False)
                    apply(k - 1, 0, 0, WR, (0, 3))
                apply(steps - 1, 0, 0, WR, (0, 3))
                dve.wait_ge(s_gelu, (l + 1) * NKEYS)
                double = steps - L.split

                def gate(k, it, every, i=None):
                    onehots(k, 1, it, every, False)
                    if i is not None:
                        act_low(i, it)
                    apply(k, 1, it, every, L.gate_banks)

                act_low(0, 0)
                if double:
                    base = link.n
                    with dve.Fori(0, double // WR) as it:
                        for j in range(WR):
                            link.n = base + per_step * (2 * WR * it + 2 * j)
                            gate(steps + 2 * j, it, 2 * WR, j + 1)
                            gate(steps + 2 * j + 1, it, 2 * WR)
                    link.n = base + per_step * 2 * double
                base = link.n
                with dve.Fori(0, (L.split - double) // WR - 1) as it:
                    for j in range(WR):
                        link.n = base + per_step * (WR * it + j)
                        gate(steps + 2 * double + j, it, WR, double + j + 1)
                link.n = base + per_step * (L.split - double - WR)
                for j in range(WR, 0, -1):
                    gate(2 * steps - j, 0, WR, L.split - j + 1 if j > 1 else None)
                act_low(L.split, 0)
                with dve.Fori(0, (NKEYS - L.split) // WR - 1) as it:
                    for j in range(WR):
                        act_low(L.split + 1 + j, it)
                for i in range(NKEYS - WR + 1, NKEYS):
                    act_low(i, 0)
                dve.wait_ge(s_use, (l + 1) * NW)
                for c in range(DC):
                    for bank, at, t0, n in L.out_at[c]:
                        hc = h[:, c, L.t0 + t0:L.t0 + t0 + n]
                        ins = v.tensor_tensor(hc, hc, ps[:, bank, at:at + n], ALU.add)
                        ins.then_inc(s_hd, 1) if c == DC - 1 and t0 + n == L.nt else link(ins)
                dve.wait_ge(s_hd, l + 1)


def weight_tiles(w):
    n = w.shape[1] // P
    return w.reshape(DC, P, n, P).transpose(2, 1, 0, 3).reshape(n, P, D)


def lay_out(a):
    f = {k: np.asarray(v) for k, v in a.items()}
    tokens = np.concatenate([f["meta"], f["x"][0]], 0)
    h0 = tokens.T.reshape(DC, P, T).transpose(1, 0, 2).reshape(P, DC * T)
    res, mix = constants()
    vec = np.zeros((P, DEPTH, NVEC), np.float32)
    lora = np.zeros((DEPTH, P, 2, 2 * P), np.float32)
    attn, rwkv = 768, 1024
    q_cols = np.concatenate([np.arange(HD) + HD * hh for c in range(4) for hh in (c, c + 4)])
    cols = np.concatenate([attn + np.arange(rwkv), attn + rwkv + np.arange(512), q_cols, 512 + np.arange(256)])
    rows = np.concatenate([q_cols, 512 + np.arange(512)])
    w, u, keys = [], [], []
    for l in range(DEPTH):
        def put(name, value):
            at, n = VEC[name]
            vec[:, l, at:at + n] = value

        for name, key in (("norm1", "norm1_g"), ("norm2", "norm2_g"), ("mu", "rwkv_mu"), ("w0", "rwkv_w0"),
                          ("a0", "rwkv_a0"), ("k_k", "rwkv_k_k"), ("k_a", "rwkv_k_a"), ("r_k", "rwkv_r_k"),
                          ("gn_g", "rwkv_gn_g"), ("gn_b", "rwkv_gn_b"), ("conv_b", "conv_b"),
                          ("ln_g", "conv_ln_g"), ("ln_b", "conv_ln_b")):
            put(name, f[key][l].reshape(-1, P).T)
        put("qg", np.concatenate([f["q_norm_g"][l]] * 2)[:, None])
        put("kg", np.concatenate([f["k_norm_g"][l]] * 2)[:, None])
        put("conv_w", f["conv_w"][l].reshape(CONV_K, 2, P).transpose(2, 1, 0).reshape(P, 2 * CONV_K))
        put("sink", np.broadcast_to(f["attn_sinks"][l], (P, AH)))
        lora[l, 0:HD, 0] = f["rwkv_w_lora"][l]
        lora[l, HD:P, 0] = f["rwkv_a_lora"][l]
        lora[l, :, 1] = f["rwkv_g_lora"][l]
        w.append(np.concatenate([weight_tiles(f["w_in"][l][:, cols]), weight_tiles(f["w_out"][l][rows]),
                                 weight_tiles(f["peer_wq"][l])], 0))
        u.append(f["peer_u"][l].reshape(NKEYS, P, DC, P).transpose(0, 3, 2, 1).reshape(NKEYS, P, D))
        keys.append(f["peer_keys"][l].reshape(NQ, NKEYS, P).transpose(2, 0, 1).reshape(P, NQ * NKEYS))
    return dict(h0=h0, vec=vec.reshape(P, DEPTH * NVEC), res_c=res, mix_c=mix,
                lora_c=lora.reshape(DEPTH, P, 4 * P), keys_c=np.stack(keys), w_c=np.stack(w), u_c=np.stack(u),
                v_c=f["peer_v"].reshape(DEPTH, NKEYS, P, D))


def kernel(**inputs):
    import concourse.bacc as bacc
    from concourse.bass_utils import run_bass_kernel_spmd

    arrays = {k: np.ascontiguousarray(a) for k, a in lay_out(inputs).items()}
    nc = bacc.Bacc("TRN2", target_bir_lowering=False, num_devices=1)
    aps = {k: nc.dram_tensor(k, a.shape, mybir.dt.from_np(a.dtype), kind="ExternalInput").ap()
           for k, a in arrays.items()}
    out = nc.dram_tensor("out", (P, DC, SEQ), F32, kind="ExternalOutput").ap()
    trunk(nc, out=out, **aps)
    got = run_bass_kernel_spmd(nc, [arrays], core_ids=[0]).results[0]["out"]
    return got.transpose(2, 1, 0).reshape(1, SEQ, D)
```

```python
from contextlib import ExitStack

import numpy as np
import concourse.bass as bass
from concourse import mybir

ALU = mybir.AluOpType
ACT = mybir.ActivationFunctionType
AX = mybir.AxisListType
F32 = mybir.dt.float32
F32R = mybir.dt.float32r
U32 = mybir.dt.uint32

P = 128
D = 1024
DC = D // P
SEQ = 256
NMETA = 16
T = SEQ + NMETA
DEPTH = 2
HD = 64
NORM_EPS = 1e-6
GN_EPS = 64e-5
CHUNK = 64
ZR, ZCU, ZCG, ZQ, ZK, ZV = 0, 8, 10, 12, 16, 17
NZ = 18
NOUT = D // P
NCH = -(-T // CHUNK)
PAD = NCH * CHUNK - T
TP = NCH * CHUNK
LEVELS = (1, 2, 4, 8, 16, 32)
CONV_K = 31
CPAD = CONV_K - 1
AH = 8
PH = 8
NKEYS = 128
TOPK = 16
NQ = PH * 2
TILES = ((0, NMETA), (NMETA, P), (NMETA + P, P))
NT = len(TILES)
NEG = -3.0e38
FAR = 1.0e30
VEC = dict(norm1=(0, 8), norm2=(8, 8), qg=(16, 1), kg=(17, 1), mu=(18, 8), w0=(26, 2), a0=(28, 2), k_k=(30, 2),
           k_a=(32, 2), r_k=(34, 2), gn_g=(36, 2), gn_b=(38, 2), conv_b=(40, 2), ln_g=(42, 2), ln_b=(44, 2),
           conv_w=(46, 2 * CONV_K), sink=(46 + 2 * CONV_K, AH))
NVEC = 46 + 2 * CONV_K + AH
RES = dict(ident=(0, P), ones=(P, P), iota=(2 * P, P), norm_eps=(3 * P, 1), gn_eps=(3 * P + 1, 1))
NRES = 3 * P + 2
MIX = {}
NMIX = 0
for _name, _n in (("blk", P), ("mask4", 4 * CHUNK), ("id2", CHUNK), ("negm1", CHUNK), ("negm1T", CHUNK),
                  ("mT", (len(LEVELS) - 1) * P), ("distM", NMETA), ("distA", 144), ("distB", 208)):
    MIX[_name] = (NMIX, _n)
    NMIX += _n
WR = 4
AHEAD = WR - 2
NPROJ = NZ + NOUT + NQ
NU0 = NPROJ
NV0 = NU0 + NKEYS
NW = NV0 + NKEYS
OHT = 4


class Layer:

    def __init__(self, l):
        self.last = l == DEPTH - 1
        self.t0 = NMETA if self.last else 0
        self.nt = T - self.t0
        self.steps = self.nt // OHT
        self.split = NKEYS - self.steps
        self.quiet = 56 if not self.last else 40
        self.tiles = [x for x in TILES if x[0] >= self.t0]
        if 2 * self.nt <= 512:
            self.gate_banks = (0, 1)
            self.out_at = [[(4 + c // 2, (c % 2) * self.nt, 0, self.nt)] for c in range(DC)]
        else:
            self.gate_banks = (0, 0)
            self.out_at = [[(1 + c, 0, 0, self.nt)] for c in range(DC - 1)]
            rest = 512 - self.nt
            self.out_at.append([(1, self.nt, 0, rest), (2, self.nt, rest, self.nt - rest)])
        assert self.split % WR == 0 and self.quiet % WR == 0 and self.quiet <= self.split


LAYERS = [Layer(l) for l in range(DEPTH)]
G0 = [sum(2 * LAYERS[m].steps for m in range(l)) for l in range(DEPTH + 1)]
SC0 = [sum(4 * len(LAYERS[m].tiles) for m in range(l)) for l in range(DEPTH)]
A0 = [sum(2 * len(LAYERS[m].tiles) for m in range(l)) for l in range(DEPTH + 1)]
KEYS_OF = (NMETA, 144, 208)
V_TILES = (("z", 0, P, (0, 0)), ("z", P, 16, (0, 1)), ("vcat", 0, P, (1, 0)), ("vcat", P, 80, (1, 1)))
Q2_AT = [(1, 0, 0, T), (2, 0, 0, T), (7, 0, 0, T), (0, 0, 0, T), (1, T, 0, 512 - T), (2, T, 512 - T, 2 * T - 512)]
WARM = dict(prepare=48, norm=30)
PE_STEPS = 7
SLOPES = [2.0 ** (-8.0 * (h + 1) / AH) for h in range(AH)]


def constants():
    res = np.zeros((P, NRES), np.float32)
    res[:, 0:P] = np.eye(P)
    res[:, P:2 * P] = 1.0
    res[:, 2 * P:3 * P] = np.arange(P)[None]
    res[:, 3 * P] = NORM_EPS
    res[:, 3 * P + 1] = GN_EPS
    mix = np.zeros((P, NMIX), np.float32)

    def put(name, a):
        a = np.asarray(a, np.float32)
        mix[:a.shape[0], MIX[name][0]:MIX[name][0] + MIX[name][1]] = a.reshape(a.shape[0], -1)

    p = np.arange(P)
    put("blk", p[:, None] // HD == p[None] // HD)
    s, t = np.arange(CHUNK)[:, None], np.arange(CHUNK)[None]
    both = lambda a: np.concatenate([a, a], 0)
    put("mask4", both(np.stack([s < t, s <= t, s < t, s <= t], 1)))
    put("id2", both(s == t))
    cross = lambda b, r, c: (r // (2 * b) == c // (2 * b)) & ((r // b) % 2 == 1) & ((c // b) % 2 == 0)
    put("negm1", both(-1.0 * cross(1, s, t)))
    put("negm1T", both(-1.0 * cross(1, t, s)))
    put("mT", np.stack([np.kron(np.eye(2), cross(b, t, s)) for b in LEVELS[1:]], 1))
    put("distM", np.abs(np.arange(NMETA)[:, None] - np.arange(NMETA)[None]))

    def dist(q0, keys):
        q = q0 + np.arange(P)[:, None]
        k = np.asarray(keys)[None]
        qc, kc = (q - NMETA) // CHUNK, (k - NMETA) // CHUNK
        ok = (k < NMETA) | ((kc <= qc) & (kc >= qc - 1))
        return np.where(ok, np.abs(q - k), FAR)

    put("distA", dist(NMETA, range(0, 144)))
    put("distB", dist(NMETA + P, list(range(16)) + list(range(80, 272))))
    return res, mix


class Link:

    def __init__(self, eng, sem):
        self.eng, self.sem, self.n = eng, sem, 0

    def __call__(self, ins):
        ins.then_inc(self.sem, 1)
        self.n = self.n + 1
        self.eng.wait_ge(self.sem, self.n)


class Arena:

    def __init__(self, tensor, start=0):
        self.t, self.at = tensor, start

    def take(self, n, parts=P):
        a = self.t[0:parts, self.at:self.at + n]
        self.at += n
        assert self.at <= self.t.shape[1], self.at
        return a


def splits(n):
    return [(a, min(P, n - a)) for a in range(0, n, P)]


def bc(ap, axis, n):
    a = ap.unsqueeze(axis)
    shape = list(a.shape)
    shape[axis] = n
    return a.broadcast_to(shape)


def trunk(nc, h0, vec, res_c, mix_c, lora_c, keys_c, w_c, u_c, v_c, out):
    with ExitStack() as ctx:
        def sb(name, cols, dt=F32, parts=P):
            return ctx.enter_context(nc.sbuf_tensor(name, [parts, cols], dt))

        def twice(raw, low, cols):
            with nc.sbuf_tensor(raw, [P, cols], F32) as a:
                pass
            return a, sb(low, cols, F32R)

        def sem(name):
            return ctx.enter_context(nc.semaphore(name))

        h_t = sb("h", DC * T)
        xh_t = sb("x_hi", DC * T, F32R)
        xn_t, xl_t = twice("x", "x_lo", DC * T)
        res_t = sb("res", NRES)
        vec_t = sb("vecs", DEPTH * NVEC)
        whi_t = sb("w_hi", WR * D, F32R)
        wraw_t, wlo_t = twice("w", "w_lo", WR * D)
        sel_t = sb("sel", 3 * T)
        ohB_t = sb("onehots_j", 2 * OHT * P)
        ohA_t = sb("onehots_i", 2 * OHT * 68)
        zero_t = sb("zeros", P)
        arena_t = sb("arena", P * T)
        ps = ctx.enter_context(nc.psum_tensor("ps", [P, 8, 512], F32))

        h = h_t[:, :].rearrange("p (c t) -> p c t", c=DC)
        tok = lambda t: t[:, :].rearrange("p (c t) -> p c t", c=DC)
        xn, xh, xl = tok(xn_t), tok(xh_t), tok(xl_t)
        vecs = vec_t[:, :].rearrange("p (l n) -> p l n", l=DEPTH)
        ring = lambda t: t[:, :].rearrange("p (s k c) -> p s k c", s=WR, k=DC)
        whi, wlo = ring(whi_t), ring(wlo_t)
        sel = sel_t[:, :].rearrange("p (s t) -> p s t", s=3)
        ohB = ohB_t[:, :].rearrange("p (b t n) -> p b t n", b=2, t=OHT)
        ohA = ohA_t[:, :].rearrange("p (b t n) -> p b t n", b=2, t=OHT)
        var = ohB_t[:, 0:T]
        act_hi = xh_t[:, 0:2 * T].rearrange("p (b t) -> p b t", b=2)
        act_lo = xh_t[:, 2 * T:4 * T].rearrange("p (b t) -> p b t", b=2)
        hid = [arena_t[:, 0:P * L.nt].rearrange("p (i t) -> p i t", i=P) for L in LAYERS]

        def res(name):
            a, n = RES[name]
            return res_t[:, a:a + n]

        ident, ones, iota = res("ident"), res("ones"), res("iota")

        def vcol(l, name, i=0, parts=slice(0, P)):
            a = VEC[name][0] + i
            return vecs[parts, l, a:a + 1]

        A = Arena(arena_t)
        mix_m = A.take(NMIX)
        lora = A.take(4 * P).rearrange("p (s n) -> p s n", s=2)
        sq = A.take(DC * T).rearrange("p (c t) -> p c t", c=DC)
        z_t = A.take(NZ * (T + 1))
        z = z_t.rearrange("p (c t) -> p c t", c=NZ)
        cat_t = A.take(DC * T)
        cat = cat_t.rearrange("p (c t) -> p c t", c=DC)
        mixed_end = A.at

        def two(n=T):
            return A.take(2 * n).rearrange("p (j t) -> p j t", j=2)

        cu = A.take(2 * (CPAD + T)).rearrange("p (j t) -> p j t", j=2)
        cacc, ctmp = two(), two()
        bonus, gg = two(), two()
        alrh = A.take(4 * TP).rearrange("p (m j t) -> p m j t", m=2, j=2)
        al, rh = alrh[:, 0], alrh[:, 1]
        be_ka = A.take(4 * TP)
        be, ka = (be_ka[:, i * 2 * TP:(i + 1) * 2 * TP].rearrange("p (j t) -> p j t", j=2) for i in range(2))
        dall = two(TP)
        yT = two(TP)
        t1, t2, t3 = two(), two(), two(TP)
        state = A.take(2 * 2 * P).rearrange("p (b j n) -> p b j n", b=2, j=2)
        B = Arena(cat_t, 4 * T)
        decayed, xs, us = (B.take(2 * P).rearrange("p (j n) -> p j n", j=2) for _ in range(3))
        over = A.at
        zs = A.take(8 * T).rearrange("p (c t) -> p c t", c=8)
        th = A.take(T)
        sg = A.take(T)
        ea = two()
        lw, cum = two(TP), two(TP)
        aa = two()
        dinv, dexc = two(TP), two(TP)
        kk, km, bb = two(), two(), two()
        over_prep = A.at

        def diag(a):
            return a.rearrange("p (j c t) -> p j c t", j=2, c=NCH)

        DIAG = 2 * NCH * P
        A.at = over + 6 * T
        al_d, v_d = diag(A.take(DIAG)), diag(A.take(DIAG))
        matrices = A.at
        A.at = over_prep
        be_d, ka_d = diag(A.take(DIAG)), diag(A.take(DIAG))
        A.at = matrices
        gram = A.take(NCH * 2 * 4 * CHUNK).rearrange("p (c j m t) -> p c j m t", c=NCH, j=2, m=4)
        cm_d, tt_d, xm_d = (diag(A.take(DIAG)) for _ in range(3))
        vkb = A.take(NCH * 3 * 2 * P).rearrange("p (c m j n) -> p c m j n", c=NCH, m=3, j=2)
        vtok, ktok, btok = (vkb[:, :, m] for m in range(3))
        g0_d = v_d
        ti, tt_, xm = (a.rearrange("p j (c t) -> p j c t", c=NCH) for a in (be, ka, t3))
        A.at = over
        vkey = A.take(2 * 2 * P).rearrange("p (s k n) -> p s k n", s=2, k=2)
        pT = A.take(2 * 4 * P).rearrange("p (k h n) -> p k h n", k=2, h=4)
        assert A.at <= over + 6 * T
        qn = sq[:, 0:5, :]
        Z = Arena(z_t)
        prob = Z.take(AH * 208)
        kcat = Z.take(208)
        vcat = Z.take(208)
        small = Z.take(8 * AH).rearrange("p (s h) -> p s h", s=8)
        assert Z.at <= 8 * (T + 1)
        A.at = 56 * T
        keys = A.take(NQ * P).rearrange("p (m n) -> p m n", m=NQ)
        pq = A.take(NQ * T).rearrange("p (m t) -> p m t", m=NQ)
        sc = A.take(NT * NQ * P).rearrange("p (s m n) -> p s m n", s=NT, m=NQ)
        comb = A.take(PH * TOPK * TOPK).rearrange("p (h n) -> p h n", h=PH)
        eqm = A.take(PH * TOPK * TOPK)
        topv = A.take(NQ * TOPK).rearrange("p (h s k) -> p h s k", h=PH, s=2)
        topi = A.take(NQ * TOPK)
        topf = A.take(NQ * TOPK).rearrange("p (h s k) -> p h s k", h=PH, s=2)
        fi = A.take(P)
        fa = A.take(2 * P).rearrange("p (s n) -> p s n", s=2)
        ff = A.take(2 * P).rearrange("p (s n) -> p s n", s=2)
        chosen = A.take(NT * 3 * P).rearrange("p (s m n) -> p s m n", s=NT, m=3)
        gsum = A.take(PH)
        topi_u = topi.bitcast(U32).rearrange("p (h s k) -> p h s k", h=PH, s=2)
        fi_u = fi.bitcast(U32)
        fa_u = fa.bitcast(U32)

        def mix(name, parts=P):
            a, n = MIX[name]
            return mix_m[0:parts, a:a + n]

        blk = mix("blk")
        mask4 = mix("mask4")
        id2, negm1, negm1T = mix("id2"), mix("negm1"), mix("negm1T")
        mT = mix("mT").rearrange("p (b t) -> p b t", b=len(LEVELS) - 1)

        s_h = sem("first_loads")
        s_zero = sem("zeros_set")
        s_mix = sem("mixer_constants_loaded")
        s_keys = sem("keys_loaded")
        s_w = [sem(f"weights_loaded_{i}") for i in range(WR)]
        s_hi = sem("weights_high_ready")
        s_lo = sem("weights_low_ready")
        s_use = sem("weight_tile_used")
        s_sq = sem("squares_ready")
        s_ss = sem("square_sums_ready")
        s_xn = sem("normed_ready")
        s_cat = sem("mixed_ready")
        s_xh = sem("x_high_ready")
        s_xl = sem("x_low_ready")
        s_ea = sem("evacuated_by_act")
        s_ed = sem("evacuated_by_dve")
        s_th = sem("tanh_ready")
        s_sg = sem("sigmoid_hg_ready")
        s_zs = sem("shifted_ready")
        s_lora = sem("lora_done")
        s_ag = sem("a_w_g_ready")
        s_pe = sem("vector_request")
        s_pd = sem("pe_step_done")
        s_ar = sem("act_request")
        s_ad = sem("act_step_done")
        s_fm = sem("v_beta_kappa_ready")
        s_dg = sem("v_beta_kappa_diagonal")
        s_g0 = sem("gram_diagonal")
        s_tm = sem("token_major_in_psum")
        s_tmc = sem("token_major_copied")
        s_gram = sem("gram_in_psum")
        s_grc = sem("gram_masked")
        s_ti = sem("inverse_ready")
        s_tt = sem("transposed_inverse_ready")
        s_x = sem("x_in_psum")
        s_xc = sem("x_copied")
        s_up = sem("update_in_psum")
        s_st = sem("state_ready")
        s_cx = sem("chunk_x_in_psum")
        s_xs = sem("chunk_x_copied")
        s_cu = sem("chunk_u_in_psum")
        s_us = sem("chunk_u_copied")
        s_cs = sem("chunk_state_in_psum")
        s_cy = sem("chunk_y_in_psum")
        s_yc = sem("chunk_y_copied")
        s_q2 = sem("qk_squares_ready")
        s_q2s = sem("qk_square_sums_in_psum")
        s_qs = sem("qk_scale_ready")
        s_qk = sem("qk_normed")
        s_vk = sem("keys_v_in_psum")
        s_vkc = sem("keys_v_copied")
        s_ts = sem("attention_scores_in_psum")
        s_tsc = sem("attention_scores_copied")
        s_te = sem("attention_exp_request")
        s_ted = sem("attention_exp_done")
        s_tn = sem("attention_normalised")
        s_tp = sem("attention_transposes_in_psum")
        s_tpc = sem("attention_transposes_copied")
        s_to = sem("attention_outputs_in_psum")
        s_toc = sem("attention_outputs_copied")
        s_var = sem("variance_ready")
        s_rs = sem("scale_ready")
        s_qr = sem("scores_in_psum")
        s_sc = sem("scores_copied")
        s_oh = sem("onehots_ready")
        s_gp = sem("gates_in_psum")
        s_gm = sem("gates_applied")
        s_gelu = sem("gelu_done")
        s_ah = sem("act_high_ready")
        s_act = sem("act_low_ready")
        s_cg = sem("conv_gate_ready")
        s_conv = sem("conv_done")
        s_gl = sem("pool_link")
        s_hd = sem("layer_done")
        s_out = sem("output_stored")
        s_dl = sem("dve_link")
        s_al = sem("act_link")

        def after(steps):
            next(steps, None)

        def groups(l):
            for i, (s, q) in enumerate((s, q) for s in range(NT) if TILES[s] in LAYERS[l].tiles for q in range(2)):
                yield A0[l] + i, s, q, KEYS_OF[s], kcat if s == 2 else qn[:, 4, :]

        block = ctx.enter_context(nc.Block())

        @block.sync
        def _(sp):
            sp.dma_start(h_t[:, :], h0).then_inc(s_h, 16)
            sp.dma_start(res_t[:, :], res_c).then_inc(s_h, 16)
            sp.dma_start(vec_t[:, :], vec).then_inc(s_h, 16)

            def load(l, n, src, it=0):
                slot = (l * NW + n) % WR
                if l or n >= WR:
                    sp.wait_ge(s_use, l * NW + n - WR + 1 + WR * it)
                sp.dma_start(wraw_t[:, slot * D:(slot + 1) * D], src).then_inc(s_w[slot], 16)

            for l in range(DEPTH):
                for n in range(WR):
                    load(l, n, w_c[l, n])
                if l:
                    sp.wait_ge(s_hd, l)
                sp.dma_start(mix_m, mix_c).then_inc(s_mix, 16)
                sp.dma_start(lora.rearrange("p s n -> p (s n)"), lora_c[l]).then_inc(s_mix, 16)
                with sp.Fori(0, (NPROJ - WR) // WR) as it:
                    for j in range(WR):
                        load(l, WR + j, w_c[l, WR * it + WR + j], it)
                for n in range(NPROJ - (NPROJ - WR) % WR, NPROJ):
                    load(l, n, w_c[l, n])
                sp.wait_ge(s_xn, (2 * l + 2) * DC)
                sp.dma_start(keys.rearrange("p m n -> p (m n)"), keys_c[l]).then_inc(s_keys, 16)
                for first, src in ((NU0, u_c), (NV0, v_c)):
                    with sp.Fori(0, NKEYS // WR) as it:
                        for j in range(WR):
                            load(l, first + j, src[l, WR * it + j], it)
            sp.wait_ge(s_hd, DEPTH)
            sp.dma_start(out, h[:, :, NMETA:T]).then_inc(s_out, 16)
            sp.wait_ge(s_out, 16)

        @block.gpsimd
        def _(pool):
            nc.gpsimd.memset(zero_t[:, :], 0.0).then_inc(s_zero, 1)
            g = nc.gpsimd
            link = Link(pool, s_gl)

            def low(l, n, it=0):
                at = (l * NW + n) % WR * D
                slot = slice(at, at + D)
                pool.wait_ge(s_hi, l * NW + n + 1 + WR * it)
                g.tensor_tensor(wlo_t[:, slot], wraw_t[:, slot], whi_t[:, slot].bitcast(F32),
                                ALU.subtract).then_inc(s_lo, 1)

            def lows(l, n0, n1):
                whole = (n1 - n0) // WR
                with pool.Fori(0, whole) as it:
                    for j in range(WR):
                        low(l, n0 + j, it)
                for n in range(n0 + whole * WR, n1):
                    low(l, n)

            for l in range(DEPTH):
                lows(l, 0 if l == 0 else AHEAD, NZ + AHEAD)
                pool.wait_ge(s_cg, 2 * (l + 1))
                link(g.memset(cu[:, :, 0:CPAD], 0.0))
                link(g.tensor_tensor(cu[:, :, CPAD:CPAD + T], z[:, ZCU:ZCU + 2, 1:T + 1], cacc[:, :, :], ALU.mult))
                for k in range(CONV_K):
                    for j in range(2):
                        dst = cacc if k == 0 else ctmp
                        ins = g.tensor_scalar(dst[:, j, :], cu[:, j, k:k + T], vcol(l, "conv_w", j * CONV_K + k),
                                              vcol(l, "conv_b", j) if k == 0 else None, ALU.mult,
                                              *((ALU.add,) if k == 0 else ()))
                        if j == 0:
                            ins.then_inc(s_gl, 1)
                            link.n += 1
                        else:
                            link(ins)
                    if k:
                        ins = g.tensor_tensor(cacc[:, :, :], cacc[:, :, :], ctmp[:, :, :], ALU.add)
                        link(ins) if k < CONV_K - 1 else ins.then_inc(s_conv, 1)
                lows(l, NZ + AHEAD, NW)
                if l < DEPTH - 1:
                    for n in range(AHEAD):
                        low(l + 1, n)

        @block.scalar
        def _(act):
            link = Link(act, s_al)
            req = [0]
            done = [0]

            def asked():
                req[0] += 1
                act.wait_ge(s_ar, req[0])

            def root(a, pieces=None, scale=1.0, eps=0.0):
                for dst, src in pieces or ((a, a),):
                    ins = nc.scalar.activation(dst, src, ACT.Sqrt, scale=scale, bias=eps)
                return ins

            def rsqrt(a, pieces=None, scale=1.0, eps=0.0):
                for dst, src in pieces or ((a, a),):
                    ins = nc.scalar.activation(dst, src, ACT.Ln, scale=scale, bias=eps)
                link(ins)
                return nc.scalar.activation(a, a, ACT.Exp, scale=-0.5)

            def norm_scale(l, k):
                act.wait_ge(s_ss, 2 * l + k + 1)
                root(var, ((var, ps[:, 0, 0:T]),), 1.0 / D, res("norm_eps")).then_inc(s_rs, 1)

            def high(l, n, it=0):
                if n >= NW:
                    l, n = l + 1, n - NW
                if l == DEPTH:
                    return
                slot = (l * NW + n) % WR
                act.wait_ge(s_w[slot], 16 * it + 16 * ((l * NW + n) // WR + 1))
                if l or n >= WR:
                    act.wait_ge(s_use, l * NW + n - WR + 1 + WR * it)
                nc.scalar.copy(whi_t[:, slot * D:(slot + 1) * D],
                               wraw_t[:, slot * D:(slot + 1) * D]).then_inc(s_hi, 1)

            def x_high(l, k, src, t0=0):
                for c in range(DC):
                    if k == 1:
                        act.wait_ge(s_cat, l + 1)
                    else:
                        act.wait_ge(s_xn, (2 * l + k // 2) * DC + c + 1)
                    nc.scalar.copy(xh[:, c, t0:T], src[:, c, t0:T]).then_inc(s_xh, 1)

            def squares(l, k):
                if 2 * l + k:
                    act.wait_ge(s_hd, l) if k == 0 else act.wait_ge(s_ed, (l + 1) * NOUT)
                else:
                    act.wait_ge(s_h, 48)
                nc.scalar.activation(sq[:, :, :], h[:, :, :], ACT.Square).then_inc(s_sq, 1)

            def evacuate(l, n, dst, nt):
                high(l, n + AHEAD)
                act.wait_ge(s_use, l * NW + n + 1)
                nc.scalar.copy(dst, ps[:, 1 + n % 2, 0:nt]).then_inc(s_ea, 1)

            def blocks(dst, src):
                for q in range(2):
                    c = slice(q * HD, (q + 1) * HD)
                    ins = nc.scalar.activation(dst[..., c], src, ACT.Copy, scale=blk[:, q * HD:q * HD + 1])
                return ins

            def attention(l):
                yield
                act.wait_ge(s_q2s, l + 1)
                root(qn, [(qn[:, min(c, 4), t0:t0 + n], ps[:, bank, at:at + n])
                           for c, (bank, at, t0, n) in enumerate(Q2_AT)], 1.0 / HD,
                      res("norm_eps")).then_inc(s_qs, 1)
                for _ in range(8):
                    yield
                for n, s, q, nk, _ in groups(l):
                    q0, nq = TILES[s]
                    if q == 0:
                        yield
                        yield
                        act.wait_ge(s_te, n // 2 + 1)
                        pr = prob[0:nq, 0:AH * nk].rearrange("p (h k) -> p h k", h=AH)
                        for hh in range(AH):
                            nc.scalar.activation(pr[:, hh, :], pr[:, hh, :], ACT.Exp, bias=small[0:nq, 1, hh:hh + 1],
                                                 scale=HD ** -0.5, accum_out=small[0:nq, 2, hh:hh + 1])
                        nc.scalar.activation(small[0:nq, 3, :], small[0:nq, 3, :], ACT.Exp).then_inc(s_ted, 1)
                        for _ in range(3):
                            yield
                    yield
                    act.wait_ge(s_tp, n + 1)
                    if n:
                        act.wait_ge(s_to, n)
                    for b, (k0, kn) in enumerate(splits(nk)):
                        ins = nc.scalar.copy(pT[0:kn, b, :, 0:nq],
                                             ps[0:kn, 1 + b, :].rearrange("p (h n) -> p h n", h=4)[:, :, 0:nq])
                    ins.then_inc(s_tpc, 1)
                    yield
                    yield
                    act.wait_ge(s_to, n + 1)
                    nc.scalar.copy(cat[q * HD:(q + 1) * HD, 0:4, q0:q0 + nq],
                                   ps[q * HD:(q + 1) * HD, 1, :].rearrange("p (h n) -> p h n",
                                                                           h=4)[:, :, 0:nq]).then_inc(s_toc, 1)

            for l in range(DEPTH):
                L = LAYERS[l]
                squares(l, 0)
                if l == 0:
                    for n in range(AHEAD):
                        high(0, n)
                norm_scale(l, 0)
                x_high(l, 0, xn)
                for n in range(12):
                    evacuate(l, n, z[:, n, 1:T + 1], T)
                act.wait_ge(s_zs, 2 * l + 2)
                nc.scalar.activation(th[0:HD, :], zs[0:HD, 6, :], ACT.Tanh).then_inc(s_th, 1)
                nc.scalar.activation(sg[:, :], zs[:, 7, :], ACT.Sigmoid).then_inc(s_sg, 1)
                act.wait_ge(s_lora, 6 * l + 6)
                for j in range(2):
                    nc.scalar.activation(ea[:, j, :], ps[:, 3 + j, 0:T], ACT.Sigmoid,
                                         bias=vcol(l, "w0", j)).then_inc(s_ag, 1)
                for j in range(2):
                    nc.scalar.activation(aa[:, j, :], ps[:, 5 + j, 0:T], ACT.Sigmoid,
                                         bias=vcol(l, "a0", j)).then_inc(s_ag, 1)
                for j in range(2):
                    nc.scalar.copy(gg[:, j, :], ps[:, 7 if j == 0 else 0, 0:T]).then_inc(s_ag, 1)
                for j in range(2):
                    nc.scalar.activation(cacc[:, j, :], z[:, ZCG + j, 1:T + 1], ACT.Sigmoid).then_inc(s_cg, 1)
                for n in range(12, NZ):
                    evacuate(l, n, z[:, n, 1:T + 1], T)
                act.wait_ge(s_var, l + 1)
                root(t2[:, :, :]).then_inc(s_rs, 1)
                asked()
                nc.scalar.activation(dall[:, :, :], cum[:, :, :], ACT.Exp).then_inc(s_ad, 1)
                nc.scalar.activation(dinv[:, :, :], cum[:, :, :], ACT.Exp, scale=-1.0).then_inc(s_ad, 1)
                nc.scalar.activation(dexc[:, :, :], lw[:, :, :], ACT.Exp).then_inc(s_ad, 1)
                act.wait_ge(s_ad, 5 * l + 3)
                for i, (src, dst) in enumerate(((t3, v_d), (be, be_d), (ka, ka_d))):
                    act.wait_ge(s_fm, 3 * l + i + 1)
                    blocks(dst.rearrange("p j c t -> p (j c) t"),
                           src.rearrange("p j (c t) -> p (j c) t", c=NCH)).then_inc(s_dg, 1)
                steps = attention(l)
                for c in range(NCH):
                    act.wait_ge(s_tm, l * NCH + c + 1)
                    nc.scalar.copy(vkb[:, c, 0:2].rearrange("p m j n -> p (m j n)"), ps[:, 3 + 2 * (c % 2), :])
                    nc.scalar.copy(vkb[:, c, 2].rearrange("p j n -> p (j n)"),
                                   ps[:, 4 + 2 * (c % 2), 0:2 * P]).then_inc(s_tmc, 1)
                after(steps)
                after(steps)
                after(steps)
                act.wait_ge(s_grc, NCH * (l + 1))
                blocks(g0_d, gram[:, :, :, 0, :].rearrange("p c j t -> p j c t")).then_inc(s_g0, 1)
                for b in range(len(LEVELS) - 1):
                    for j in range(2):
                        act.wait_ge(s_x, 2 * (len(LEVELS) - 1) * l + 2 * b + j + 1)
                        src = ps[:, 3 + j, 0:NCH * CHUNK].rearrange("p (c t) -> p c t", c=NCH)
                        nc.scalar.copy(xm[:, j], src)
                        blocks(xm_d[:, j], src).then_inc(s_xc, 1)
                    for _ in range(5):
                        after(steps)
                for c in range(NCH):
                    after(steps)
                    after(steps)
                    act.wait_ge(s_cy, NCH * l + c + 1)
                    nc.scalar.copy(yT[:, :, c * CHUNK:(c + 1) * CHUNK],
                                   ps[:, 6 + c % 2, 0:2 * CHUNK].rearrange("p (j t) -> p j t",
                                                                          j=2)).then_inc(s_yc, 1)
                    after(steps)
                act.wait_ge(s_pd, PE_STEPS * l + 4)
                root(t2[:, :, :], [(t2[:, j, :], ps[:, 3 + j, 0:T]) for j in range(2)], 1.0 / HD,
                      res("gn_eps")).then_inc(s_rs, 1)
                for _ in steps:
                    pass
                act.wait_ge(s_pd, PE_STEPS * l + 6)
                root(t3[:, 0, 0:T], ((t3[:, 0, 0:T], ps[:, 3, 0:T]),), 1.0 / (2 * P),
                      res("norm_eps")).then_inc(s_rs, 1)
                asked()
                nc.scalar.activation(t2[:, :, :], t1[:, :, :], ACT.Sigmoid).then_inc(s_ad, 1)
                act.wait_ge(s_toc, A0[l + 1])
                x_high(l, 1, cat, L.t0)
                for m in range(NOUT):
                    high(l, NZ + m + AHEAD)
                squares(l, 1)
                norm_scale(l, 1)
                x_high(l, 2, xn, L.t0)
                for m in range(NQ):
                    if m == 0:
                        act.wait_ge(s_xn, (2 * l + 2) * DC)
                    evacuate(l, NZ + NOUT + m, pq[:, m, L.t0:T], L.nt)
                for s, (t0, nt) in enumerate(L.tiles):
                    for g in range(4):
                        k = 4 * s + g
                        act.wait_ge(s_qr, SC0[l] + k + 1)
                        nc.scalar.copy(sc[0:nt, s, 4 * g:4 * g + 4, :].rearrange("p m n -> p (m n)"),
                                       ps[0:nt, 3 + k % 2, :]).then_inc(s_sc, 1)

                def gelus(i0, i1):
                    with act.Fori(0, (i1 - i0) // WR) as it:
                        for j in range(WR):
                            high(l, NU0 + i0 + j + AHEAD, it)
                            act.wait_ge(s_use, l * NW + NU0 + i0 + j + 1 + WR * it)
                            nc.scalar.activation(hid[l][:, bass.ds(WR * it + (i0 + j), 1), :].squeeze(1),
                                                 ps[:, 1 + j % 2, 0:L.nt], ACT.Gelu_apprx_tanh).then_inc(s_gelu, 1)

                gelus(0, L.quiet)
                asked()
                for s, (t0, nt) in enumerate(L.tiles):
                    ins = nc.scalar.activation(chosen[0:nt, s, 0, :], chosen[0:nt, s, 0, :], ACT.Exp)
                ins.then_inc(s_ad, 1)
                gelus(L.quiet, NKEYS)

                def act_highs(i0, i1):
                    with act.Fori(0, (i1 - i0) // WR) as it:
                        for j in range(WR):
                            act.wait_ge(s_use, l * NW + NV0 + i0 + j - 1 + WR * it)
                            nc.scalar.copy(act_hi[:, j % 2, 0:L.nt],
                                           hid[l][:, bass.ds(WR * it + (i0 + j), 1), :].squeeze(1)).then_inc(s_ah, 1)
                            high(l, NV0 + i0 + j + AHEAD, it)

                act.wait_ge(s_gm, G0[l] + L.steps)
                act_highs(0, L.split)
                act.wait_ge(s_gm, G0[l + 1])
                act_highs(L.split, NKEYS - WR)
                for i in range(NKEYS - WR, NKEYS):
                    act.wait_ge(s_use, l * NW + NV0 + i - 1)
                    nc.scalar.copy(act_hi[:, i % 2, 0:L.nt], hid[l][:, i, :]).then_inc(s_ah, 1)
                    high(l, NV0 + i + AHEAD)

        @block.tensor
        def _(pe):
            def mm(out_, lhsT, rhs, start, stop):
                return nc.tensor.matmul(out_, lhsT, rhs, start=start, stop=stop, skip_group_check=True)

            req = [0]

            def asked():
                req[0] += 1
                pe.wait_ge(s_pe, req[0])

            def warm(n, bank):
                for _ in range(n):
                    mm(ps[:, bank, 0:P], zero_t[:, :], zero_t[:, :], True, True)

            def square_sums(l, k):
                pe.wait_ge(s_sq, 2 * l + k + 1)
                for c in range(DC):
                    last = mm(ps[:, 0, 0:T], ones, sq[:, c, :], c == 0, c == DC - 1)
                last.then_inc(s_ss, 1)

            def tile(l, n, out_of, hi_of, lo_of, it=0, between=None):
                slot = (l * NW + n) % WR
                pe.wait_ge(s_lo, l * NW + n + 1 + WR * it)
                for c in range(DC):
                    if between and c == DC // 2:
                        between()
                    for o, w in out_of(c):
                        for k, (a, b) in enumerate(((whi, hi_of), (whi, lo_of), (wlo, hi_of))):
                            last = mm(o, a[:, slot, c, :], b(c, w), *flags(out_of, c, k))
                last.then_inc(s_use, 1)

            def flags(out_of, c, k):
                return (False, True) if out_of.keeps else (c == 0 and k == 0, c == DC - 1 and k == 2)

            def summed(bank, t0=0):
                def f(c):
                    return [(ps[:, bank, 0:T - t0], slice(t0, T))]
                f.keeps = False
                return f

            def project(l, n, t0=0, it=0):
                tile(l, n, summed(1 + n % 2, t0), lambda c, w: xh[:, c, w], lambda c, w: xl[:, c, w], it)

            def attention(l):
                pe.wait_ge(s_q2, l + 1)
                pe.wait_ge(s_ea, l * (NZ + NQ) + NZ)
                for c, (bank, at, t0, n) in enumerate(Q2_AT):
                    last = mm(ps[:, bank, at:at + n], blk, sq[:, min(c, 4), t0:t0 + n], True, True)
                last.then_inc(s_q2s, 1)
                yield
                for _ in range(7):
                    yield
                pe.wait_ge(s_qk, l + 1)
                for s, (src, k0, nk, _) in enumerate(V_TILES):
                    a = z[:, ZV, 1 + k0:1 + k0 + nk] if src == "z" else vcat[:, k0:k0 + nk]
                    last = nc.tensor.transpose(ps[0:nk, 1 + s % 2, (s // 2) * P:(s // 2 + 1) * P], a, ident)
                last.then_inc(s_vk, 1)
                yield
                pe.wait_ge(s_vkc, l + 1)

                def scores(n, s, q, nk, kt):
                    r = slice(q * HD, (q + 1) * HD)
                    q0, nq = TILES[s]
                    for c in range(4):
                        last = mm(ps[0:nq, 1 + c // 2, (c % 2) * nk:(c % 2 + 1) * nk], qn[r, c, q0:q0 + nq],
                                  kt[r, 0:nk], True, True)
                    last.then_inc(s_ts, 1)

                for n, s, q, nk, kt in groups(l):
                    q0, nq = TILES[s]
                    if n > A0[l]:
                        pe.wait_ge(s_toc, n)
                    if q == 0:
                        scores(n, s, 0, nk, kt)
                        yield
                        pe.wait_ge(s_tsc, n + 1)
                        scores(n, s, 1, nk, kt)
                        for _ in range(4):
                            yield
                        pe.wait_ge(s_tn, n // 2 + 1)
                    for b, (k0, kn) in enumerate(splits(nk)):
                        for c in range(4):
                            at = (4 * q + c) * nk + k0
                            last = nc.tensor.transpose(ps[0:kn, 1 + b, c * P:c * P + nq], prob[0:nq, at:at + kn],
                                                       ident[0:nq, 0:nq])
                    last.then_inc(s_tp, 1)
                    yield
                    yield
                    pe.wait_ge(s_tpc, n + 1)
                    for c in range(4):
                        for b, (k0, kn) in enumerate(splits(nk)):
                            last = mm(ps[q * HD:(q + 1) * HD, 1, c * P:c * P + nq],
                                      vkey[0:kn, max(s, 1) - 1, b, q * HD:(q + 1) * HD], pT[0:kn, b, c, 0:nq],
                                      b == 0, k0 + kn == nk)
                    last.then_inc(s_to, 1)
                    yield

            def x_split(l, k):
                pe.wait_ge(s_xl, (3 * l + k + 1) * DC)

            for l in range(DEPTH):
                if l == 0:
                    pe.wait_ge(s_h, 48)
                    pe.wait_ge(s_zero, 1)
                pe.wait_ge(s_mix, 32 * (l + 1))
                square_sums(l, 0)
                warm(WARM["norm"], 3)
                x_split(l, 0)
                L = LAYERS[l]

                def proj_in(n):
                    if n >= 2:
                        pe.wait_ge(s_ea, l * (NZ + NQ) + n - 1)
                    project(l, n)

                for n in range(NZ):
                    if n == 12:
                        pe.wait_ge(s_th, l + 1)
                        pe.wait_ge(s_sg, l + 1)
                        for j in range(2):
                            mm(ps[:, 3 + j, 0:T], lora[0:HD, 0, j * P:(j + 1) * P], th[0:HD, :],
                               True, True).then_inc(s_lora, 1)
                        for j in range(2):
                            mm(ps[:, 5 + j, 0:T], lora[HD:P, 0, j * P:(j + 1) * P], zs[HD:P, 6, :],
                               True, True).then_inc(s_lora, 1)
                        for j in range(2):
                            mm(ps[:, 7 if j == 0 else 0, 0:T], lora[:, 1, j * P:(j + 1) * P], sg[:, :],
                               True, True).then_inc(s_lora, 1)
                    proj_in(n)

                pe.wait_ge(s_ag, 6 * l + 6)
                asked()
                for j in range(2):
                    last = mm(ps[:, 3 + j, 0:T], blk, t2[:, j, :], True, True)
                last.then_inc(s_pd, 1)
                asked()
                for j in range(2):
                    last = mm(ps[:, 5 + j, 0:T], blk, t1[:, j, :], True, True)
                last.then_inc(s_pd, 1)
                steps = attention(l)
                pe.wait_ge(s_ea, l * (NZ + NQ) + NZ)
                warm(WARM["prepare"], 1)
                asked()
                pe.wait_ge(s_dg, 3 * (l + 1))
                for c in range(NCH):
                    if c >= 2:
                        pe.wait_ge(s_tmc, l * NCH + c - 1)
                    for m, src in enumerate((v_d, ka_d, be_d)):
                        for j in range(2):
                            last = nc.tensor.transpose(ps[:, 3 + 2 * (c % 2) + m // 2,
                                                          (2 * (m % 2) + j) * P:(2 * (m % 2) + j + 1) * P],
                                                       src[:, j, c, :], ident)
                    last.then_inc(s_tm, 1)
                after(steps)
                pe.wait_ge(s_tmc, (l + 1) * NCH)
                for c in range(NCH):
                    if c >= 2:
                        pe.wait_ge(s_grc, l * NCH + c - 1)
                    w = slice(c * CHUNK, (c + 1) * CHUNK)
                    for j in range(2):
                        for m, a in enumerate((ka_d, be_d)):
                            mm(ps[:, 5 + c % 2, (j * 4 + 2 * m) * CHUNK:(j * 4 + 2 * m + 2) * CHUNK],
                               a[:, j, c, :], alrh[:, :, j, w], True, True)
                        last = mm(ps[:, 3 + j, c * CHUNK:(c + 1) * CHUNK], al_d[:, j, c, :], be[:, j, w], True, True)
                    last.then_inc(s_gram, 1)
                    if c >= 3:
                        after(steps)
                pe.wait_ge(s_qs, l + 1)
                nlev = len(LEVELS) - 1
                for b in range(nlev):
                    for j in range(2):
                        pe.wait_ge(s_ti, 2 * nlev * l + 2 * b + j + 1)
                        for c in range(NCH):
                            last = mm(ps[:, 3 + j, c * CHUNK:(c + 1) * CHUNK], cm_d[:, j, c, :], ti[:, j, c, :],
                                      True, True)
                        last.then_inc(s_x, 1)
                    after(steps)
                    for j in range(2):
                        pe.wait_ge(s_xc, 2 * nlev * l + 2 * b + j + 1)
                        pe.wait_ge(s_tt, 2 * (nlev + 1) * l + 2 * b + j + 1)
                        if b < nlev - 1:
                            for c in range(NCH):
                                last = mm(ps[:, 5 + j, c * CHUNK:(c + 1) * CHUNK], tt_d[:, j, c, :], xm[:, j, c, :],
                                          True, True)
                            last.then_inc(s_up, 1)
                        after(steps)
                        for c in range(NCH):
                            last = mm(ps[:, 7 - 7 * j, c * CHUNK:(c + 1) * CHUNK], xm_d[:, j, c, :],
                                      tt_[:, j, c, :], True, True)
                        last.then_inc(s_up, 1)
                        after(steps)
                pe.wait_ge(s_tt, 2 * (nlev + 1) * (l + 1))
                pe.wait_ge(s_g0, l + 1)
                for c in range(NCH):
                    w = slice(c * CHUNK, (c + 1) * CHUNK)
                    k = NCH * l + c
                    jw = lambda j, n: slice(j * n, (j + 1) * n)
                    yb = 6 + c % 2
                    for j in range(2):
                        mm(ps[:, 3, jw(j, P)], g0_d[:, j, c, :], vtok[:, c, j, :], j == 0, False)
                    pe.wait_ge(s_st, k + 1)
                    for j in range(2):
                        last = mm(ps[:, 3, jw(j, P)], al_d[:, j, c, :], state[:, c % 2, j, :], False, True)
                    last.then_inc(s_cx, 1)
                    if c < NCH - 1:
                        for j in range(2):
                            mm(ps[:, 5, jw(j, P)], ktok[:, c, j, :], vtok[:, c, j, :], j == 0, False)
                    after(steps)
                    pe.wait_ge(s_xs, k + 1)
                    for j in range(2):
                        last = mm(ps[:, 4, jw(j, P)], tt_d[:, j, c, :], xs[:, j, :], True, True)
                    last.then_inc(s_cu, 1)
                    if c >= 2:
                        pe.wait_ge(s_yc, k - 1)
                    for j in range(2):
                        mm(ps[:, yb, jw(j, CHUNK)], state[:, c % 2, j, :], rh[:, j, w], j == 0, False)
                        mm(ps[:, yb, jw(j, CHUNK)], vtok[:, c, j, :], gram[:, c, j, 1, :], False, False)
                    after(steps)
                    pe.wait_ge(s_us, k + 1)
                    if c < NCH - 1:
                        for j in range(2):
                            last = mm(ps[:, 5, jw(j, P)], btok[:, c, j, :], us[:, j, :], False, True)
                        last.then_inc(s_cs, 1)
                    for j in range(2):
                        last = mm(ps[:, yb, jw(j, CHUNK)], us[:, j, :], gram[:, c, j, 3, :], False, True)
                    last.then_inc(s_cy, 1)
                    after(steps)
                for k in range(2):
                    if k:
                        asked()
                    else:
                        pe.wait_ge(s_yc, NCH * (l + 1))
                    for j in range(2):
                        last = mm(ps[:, 3 + j, 0:T], blk, yT[:, j, PAD:TP] if k == 0 else t2[:, j, :], True, True)
                    last.then_inc(s_pd, 1)
                for _ in steps:
                    pass
                pe.wait_ge(s_conv, l + 1)
                for k in range(2):
                    asked()
                    for j in range(2):
                        last = mm(ps[:, 3, 0:T], ones, cacc[:, j, :] if k == 0 else t2[:, j, :], j == 0, j == 1)
                    last.then_inc(s_pd, 1)
                warm(WARM["norm"], 0)
                x_split(l, 1)
                for m in range(NOUT):
                    n = NZ + m
                    if m >= 2:
                        pe.wait_ge(s_ed, l * NOUT + m - 1)
                    else:
                        pe.wait_ge(s_ea, l * (NZ + NQ) + NZ)
                    project(l, n, L.t0)
                square_sums(l, 1)
                warm(WARM["norm"], 3)
                x_split(l, 2)
                for m in range(NQ):
                    n = NZ + NOUT + m
                    if m >= 2:
                        pe.wait_ge(s_ea, l * (NZ + NQ) + NZ + m - 1)
                    project(l, n, L.t0)
                pe.wait_ge(s_keys, 16 * (l + 1))
                pe.wait_ge(s_ea, (l + 1) * (NZ + NQ))
                for s, (t0, nt) in enumerate(L.tiles):
                    for g in range(4):
                        k = 4 * s + g
                        if k >= 2:
                            pe.wait_ge(s_sc, SC0[l] + k - 1)
                        for m in range(4):
                            last = mm(ps[0:nt, 3 + k % 2, m * P:(m + 1) * P], pq[:, 4 * g + m, t0:t0 + nt],
                                      keys[:, 4 * g + m, :], True, True)
                        last.then_inc(s_qr, 1)

                def hidden(i, it):
                    if not (isinstance(it, int) and i < 2):
                        pe.wait_ge(s_gelu, l * NKEYS + i - 1 + WR * it)
                    project(l, NU0 + i, L.t0, it)

                def spread(k, it, banks, n, first, every=WR):
                    pe.wait_ge(s_oh, G0[l] + k + 1 + every * it)
                    if not first:
                        pe.wait_ge(s_gm, G0[l] + k - (banks[0] != banks[1]) + every * it)
                    for t in range(OHT):
                        last = mm(ps[:, banks[k % 2], t * n:(t + 1) * n], ohB[:, k % 2, t, :],
                                  ohA[:, k % 2, t, 0:n], True, True)
                    last.then_inc(s_gp, 1)

                for i in range(WR):
                    hidden(i, 0)
                with pe.Fori(0, L.split // WR - 1) as it:
                    for j in range(WR):
                        hidden(WR + j, it)
                asked()
                for s, (t0, nt) in enumerate(L.tiles):
                    for m in range(3):
                        last = nc.tensor.transpose(ps[:, 5 + s, m * P:m * P + nt], chosen[0:nt, s, m, :],
                                                   ident[0:nt, 0:nt])
                last.then_inc(s_pd, 1)
                for j in range(WR):
                    hidden(L.split + j, 0)
                    spread(j, 0, (0, 3), L.split, j < 2)
                with pe.Fori(0, L.steps // WR - 1) as it:
                    for j in range(WR):
                        hidden(L.split + WR + j, it)
                        spread(WR + j, it, (0, 3), L.split, False)
                pe.wait_ge(s_gm, G0[l] + L.steps)
                pe.wait_ge(s_gelu, (l + 1) * NKEYS)
                for bank in sorted({q[0] for c in range(DC) for q in L.out_at[c]}):
                    mm(ps[:, bank, :], zero_t[:, :], h_t[:, 0:512], True, True)

                def pieces(c):
                    return [(ps[:, bank, at:at + n], slice(t0, t0 + n)) for bank, at, t0, n in L.out_at[c]]

                pieces.keeps = True

                def output(i, it, between=None):
                    pe.wait_ge(s_act, l * NKEYS + i + 1 + WR * it)
                    tile(l, NV0 + i, pieces, lambda c, w: act_hi[:, i % 2, w], lambda c, w: act_lo[:, i % 2, w], it,
                         between)

                double = L.steps - L.split
                n2 = NKEYS - L.split
                if double:
                    with pe.Fori(0, double // WR) as it:
                        for j in range(WR):
                            k = L.steps + 2 * j
                            output(j, it, lambda: spread(k, it, L.gate_banks, n2, False, 2 * WR))
                            spread(k + 1, it, L.gate_banks, n2, False, 2 * WR)
                with pe.Fori(0, (L.split - double) // WR) as it:
                    for j in range(WR):
                        output(double + j, it)
                        spread(L.steps + 2 * double + j, it, L.gate_banks, n2, False)
                pe.wait_ge(s_gm, G0[l + 1])
                with pe.Fori(0, (NKEYS - L.split) // WR) as it:
                    for j in range(WR):
                        output(L.split + j, it)

        @block.vector
        def _(dve):
            v = nc.vector
            link = Link(dve, s_dl)
            npd, nad, npe = [0], [0], [0]

            def ask_pe(ins):
                ins.then_inc(s_pe, 1)
                npe[0] += 1

            def ask_pe_and_wait(ins):
                ask_pe(ins)
                dve.wait_ge(s_pe, npe[0])

            def pe_done():
                npd[0] += 1
                dve.wait_ge(s_pd, npd[0])

            def act_done(n=1):
                nad[0] += n
                dve.wait_ge(s_ad, nad[0])

            nrs = [0]

            def scaled(a):
                nrs[0] += 1
                dve.wait_ge(s_rs, nrs[0])
                link(v.reciprocal(a, a))

            def x_low(l, k, src, dst, t0, c):
                dve.wait_ge(s_xh, (3 * l + k) * DC + c + 1)
                v.tensor_tensor(dst[:, c, t0:T], src[:, c, t0:T], xh[:, c, t0:T].bitcast(F32),
                                ALU.subtract).then_inc(s_xl, 1)

            def norm(l, k, t0=0):
                scaled(var)
                for c in range(DC):
                    v.scalar_tensor_tensor(xn[:, c, t0:T], h[:, c, t0:T], vcol(l, "norm2" if k else "norm1", c),
                                           var[:, t0:T], ALU.mult, ALU.mult).then_inc(s_xn, 1)
                    if c:
                        x_low(l, 2 * k, xn, xl, t0, c - 1)
                x_low(l, 2 * k, xn, xl, t0, DC - 1)

            def cms(j, b):
                return v.tensor_tensor(cm_d[:, j].rearrange("p c (q t) -> p c q t", q=2),
                                       bc(gram[:, :, j, 2, :], 2, 2),
                                       bc(mT[:, b].rearrange("p (q t) -> p q t", q=2), 1, NCH), ALU.mult)

            def tt_diag(j):
                v.tensor_tensor(tt_d[:, j].rearrange("p c (q t) -> p c q t", q=2), bc(tt_[:, j], 2, 2),
                                bc(blk.rearrange("p (q t) -> p q t", q=2), 1, NCH), ALU.mult).then_inc(s_tt, 1)

            def update(bank):
                return ps[:, bank, 0:NCH * CHUNK].rearrange("p (c t) -> p c t", c=NCH)

            def attention(l):
                L = LAYERS[l]
                yield
                yield
                yield
                dve.wait_ge(s_qs, l + 1)
                for c in range(0, 5, 2):
                    a = qn[:, c:min(c + 2, 5), :]
                    link(v.reciprocal(a, a))
                    yield
                for c in range(5):
                    link(v.scalar_tensor_tensor(qn[:, c, :], z[:, ZQ + c, 1:T + 1], vcol(l, "kg" if c == 4 else "qg"),
                                                qn[:, c, :], ALU.mult, ALU.mult))
                for src, dst in ((qn[:, 4, :], kcat), (z[:, ZV, 1:T + 1], vcat)):
                    link(v.tensor_copy(dst[:, 0:NMETA], src[:, 0:NMETA]))
                    ins = v.tensor_copy(dst[:, NMETA:208], src[:, 80:T])
                    link(ins) if dst is kcat else ins.then_inc(s_qk, 1)
                for _ in range(3):
                    yield
                dve.wait_ge(s_vk, l + 1)
                for s, (src, k0, nk, (sl, b)) in enumerate(V_TILES):
                    ins = v.tensor_copy(vkey[0:nk, sl, b, :], ps[0:nk, 1 + s % 2, (s // 2) * P:(s // 2 + 1) * P])
                    link(ins) if s < len(V_TILES) - 1 else ins.then_inc(s_vkc, 1)
                for n, s, q, nk, _ in groups(l):
                    yield
                    if q:
                        for _ in range(5):
                            yield
                        continue
                    q0, nq = TILES[s]
                    dist = mix(("distM", "distA", "distB")[s], nq)
                    pr = prob[0:nq, 0:AH * nk].rearrange("p (h k) -> p h k", h=AH)
                    m_, nm, rs, es, rd = (small[0:nq, i, :] for i in range(5))
                    sink = vecs[0:nq, l, VEC["sink"][0]:VEC["sink"][0] + AH]
                    for qq in range(2):
                        dve.wait_ge(s_ts, n + qq + 1)
                        for c in range(4):
                            hh = 4 * qq + c
                            ins = v.scalar_tensor_tensor(pr[:, hh, :], dist, -SLOPES[hh] * HD ** 0.5,
                                                         ps[0:nq, 1 + c // 2, (c % 2) * nk:(c % 2 + 1) * nk],
                                                         ALU.mult, ALU.add)
                            link(ins) if c < 3 else ins.then_inc(s_tsc, 1)
                        if qq == 0:
                            yield
                    dve.wait_ge(s_tsc, n + 2)
                    link(v.tensor_reduce(m_, pr, AX.X, ALU.max))
                    link(v.scalar_tensor_tensor(m_, m_, HD ** -0.5, sink, ALU.mult, ALU.max))
                    link(v.tensor_scalar(nm, m_, -1.0, None, ALU.mult))
                    v.tensor_tensor(es, sink, m_, ALU.subtract).then_inc(s_te, 1)
                    yield
                    yield
                    dve.wait_ge(s_ted, n // 2 + 1)
                    link(v.tensor_tensor(rs, rs, es, ALU.add))
                    link(v.reciprocal(rd, rs))
                    v.tensor_tensor(pr, pr, bc(rd, 2, nk), ALU.mult).then_inc(s_tn, 1)
                    yield

            for l in range(DEPTH):
                if l == 0:
                    dve.wait_ge(s_h, 48)
                L = LAYERS[l]
                norm(l, 0)
                dve.wait_ge(s_mix, 32 * (l + 1))
                link(v.memset(z[:, :, 0:1], 0.0))
                dve.wait_ge(s_ea, l * (NZ + NQ) + 8)
                for c in (6, 7, 0, 1, 2, 3, 4, 5):
                    link(v.tensor_tensor(t1[:, 0, :], z[:, c, 0:T], z[:, c, 1:T + 1], ALU.subtract))
                    ins = v.scalar_tensor_tensor(zs[:, c, :], t1[:, 0, :], vcol(l, "mu", c), z[:, c, 1:T + 1],
                                                 ALU.mult, ALU.add)
                    if c in (6, 7):
                        ins.then_inc(s_zs, 1)
                        dve.wait_ge(s_zs, 2 * l + c - 5)
                    else:
                        link(ins)
                r_, k_, v_ = zs[:, 0:2, :], zs[:, 2:4, :], zs[:, 4:6, :]
                for j in range(2):
                    link(v.tensor_scalar(kk[:, j, :], k_[:, j, :], vcol(l, "k_k", j), None, ALU.mult))
                ask_pe(v.tensor_tensor(t2[:, :, :], kk[:, :, :], kk[:, :, :], ALU.mult))
                link(v.memset(lw[:, :, 0:PAD], 0.0))
                dve.wait_ge(s_ag, 6 * (l + 1))
                link(v.tensor_scalar(lw[:, :, PAD:TP], ea[:, :, :], -float(np.exp(-0.5)), None, ALU.mult))
                for j in range(2):
                    for c in range(NCH):
                        w = slice(c * CHUNK, (c + 1) * CHUNK)
                        link(v.tensor_tensor_scan(cum[:, j, w], ones[:, 0:CHUNK], lw[:, j, w], 0.0,
                                                  ALU.mult, ALU.add))
                v.tensor_tensor(lw[:, :, :], cum[:, :, :], lw[:, :, :], ALU.subtract).then_inc(s_ar, 1)
                for a in (al, be, ka, rh):
                    link(v.memset(a[:, :, 0:PAD], 0.0))
                for j in range(2):
                    link(v.tensor_scalar(t1[:, j, :], aa[:, j, :], -1.0, vcol(l, "k_a", j), ALU.add, ALU.mult))
                link(v.scalar_tensor_tensor(km[:, :, :], t1[:, :, :], 1.0, k_, ALU.add, ALU.mult))
                link(v.memset(t3[:, :, 0:PAD], 0.0))
                v.tensor_copy(t3[:, :, PAD:TP], v_).then_inc(s_fm, 1)
                for j in range(2):
                    ins = v.scalar_tensor_tensor(t1[:, j, :], r_[:, j, :], vcol(l, "r_k", j), km[:, j, :],
                                                 ALU.mult, ALU.mult)
                    (ask_pe if j else link)(ins)
                pe_done()
                for j in range(2):
                    ins = v.tensor_scalar(t2[:, j, :], ps[:, 3 + j, 0:T], 1e-12, None, ALU.max)
                    link(ins) if j == 0 else ins.then_inc(s_var, 1)
                scaled(t2[:, :, :])
                link(v.tensor_tensor(kk[:, :, :], kk[:, :, :], t2[:, :, :], ALU.mult))
                link(v.tensor_tensor(bb[:, :, :], kk[:, :, :], aa[:, :, :], ALU.mult))
                pe_done()
                for j in range(2):
                    link(v.tensor_tensor(bonus[:, j, :], ps[:, 5 + j, 0:T], v_[:, j, :], ALU.mult))
                act_done(3)
                w = slice(PAD, TP)
                v.tensor_tensor(be[:, :, w], dinv[:, :, w], bb[:, :, :], ALU.mult).then_inc(s_fm, 1)
                v.tensor_tensor(ka[:, :, w], dinv[:, :, w], km[:, :, :], ALU.mult).then_inc(s_fm, 1)
                link(v.tensor_tensor(al[:, :, w], dexc[:, :, w], kk[:, :, :], ALU.mult))
                link(v.tensor_tensor(al_d.rearrange("p j c (q t) -> p (j c) q t", q=2),
                                     bc(al.rearrange("p j (c t) -> p (j c) t", c=NCH), 2, 2),
                                     bc(blk.rearrange("p (q t) -> p q t", q=2), 1, 2 * NCH), ALU.mult))
                ask_pe(v.tensor_tensor(rh[:, :, w], dall[:, :, w], r_, ALU.mult))
                v.memset(state[:, 0], 0.0).then_inc(s_st, 1)
                v.tensor_tensor(sq[:, 0:5, :], z[:, ZQ:ZQ + 5, 1:T + 1], z[:, ZQ:ZQ + 5, 1:T + 1],
                                ALU.mult).then_inc(s_q2, 1)
                steps = attention(l)
                nlev = len(LEVELS) - 1
                after(steps)
                for c in range(NCH):
                    dve.wait_ge(s_gram, NCH * l + c + 1)
                    v.tensor_tensor(gram[:, c].rearrange("p j m t -> p j (m t)"),
                                    ps[:, 5 + c % 2, :].rearrange("p (j m) -> p j m", j=2),
                                    bc(mask4, 1, 2), ALU.mult).then_inc(s_grc, 1)
                    if c >= 3:
                        after(steps)
                dve.wait_ge(s_grc, NCH * (l + 1))
                for j in range(2):
                    link(v.tensor_tensor(ti[:, j], ps[:, 3 + j, 0:NCH * CHUNK].rearrange("p (c t) -> p c t", c=NCH),
                                         bc(negm1, 1, NCH), ALU.mult))
                    link(v.tensor_tensor(ti[:, j], ti[:, j], bc(id2, 1, NCH), ALU.add))
                    cms(j, 0).then_inc(s_ti, 1)
                    link(v.tensor_tensor(tt_[:, j], gram[:, :, j, 2, :], bc(negm1T, 1, NCH), ALU.mult))
                    link(v.tensor_tensor(tt_[:, j], tt_[:, j], bc(id2, 1, NCH), ALU.add))
                    tt_diag(j)
                for b in range(nlev):
                    last = b == nlev - 1
                    for j in range(2):
                        if not last:
                            dve.wait_ge(s_x, 2 * nlev * l + 2 * b + j + 1)
                            link(cms(j, b + 1))
                    after(steps)
                    for j in range(2):
                        up = (2 * (2 * nlev - 1) * l + 4 * b + 2 * j) if not last else \
                            (2 * (2 * nlev - 1) * l + 4 * b + j - 1)
                        if not last:
                            dve.wait_ge(s_up, up + 1)
                            v.tensor_tensor(ti[:, j], ti[:, j], update(5 + j), ALU.subtract).then_inc(s_ti, 1)
                        after(steps)
                        dve.wait_ge(s_up, up + 2)
                        link(v.tensor_tensor(tt_[:, j], tt_[:, j], update(7 - 7 * j), ALU.subtract))
                        tt_diag(j)
                        after(steps)
                for c in range(NCH):
                    e = (c + 1) * CHUNK
                    k = NCH * l + c
                    flat = lambda a: a.rearrange("p j n -> p (j n)")
                    dve.wait_ge(s_st, k + 1)
                    if c < NCH - 1:
                        for j in range(2):
                            link(v.tensor_scalar(decayed[:, j, :], state[:, c % 2, j, :], dall[:, j, e - 1:e], None,
                                                 ALU.mult))
                    dve.wait_ge(s_cx, k + 1)
                    v.tensor_copy(flat(xs), ps[:, 3, 0:2 * P]).then_inc(s_xs, 1)
                    after(steps)
                    dve.wait_ge(s_cu, k + 1)
                    v.tensor_scalar(flat(us), ps[:, 4, 0:2 * P], -1.0, None, ALU.mult).then_inc(s_us, 1)
                    after(steps)
                    if c < NCH - 1:
                        dve.wait_ge(s_cs, (NCH - 1) * l + c + 1)
                        for j in range(2):
                            ins = v.scalar_tensor_tensor(state[:, (c + 1) % 2, j, :], ps[:, 5, j * P:(j + 1) * P],
                                                         dall[:, j, e - 1:e], decayed[:, j, :], ALU.mult, ALU.add)
                            link(ins) if j == 0 else ins.then_inc(s_st, 1)
                    after(steps)
                pe_done()
                for j in range(2):
                    link(v.scalar_tensor_tensor(t1[:, j, :], ps[:, 3 + j, 0:T], -1.0 / HD, yT[:, j, PAD:TP],
                                                ALU.mult, ALU.add))
                ask_pe(v.tensor_tensor(t2[:, :, :], t1[:, :, :], t1[:, :, :], ALU.mult))
                pe_done()
                scaled(t2[:, :, :])
                link(v.tensor_tensor(t1[:, :, :], t1[:, :, :], t2[:, :, :], ALU.mult))
                for j in range(2):
                    link(v.tensor_scalar(t1[:, j, :], t1[:, j, :], vcol(l, "gn_g", j), vcol(l, "gn_b", j),
                                         ALU.mult, ALU.add))
                link(v.tensor_tensor(t1[:, :, :], t1[:, :, :], bonus[:, :, :], ALU.add))
                ask_pe_and_wait(v.tensor_tensor(cat[:, 4:6, :], t1[:, :, :], gg[:, :, :], ALU.mult))
                for _ in steps:
                    pass
                pe_done()
                for j in range(2):
                    link(v.scalar_tensor_tensor(cacc[:, j, :], ps[:, 3, 0:T], -1.0 / (2 * P), cacc[:, j, :],
                                                ALU.mult, ALU.add))
                ask_pe(v.tensor_tensor(t2[:, :, :], cacc[:, :, :], cacc[:, :, :], ALU.mult))
                pe_done()
                scaled(t3[:, 0, 0:T])
                link(v.tensor_tensor(t1[:, :, :], cacc[:, :, :], bc(t3[:, 0, 0:T], 1, 2), ALU.mult))
                for j in range(2):
                    ins = v.tensor_scalar(t1[:, j, :], t1[:, j, :], vcol(l, "ln_g", j), vcol(l, "ln_b", j),
                                          ALU.mult, ALU.add)
                    link(ins) if j == 0 else ins.then_inc(s_ar, 1)
                act_done(1)
                v.tensor_tensor(cat[:, 6:8, :], t1[:, :, :], t2[:, :, :], ALU.mult).then_inc(s_cat, 1)
                for c in range(DC):
                    x_low(l, 1, cat, xl, L.t0, c)
                for m in range(NOUT):
                    dve.wait_ge(s_use, l * NW + NZ + m + 1)
                    v.tensor_tensor(h[:, m, L.t0:T], h[:, m, L.t0:T], ps[:, 1 + (NZ + m) % 2, 0:L.nt],
                                    ALU.add).then_inc(s_ed, 1)
                dve.wait_ge(s_ed, (l + 1) * NOUT)
                norm(l, 1, L.t0)
                for s, (t0, nt) in enumerate(L.tiles):
                    dve.wait_ge(s_sc, SC0[l] + 4 * s + 4)
                    hs = [(hh, p) for hh in range(PH) for p in range(2)]
                    score = lambda hh, p: sc[0:nt, s, 2 * hh + p, :]

                    def top16(items, val, idx, src):
                        def each(f):
                            for it_ in items[:-1]:
                                f(*it_).then_inc(s_dl, 1)
                                link.n += 1
                            link(f(*items[-1]))

                        each(lambda *a: v.max(val(*a)[:, 0:8], src(*a)))
                        each(lambda *a: v.max_index(idx(*a)[:, 0:8], val(*a)[:, 0:8], src(*a)))
                        each(lambda *a: v.match_replace(src(*a), val(*a)[:, 0:8], src(*a), NEG))
                        each(lambda *a: v.max(val(*a)[:, 8:16], src(*a)))
                        each(lambda *a: v.max_index(idx(*a)[:, 8:16], val(*a)[:, 8:16], src(*a)))

                    top16(hs, lambda hh, p: topv[0:nt, hh, p, :], lambda hh, p: topi_u[0:nt, hh, p, :], score)
                    link(v.tensor_copy(topf[0:nt].rearrange("p h s k -> p (h s k)"),
                                       topi_u[0:nt].rearrange("p h s k -> p (h s k)")))
                    cb = comb[0:nt].rearrange("p h (a b) -> p h a b", a=TOPK)
                    link(v.tensor_tensor(cb, bc(topv[0:nt, :, 0, :], 3, TOPK), bc(topv[0:nt, :, 1, :], 2, TOPK),
                                         ALU.add))
                    fvh = chosen[0:nt, s, 0, :].rearrange("p (h k) -> p h k", h=PH)
                    fih = fi_u[0:nt].rearrange("p (h k) -> p h k", h=PH)
                    top16([(hh,) for hh in range(PH)], lambda hh: fvh[:, hh, :], lambda hh: fih[:, hh, :],
                          lambda hh: comb[0:nt, hh, :])
                    link(v.tensor_scalar(fa_u[0:nt, 0, :], fi_u[0:nt], 4, None, ALU.logical_shift_right))
                    link(v.tensor_scalar(fa_u[0:nt, 1, :], fi_u[0:nt], 15, None, ALU.bitwise_and))
                    link(v.tensor_copy(ff[0:nt].rearrange("p s n -> p (s n)"),
                                       fa_u[0:nt].rearrange("p s n -> p (s n)")))
                    e4 = eqm[0:nt].rearrange("p (n a) -> p n a", a=TOPK)
                    e5 = eqm[0:nt].rearrange("p (h k a) -> p h k a", h=PH, a=TOPK)
                    for p in range(2):
                        link(v.tensor_tensor(e4, bc(ff[0:nt, p, :], 2, TOPK), bc(iota[0:nt, 0:TOPK], 1, P),
                                             ALU.is_equal))
                        link(v.tensor_tensor(e5, e5, bc(topf[0:nt, :, p, :], 2, TOPK), ALU.mult))
                        link(v.tensor_reduce(chosen[0:nt, s, 1 + p, :], e4, AX.X, ALU.add))
                    link(v.tensor_copy(gsum[0:nt, :], fvh[:, :, 0]))
                    ins = v.tensor_tensor(fvh, fvh, bc(gsum[0:nt, :], 2, TOPK), ALU.subtract)
                    link(ins) if s < len(L.tiles) - 1 else ins.then_inc(s_ar, 1)
                act_done(1)
                for s, (t0, nt) in enumerate(L.tiles):
                    gh = chosen[0:nt, s, 0, :].rearrange("p (h k) -> p h k", h=PH)
                    link(v.tensor_reduce(gsum[0:nt, :], gh, AX.X, ALU.add))
                    link(v.reciprocal(gsum[0:nt, :], gsum[0:nt, :]))
                    ins = v.tensor_tensor(gh, gh, bc(gsum[0:nt, :], 2, TOPK), ALU.mult)
                    (ask_pe if s == len(L.tiles) - 1 else link)(ins)
                pe_done()
                for s, (t0, nt) in enumerate(L.tiles):
                    link(v.tensor_copy(sel[:, :, t0:t0 + nt],
                                       ps[:, 5 + s, 0:3 * P].rearrange("p (m n) -> p m n", m=3)[:, :, 0:nt]))

                def onehots(k, part, it, every, first):
                    i0, n = (0, L.split) if part == 0 else (L.split, NKEYS - L.split)
                    b = k % 2
                    t0 = OHT * every * it + (L.t0 + OHT * (k - part * L.steps))
                    if not first:
                        dve.wait_ge(s_gp, G0[l] + k - 1 + every * it)
                    v.tensor_tensor(ohB[:, b], bc(iota, 1, OHT), bc(sel[:, 2, bass.ds(t0, OHT)], 2, P),
                                    ALU.is_equal).then_inc(s_dl, 1)
                    link.n = link.n + 1
                    a = ohA[:, b, :, 0:n]
                    link(v.tensor_tensor(a, bc(iota[:, i0:i0 + n], 1, OHT), bc(sel[:, 1, bass.ds(t0, OHT)], 2, n),
                                         ALU.is_equal))
                    v.tensor_tensor(a, a, bc(sel[:, 0, bass.ds(t0, OHT)], 2, n), ALU.mult).then_inc(s_oh, 1)

                def apply(k, part, it, every, banks):
                    i0, n = (0, L.split) if part == 0 else (L.split, NKEYS - L.split)
                    t0 = OHT * every * it + OHT * (k - part * L.steps)
                    dve.wait_ge(s_gp, G0[l] + k + 1 + every * it)
                    hv = hid[l][:, i0:i0 + n, bass.ds(t0, OHT)]
                    v.tensor_tensor(hv, hv, ps[:, banks[k % 2], 0:OHT * n].rearrange("p (t i) -> p i t", t=OHT),
                                    ALU.mult).then_inc(s_gm, 1)

                def act_low(i, it):
                    dve.wait_ge(s_ah, l * NKEYS + i + 1 + WR * it)
                    v.tensor_tensor(act_lo[:, i % 2, 0:L.nt], hid[l][:, bass.ds(WR * it + i, 1), :].squeeze(1),
                                    act_hi[:, i % 2, 0:L.nt].bitcast(F32), ALU.subtract).then_inc(s_act, 1)

                dve.wait_ge(s_gelu, l * NKEYS + L.split)
                steps, per_step = L.steps, 2
                onehots(0, 0, 0, WR, True)
                for k in range(1, WR + 1):
                    onehots(k, 0, 0, WR, k < 2)
                    apply(k - 1, 0, 0, WR, (0, 3))
                base = link.n
                with dve.Fori(0, steps // WR - 2) as it:
                    for j in range(WR):
                        link.n = base + per_step * (WR * it + j)
                        onehots(WR + 1 + j, 0, it, WR, False)
                        apply(WR + j, 0, it, WR, (0, 3))
                link.n = base + per_step * (steps - 2 * WR)
                for k in range(steps - WR + 1, steps):
                    onehots(k, 0, 0, WR, False)
                    apply(k - 1, 0, 0, WR, (0, 3))
                apply(steps - 1, 0, 0, WR, (0, 3))
                dve.wait_ge(s_gelu, (l + 1) * NKEYS)
                double = steps - L.split

                def gate(k, it, every, i=None):
                    onehots(k, 1, it, every, False)
                    if i is not None:
                        act_low(i, it)
                    apply(k, 1, it, every, L.gate_banks)

                act_low(0, 0)
                if double:
                    base = link.n
                    with dve.Fori(0, double // WR) as it:
                        for j in range(WR):
                            link.n = base + per_step * (2 * WR * it + 2 * j)
                            gate(steps + 2 * j, it, 2 * WR, j + 1)
                            gate(steps + 2 * j + 1, it, 2 * WR)
                    link.n = base + per_step * 2 * double
                base = link.n
                with dve.Fori(0, (L.split - double) // WR - 1) as it:
                    for j in range(WR):
                        link.n = base + per_step * (WR * it + j)
                        gate(steps + 2 * double + j, it, WR, double + j + 1)
                link.n = base + per_step * (L.split - double - WR)
                for j in range(WR, 0, -1):
                    gate(2 * steps - j, 0, WR, L.split - j + 1 if j > 1 else None)
                act_low(L.split, 0)
                with dve.Fori(0, (NKEYS - L.split) // WR - 1) as it:
                    for j in range(WR):
                        act_low(L.split + 1 + j, it)
                for i in range(NKEYS - WR + 1, NKEYS):
                    act_low(i, 0)
                dve.wait_ge(s_use, (l + 1) * NW)
                for c in range(DC):
                    for bank, at, t0, n in L.out_at[c]:
                        hc = h[:, c, L.t0 + t0:L.t0 + t0 + n]
                        ins = v.tensor_tensor(hc, hc, ps[:, bank, at:at + n], ALU.add)
                        ins.then_inc(s_hd, 1) if c == DC - 1 and t0 + n == L.nt else link(ins)
                dve.wait_ge(s_hd, l + 1)


def weight_tiles(w):
    n = w.shape[1] // P
    return w.reshape(DC, P, n, P).transpose(2, 1, 0, 3).reshape(n, P, D)


def lay_out(a):
    f = {k: np.asarray(v) for k, v in a.items()}
    tokens = np.concatenate([f["meta"], f["x"][0]], 0)
    h0 = tokens.T.reshape(DC, P, T).transpose(1, 0, 2).reshape(P, DC * T)
    res, mix = constants()
    vec = np.zeros((P, DEPTH, NVEC), np.float32)
    lora = np.zeros((DEPTH, P, 2, 2 * P), np.float32)
    attn, rwkv = 768, 1024
    q_cols = np.concatenate([np.arange(HD) + HD * hh for c in range(4) for hh in (c, c + 4)])
    cols = np.concatenate([attn + np.arange(rwkv), attn + rwkv + np.arange(512), q_cols, 512 + np.arange(256)])
    rows = np.concatenate([q_cols, 512 + np.arange(512)])
    w, u, keys = [], [], []
    for l in range(DEPTH):
        def put(name, value):
            at, n = VEC[name]
            vec[:, l, at:at + n] = value

        for name, key in (("norm1", "norm1_g"), ("norm2", "norm2_g"), ("mu", "rwkv_mu"), ("w0", "rwkv_w0"),
                          ("a0", "rwkv_a0"), ("k_k", "rwkv_k_k"), ("k_a", "rwkv_k_a"), ("r_k", "rwkv_r_k"),
                          ("gn_g", "rwkv_gn_g"), ("gn_b", "rwkv_gn_b"), ("conv_b", "conv_b"),
                          ("ln_g", "conv_ln_g"), ("ln_b", "conv_ln_b")):
            put(name, f[key][l].reshape(-1, P).T)
        put("qg", np.concatenate([f["q_norm_g"][l]] * 2)[:, None])
        put("kg", np.concatenate([f["k_norm_g"][l]] * 2)[:, None])
        put("conv_w", f["conv_w"][l].reshape(CONV_K, 2, P).transpose(2, 1, 0).reshape(P, 2 * CONV_K))
        put("sink", np.broadcast_to(f["attn_sinks"][l], (P, AH)))
        lora[l, 0:HD, 0] = f["rwkv_w_lora"][l]
        lora[l, HD:P, 0] = f["rwkv_a_lora"][l]
        lora[l, :, 1] = f["rwkv_g_lora"][l]
        w.append(np.concatenate([weight_tiles(f["w_in"][l][:, cols]), weight_tiles(f["w_out"][l][rows]),
                                 weight_tiles(f["peer_wq"][l])], 0))
        u.append(f["peer_u"][l].reshape(NKEYS, P, DC, P).transpose(0, 3, 2, 1).reshape(NKEYS, P, D))
        keys.append(f["peer_keys"][l].reshape(NQ, NKEYS, P).transpose(2, 0, 1).reshape(P, NQ * NKEYS))
    return dict(h0=h0, vec=vec.reshape(P, DEPTH * NVEC), res_c=res, mix_c=mix,
                lora_c=lora.reshape(DEPTH, P, 4 * P), keys_c=np.stack(keys), w_c=np.stack(w), u_c=np.stack(u),
                v_c=f["peer_v"].reshape(DEPTH, NKEYS, P, D))


def kernel(**inputs):
    import concourse.bacc as bacc
    from concourse.bass_utils import run_bass_kernel_spmd

    arrays = {k: np.ascontiguousarray(a) for k, a in lay_out(inputs).items()}
    nc = bacc.Bacc("TRN2", target_bir_lowering=False, num_devices=1)
    aps = {k: nc.dram_tensor(k, a.shape, mybir.dt.from_np(a.dtype), kind="ExternalInput").ap()
           for k, a in arrays.items()}
    out = nc.dram_tensor("out", (P, DC, SEQ), F32, kind="ExternalOutput").ap()
    trunk(nc, out=out, **aps)
    got = run_bass_kernel_spmd(nc, [arrays], core_ids=[0]).results[0]["out"]
    return got.transpose(2, 1, 0).reshape(1, SEQ, D)
```
